# Optimizing a Trainium2 kernel written in Bass

```python
import math, functools
import jax, jax.numpy as jnp
from jax import lax
import numpy as np

D_MODEL = 2048
BATCH = 1
SEQ = 256
DEPTH = 1
DEC_BATCH = 8
DEC_SEQ = 8
PAST_LEN = 2048
PAGE_SIZE = 128

NORM_EPS = 1e-6
RWKV_HEAD_DIM = 64
RWKV_WIDTH = D_MODEL // 2
RWKV_HEADS = RWKV_WIDTH // RWKV_HEAD_DIM
W_LORA = 96
A_LORA = 96
G_LORA = 256
RWKV_PROJ = 3 * RWKV_WIDTH + W_LORA + A_LORA + G_LORA
RWKV_GN_EPS = 64e-5
V_DIM = 128
MLA_WIDTH = D_MODEL - RWKV_WIDTH
MLA_HEADS = MLA_WIDTH // V_DIM
Q_LORA = 512
KV_LORA = 256
NOPE_DIM = 128
ROPE_DIM = 64
ROPE_THETA = 10000.0
MLA_SCALE = (NOPE_DIM + ROPE_DIM) ** -0.5
Q_BLOCK = 128
IN_PROJ = RWKV_PROJ + Q_LORA + KV_LORA + ROPE_DIM
MIX_WIDTH = RWKV_WIDTH + MLA_WIDTH
MEM_TOKENS = 256
MEM_HEADS = 4
MEM_HEAD_DIM = 128
MEM_WIDTH = MEM_HEADS * MEM_HEAD_DIM
MEM_SCALE = MEM_HEAD_DIM ** -0.5
N_GROUPS = 4
EXPERTS_PER_GROUP = 8
N_EXPERTS = N_GROUPS * EXPERTS_PER_GROUP
TOP_K = 2
EXPERT_FF = 512
MOE_BLOCK = 128

kernel_name = "hymba_rwkv7_mla_hmoe_step"

F32 = jnp.float32

def rmsnorm(x, g):
    xf = x.astype(F32)
    y = xf * lax.rsqrt(jnp.mean(xf * xf, axis=-1, keepdims=True) + NORM_EPS)
    return (y * g.astype(F32)).astype(x.dtype)

def rope_tables(pos):
    half = ROPE_DIM // 2
    inv = ROPE_THETA ** (-jnp.arange(half, dtype=F32) / half)
    ang = pos.astype(F32)[:, None] * inv[None, :]
    return jnp.cos(ang), jnp.sin(ang)

def apply_rope(x, cos, sin):
    half = ROPE_DIM // 2
    xf = x.astype(F32)
    x1, x2 = xf[..., :half], xf[..., half:]
    return jnp.concatenate([x1 * cos - x2 * sin, x1 * sin + x2 * cos], axis=-1).astype(x.dtype)

def rwkv7_mix(p, prev, state0, mu, w0, w_w2, a0, w_a2, w_g2, k_k, k_a, r_k, gn_g, gn_b):
    B, S, _ = p.shape
    H, N = RWKV_HEADS, RWKV_HEAD_DIM
    shifted = jnp.concatenate([prev[:, None, :].astype(p.dtype), p[:, :-1]], axis=1)
    ps = p + (shifted - p) * mu
    i1, i2, i3 = RWKV_WIDTH, 2 * RWKV_WIDTH, 3 * RWKV_WIDTH
    i4 = i3 + W_LORA
    i5 = i4 + A_LORA
    r, k, v = ps[..., :i1], ps[..., i1:i2], ps[..., i2:i3]
    xw, xa, xg = ps[..., i3:i4], ps[..., i4:i5], ps[..., i5:]
    w_log = -jax.nn.softplus(-(w0 + jnp.tanh(xw) @ w_w2).astype(F32)) - 0.5
    hs = (B, S, H, N)
    decay = jnp.exp(-jnp.exp(w_log)).reshape(hs)
    a = jax.nn.sigmoid((a0 + xa @ w_a2).astype(F32)).reshape(hs)
    g = jax.nn.sigmoid(xg) @ w_g2
    rf = r.astype(F32).reshape(hs)
    kf = k.astype(F32).reshape(hs)
    vf = v.astype(F32).reshape(hs)
    kk = kf * k_k.astype(F32).reshape(H, N)
    kk = kk / jnp.maximum(jnp.sqrt(jnp.sum(kk * kk, axis=-1, keepdims=True)), 1e-12)
    kf = kf * (1.0 + (a - 1.0) * k_a.astype(F32).reshape(H, N))

    def step(st, inp):
        r_t, w_t, k_t, v_t, kk_t, b_t = inp
        sa = jnp.einsum('bhvk,bhk->bhv', st, -kk_t)
        st = st * w_t[:, :, None, :] + sa[..., None] * b_t[:, :, None, :] + v_t[..., None] * k_t[:, :, None, :]
        return st, jnp.einsum('bhvk,bhk->bhv', st, r_t)

    xs = (jnp.swapaxes(rf, 0, 1), jnp.swapaxes(decay, 0, 1), jnp.swapaxes(kf, 0, 1),
          jnp.swapaxes(vf, 0, 1), jnp.swapaxes(kk, 0, 1), jnp.swapaxes(kk * a, 0, 1))
    st_final, ys = lax.scan(step, state0.astype(F32), xs)
    y = jnp.swapaxes(ys, 0, 1)
    mean = jnp.mean(y, axis=-1, keepdims=True)
    var = jnp.mean(jnp.square(y - mean), axis=-1, keepdims=True)
    y = ((y - mean) * lax.rsqrt(var + RWKV_GN_EPS)).reshape(B, S, RWKV_WIDTH)
    y = y * gn_g.astype(F32) + gn_b.astype(F32)
    bonus = jnp.sum(rf * kf * r_k.astype(F32), axis=-1, keepdims=True) * vf
    out = ((y + bonus.reshape(B, S, RWKV_WIDTH)) * g.astype(F32)).astype(p.dtype)
    return out, st_final.astype(state0.dtype), p[:, -1].astype(prev.dtype)

def mla_project(q_a, kv_a, cos, sin, q_norm_g, w_qb, kv_norm_g, w_kvb):
    B, S, _ = q_a.shape
    q = (rmsnorm(q_a, q_norm_g) @ w_qb).reshape(B, S, MLA_HEADS, NOPE_DIM + ROPE_DIM)
    q_nope = q[..., :NOPE_DIM]
    q_pe = apply_rope(q[..., NOPE_DIM:], cos[:, None, :], sin[:, None, :])
    c_kv = rmsnorm(kv_a[..., :KV_LORA], kv_norm_g)
    k_pe = apply_rope(kv_a[..., KV_LORA:], cos, sin)
    w_uk = w_kvb.reshape(KV_LORA, MLA_HEADS, NOPE_DIM + V_DIM)[..., :NOPE_DIM]
    q_lat = jnp.einsum('bshd,chd->bshc', q_nope, w_uk)
    return q_lat, q_pe, c_kv, k_pe

def mla_attend_prompt(q_lat, q_pe, c_kv, k_pe):
    B, S, H, C = q_lat.shape
    nb = S // Q_BLOCK
    ql = jnp.swapaxes(q_lat.reshape(B, nb, Q_BLOCK, H, C), 0, 1)
    qp = jnp.swapaxes(q_pe.reshape(B, nb, Q_BLOCK, H, ROPE_DIM), 0, 1)
    kpos = jnp.arange(S)

    def one_block(args):
        blk, ql_b, qp_b = args
        s = (jnp.einsum('bqhc,bkc->bhqk', ql_b, c_kv) + jnp.einsum('bqhr,bkr->bhqk', qp_b, k_pe)).astype(F32) * MLA_SCALE
        qpos = blk * Q_BLOCK + jnp.arange(Q_BLOCK)
        s = jnp.where(kpos[None, :] <= qpos[:, None], s, -jnp.inf)
        pr = jax.nn.softmax(s, axis=-1).astype(c_kv.dtype)
        return jnp.einsum('bhqk,bkc->bqhc', pr, c_kv)

    o = lax.map(one_block, (jnp.arange(nb), ql, qp))
    return jnp.swapaxes(o, 0, 1).reshape(B, S, H, C)

def mla_attend_sample(q_lat, q_pe, c_kv, k_pe, past_c, past_kpe):
    T = q_lat.shape[1]
    P = past_c.shape[1]
    s_past = (jnp.einsum('bqhc,bkc->bhqk', q_lat, past_c) + jnp.einsum('bqhr,bkr->bhqk', q_pe, past_kpe)).astype(F32) * MLA_SCALE
    s_new = (jnp.einsum('bqhc,bkc->bhqk', q_lat, c_kv) + jnp.einsum('bqhr,bkr->bhqk', q_pe, k_pe)).astype(F32) * MLA_SCALE
    causal = jnp.tril(jnp.ones((T, T), dtype=bool))
    s_new = jnp.where(causal, s_new, -jnp.inf)
    pr = jax.nn.softmax(jnp.concatenate([s_past, s_new], axis=-1), axis=-1).astype(c_kv.dtype)
    return jnp.einsum('bhqk,bkc->bqhc', pr[..., :P], past_c) + jnp.einsum('bhqk,bkc->bqhc', pr[..., P:], c_kv)

def memory_kv(mem, mem_norm_g, w_mk, w_mv):
    B, M, _ = mem.shape
    m = rmsnorm(mem, mem_norm_g)
    return ((m @ w_mk).reshape(B, M, MEM_HEADS, MEM_HEAD_DIM),
            (m @ w_mv).reshape(B, M, MEM_HEADS, MEM_HEAD_DIM))

def memory_attend(h, mem_k, mem_v, w_mq, w_mo):
    B, S, _ = h.shape
    q = (h @ w_mq).reshape(B, S, MEM_HEADS, MEM_HEAD_DIM)
    s = jnp.einsum('bqhd,bkhd->bhqk', q, mem_k).astype(F32) * MEM_SCALE
    pr = jax.nn.softmax(s, axis=-1).astype(mem_v.dtype)
    o = jnp.einsum('bhqk,bkhd->bqhd', pr, mem_v).reshape(B, S, MEM_WIDTH)
    return o @ w_mo

def moe_dispatch(xt, eid, wts, w_gate, w_up, w_down):
    N, D = xt.shape
    A = N * TOP_K
    flat_e = eid.reshape(-1).astype(jnp.int32)
    flat_tok = jnp.repeat(jnp.arange(N, dtype=jnp.int32), TOP_K)
    flat_w = wts.reshape(-1)
    order = jnp.argsort(flat_e)
    se, stok, sw = flat_e[order], flat_tok[order], flat_w[order]
    counts = jnp.bincount(flat_e, length=N_EXPERTS).astype(jnp.int32)
    starts = jnp.cumsum(counts) - counts
    padded = (counts + MOE_BLOCK - 1) // MOE_BLOCK * MOE_BLOCK
    pends = jnp.cumsum(padded)
    pstarts = pends - padded
    dest = pstarts[se] + (jnp.arange(A, dtype=jnp.int32) - starts[se])
    n_blocks = -(-A // MOE_BLOCK) + N_EXPERTS
    n_slots = n_blocks * MOE_BLOCK
    slot_tok = jnp.full((n_slots,), N, dtype=jnp.int32).at[dest].set(stok)
    slot_w = jnp.zeros((n_slots,), F32).at[dest].set(sw)
    block_start = jnp.arange(n_blocks, dtype=jnp.int32) * MOE_BLOCK
    block_e = jnp.minimum(jnp.searchsorted(pends, block_start, side='right'), N_EXPERTS - 1)
    x_pad = jnp.concatenate([xt, jnp.zeros((1, D), xt.dtype)], axis=0)
    xb = x_pad[slot_tok].reshape(n_blocks, MOE_BLOCK, D)

    def expert_block(args):
        xblk, e = args
        hid = jax.nn.silu(xblk @ w_gate[e]) * (xblk @ w_up[e])
        return hid @ w_down[e]

    yb = lax.map(expert_block, (xb, block_e)).reshape(n_slots, D)
    y = jnp.zeros((N + 1, D), F32).at[slot_tok].add(yb.astype(F32) * slot_w[:, None])
    return y[:N].astype(xt.dtype)

def hmoe(h, w_router_c, b_router_c, w_router_f, b_router_f, w_gate, w_up, w_down):
    B, S, D = h.shape
    xt = h.reshape(B * S, D)
    lc = (xt @ w_router_c).astype(F32) + b_router_c.astype(F32)
    pc = jax.nn.softmax(lc, axis=-1)
    grp = jnp.argmax(lc, axis=-1)
    gate_c = jnp.take_along_axis(pc, grp[:, None], axis=-1)
    lf = ((xt @ w_router_f).astype(F32) + b_router_f.astype(F32)).reshape(-1, N_GROUPS, EXPERTS_PER_GROUP)
    lf_g = jnp.take_along_axis(lf, grp[:, None, None], axis=1)[:, 0]
    pf = jax.nn.softmax(lf_g, axis=-1)
    topv, topi = lax.top_k(pf, TOP_K)
    wts = gate_c * topv / jnp.sum(topv, axis=-1, keepdims=True)
    eid = grp[:, None] * EXPERTS_PER_GROUP + topi
    return moe_dispatch(xt, eid, wts, w_gate, w_up, w_down).reshape(B, S, D)

def decoder_layer(x, cos, sin, rwkv_prev, rwkv_state0, attend, mem_k, mem_v, lp):
    B, S, _ = x.shape
    h = rmsnorm(x, lp['ln_mix_g'])
    proj = h @ lp['w_in']
    p_rwkv = proj[..., :RWKV_PROJ]
    q_a = proj[..., RWKV_PROJ:RWKV_PROJ + Q_LORA]
    kv_a = proj[..., RWKV_PROJ + Q_LORA:]
    o_rwkv, rwkv_state, rwkv_shift = rwkv7_mix(
        p_rwkv, rwkv_prev, rwkv_state0, lp['rwkv_mu'], lp['rwkv_w0'], lp['rwkv_w_w2'], lp['rwkv_a0'],
        lp['rwkv_w_a2'], lp['rwkv_w_g2'], lp['rwkv_k_k'], lp['rwkv_k_a'], lp['rwkv_r_k'], lp['rwkv_gn_g'], lp['rwkv_gn_b'])
    q_lat, q_pe, c_kv, k_pe = mla_project(q_a, kv_a, cos, sin, lp['mla_q_norm_g'], lp['mla_w_qb'],
                                          lp['mla_kv_norm_g'], lp['mla_w_kvb'])
    o_lat = attend(q_lat, q_pe, c_kv, k_pe)
    w_uv = lp['mla_w_kvb'].reshape(KV_LORA, MLA_HEADS, NOPE_DIM + V_DIM)[..., NOPE_DIM:]
    o_mla = jnp.einsum('bshc,chv->bshv', o_lat, w_uv).reshape(B, S, MLA_WIDTH)
    x = x + jnp.concatenate([o_rwkv, o_mla], axis=-1) @ lp['w_out']
    x = x + memory_attend(rmsnorm(x, lp['ln_mem_g']), mem_k, mem_v, lp['w_mq'], lp['w_mo'])
    x = x + hmoe(rmsnorm(x, lp['ln_moe_g']), lp['w_router_c'], lp['b_router_c'], lp['w_router_f'],
                 lp['b_router_f'], lp['w_gate'], lp['w_up'], lp['w_down'])
    return x, c_kv, k_pe, rwkv_state, rwkv_shift

def setup_inputs(seed: int = 0) -> dict:
    key = jax.random.key(seed)
    ks = iter(jax.random.split(key, 64))
    L = DEPTH
    n_pages = PAST_LEN // PAGE_SIZE
    n_used = DEC_BATCH * n_pages
    n_phys = n_used + n_used // 4

    def nrm(shape, scale):
        return jax.random.normal(next(ks), shape, F32) * scale

    def gain(shape):
        return 1.0 + nrm(shape, 0.02)

    def unif(shape, lo, hi):
        return jax.random.uniform(next(ks), shape, F32, lo, hi)

    return {
        'x_prompt': nrm((BATCH, SEQ, D_MODEL), 1.0),
        'x_sample': nrm((DEC_BATCH, DEC_SEQ, D_MODEL), 1.0),
        'mem_prompt': nrm((BATCH, MEM_TOKENS, D_MODEL), 1.0),
        'cache_kv_latent': nrm((L, n_phys, PAGE_SIZE, KV_LORA), 1.0),
        'cache_k_rope': nrm((L, n_phys, PAGE_SIZE, ROPE_DIM), 1.0),
        'cache_mem_k': nrm((L, DEC_BATCH, MEM_TOKENS, MEM_HEADS, MEM_HEAD_DIM), 1.0),
        'cache_mem_v': nrm((L, DEC_BATCH, MEM_TOKENS, MEM_HEADS, MEM_HEAD_DIM), 1.0),
        'state_rwkv': nrm((L, DEC_BATCH, RWKV_HEADS, RWKV_HEAD_DIM, RWKV_HEAD_DIM), 0.5),
        'state_rwkv_shift': nrm((L, DEC_BATCH, RWKV_PROJ), 1.0),
        'page_table': jax.random.permutation(next(ks), n_phys)[:n_used].reshape(DEC_BATCH, n_pages).astype(jnp.int32),
        'ln_mix_g': gain((L, D_MODEL)),
        'w_in': nrm((L, D_MODEL, IN_PROJ), D_MODEL ** -0.5),
        'rwkv_mu': unif((L, RWKV_PROJ), 0.0, 1.0),
        'rwkv_w0': unif((L, RWKV_WIDTH), -6.0, 1.0),
        'rwkv_w_w2': nrm((L, W_LORA, RWKV_WIDTH), 0.5 * W_LORA ** -0.5),
        'rwkv_a0': nrm((L, RWKV_WIDTH), 0.5),
        'rwkv_w_a2': nrm((L, A_LORA, RWKV_WIDTH), 0.5 * A_LORA ** -0.5),
        'rwkv_w_g2': nrm((L, G_LORA, RWKV_WIDTH), G_LORA ** -0.5),
        'rwkv_k_k': 0.85 + nrm((L, RWKV_WIDTH), 0.05),
        'rwkv_k_a': gain((L, RWKV_WIDTH)),
        'rwkv_r_k': nrm((L, RWKV_HEADS, RWKV_HEAD_DIM), 0.1),
        'rwkv_gn_g': gain((L, RWKV_WIDTH)),
        'rwkv_gn_b': nrm((L, RWKV_WIDTH), 0.02),
        'mla_q_norm_g': gain((L, Q_LORA)),
        'mla_w_qb': nrm((L, Q_LORA, MLA_HEADS * (NOPE_DIM + ROPE_DIM)), Q_LORA ** -0.5),
        'mla_kv_norm_g': gain((L, KV_LORA)),
        'mla_w_kvb': nrm((L, KV_LORA, MLA_HEADS * (NOPE_DIM + V_DIM)), KV_LORA ** -0.5),
        'w_out': nrm((L, MIX_WIDTH, D_MODEL), MIX_WIDTH ** -0.5),
        'ln_mem_g': gain((L, D_MODEL)),
        'mem_norm_g': gain((L, D_MODEL)),
        'w_mq': nrm((L, D_MODEL, MEM_WIDTH), D_MODEL ** -0.5),
        'w_mk': nrm((L, D_MODEL, MEM_WIDTH), D_MODEL ** -0.5),
        'w_mv': nrm((L, D_MODEL, MEM_WIDTH), D_MODEL ** -0.5),
        'w_mo': nrm((L, MEM_WIDTH, D_MODEL), MEM_WIDTH ** -0.5),
        'ln_moe_g': gain((L, D_MODEL)),
        'w_router_c': nrm((L, D_MODEL, N_GROUPS), D_MODEL ** -0.5),
        'b_router_c': nrm((L, N_GROUPS), 0.01),
        'w_router_f': nrm((L, D_MODEL, N_EXPERTS), D_MODEL ** -0.5),
        'b_router_f': nrm((L, N_EXPERTS), 0.01),
        'w_gate': nrm((L, N_EXPERTS, D_MODEL, EXPERT_FF), D_MODEL ** -0.5),
        'w_up': nrm((L, N_EXPERTS, D_MODEL, EXPERT_FF), D_MODEL ** -0.5),
        'w_down': nrm((L, N_EXPERTS, EXPERT_FF, D_MODEL), EXPERT_FF ** -0.5),
        'final_norm_g': gain((D_MODEL,)),
    }

def reference(x_prompt, x_sample, mem_prompt, cache_kv_latent, cache_k_rope, cache_mem_k, cache_mem_v,
              state_rwkv, state_rwkv_shift, page_table, ln_mix_g, w_in, rwkv_mu, rwkv_w0, rwkv_w_w2, rwkv_a0,
              rwkv_w_a2, rwkv_w_g2, rwkv_k_k, rwkv_k_a, rwkv_r_k, rwkv_gn_g, rwkv_gn_b, mla_q_norm_g, mla_w_qb,
              mla_kv_norm_g, mla_w_kvb, w_out, ln_mem_g, mem_norm_g, w_mq, w_mk, w_mv, w_mo, ln_moe_g,
              w_router_c, b_router_c, w_router_f, b_router_f, w_gate, w_up, w_down, final_norm_g):
    B, S, _ = x_prompt.shape
    DB, T, _ = x_sample.shape
    past_len = page_table.shape[1] * PAGE_SIZE
    cos_p, sin_p = rope_tables(jnp.arange(S))
    cos_s, sin_s = rope_tables(past_len + jnp.arange(T))
    xp, xs = x_prompt, x_sample
    kvp, kpp, mkp, mvp, stp, shp = [], [], [], [], [], []
    kvs, kps, sts, shs = [], [], [], []
    for l in range(DEPTH):
        lp = {
            'ln_mix_g': ln_mix_g[l], 'w_in': w_in[l], 'rwkv_mu': rwkv_mu[l], 'rwkv_w0': rwkv_w0[l],
            'rwkv_w_w2': rwkv_w_w2[l], 'rwkv_a0': rwkv_a0[l], 'rwkv_w_a2': rwkv_w_a2[l], 'rwkv_w_g2': rwkv_w_g2[l],
            'rwkv_k_k': rwkv_k_k[l], 'rwkv_k_a': rwkv_k_a[l], 'rwkv_r_k': rwkv_r_k[l], 'rwkv_gn_g': rwkv_gn_g[l],
            'rwkv_gn_b': rwkv_gn_b[l], 'mla_q_norm_g': mla_q_norm_g[l], 'mla_w_qb': mla_w_qb[l],
            'mla_kv_norm_g': mla_kv_norm_g[l], 'mla_w_kvb': mla_w_kvb[l], 'w_out': w_out[l],
            'ln_mem_g': ln_mem_g[l], 'w_mq': w_mq[l], 'w_mo': w_mo[l], 'ln_moe_g': ln_moe_g[l],
            'w_router_c': w_router_c[l], 'b_router_c': b_router_c[l], 'w_router_f': w_router_f[l],
            'b_router_f': b_router_f[l], 'w_gate': w_gate[l], 'w_up': w_up[l], 'w_down': w_down[l],
        }
        mem_k, mem_v = memory_kv(mem_prompt, mem_norm_g[l], w_mk[l], w_mv[l])
        prev0 = jnp.zeros((B, RWKV_PROJ), state_rwkv_shift.dtype)
        st0 = jnp.zeros((B, RWKV_HEADS, RWKV_HEAD_DIM, RWKV_HEAD_DIM), state_rwkv.dtype)
        xp, c_p, k_p, st_p, sh_p = decoder_layer(xp, cos_p, sin_p, prev0, st0, mla_attend_prompt, mem_k, mem_v, lp)
        kvp.append(c_p); kpp.append(k_p); mkp.append(mem_k); mvp.append(mem_v); stp.append(st_p); shp.append(sh_p)
        past_c = cache_kv_latent[l, page_table].reshape(DB, past_len, KV_LORA)
        past_kpe = cache_k_rope[l, page_table].reshape(DB, past_len, ROPE_DIM)
        attend_s = functools.partial(mla_attend_sample, past_c=past_c, past_kpe=past_kpe)
        xs, c_s, k_s, st_s, sh_s = decoder_layer(xs, cos_s, sin_s, state_rwkv_shift[l], state_rwkv[l], attend_s,
                                                 cache_mem_k[l], cache_mem_v[l], lp)
        kvs.append(c_s); kps.append(k_s); sts.append(st_s); shs.append(sh_s)
    y_prompt = rmsnorm(xp, final_norm_g)
    y_sample = rmsnorm(xs, final_norm_g)
    return (y_prompt, y_sample, jnp.stack(kvp), jnp.stack(kpp), jnp.stack(mkp), jnp.stack(mvp), jnp.stack(stp),
            jnp.stack(shp), jnp.stack(kvs), jnp.stack(kps), jnp.stack(sts), jnp.stack(shs))


_drawn_inputs = setup_inputs


def setup_inputs(seed=0):
    import zlib

    import numpy as np

    out = dict(_drawn_inputs(seed))
    spreads = {}
    factors = {'cache_k_rope': 4.278,
     'rwkv_gn_g': 2.791,
     'rwkv_gn_b': 2.991,
     'mla_q_norm_g': 7.729,
     'mla_kv_norm_g': 3.034,
     'ln_mem_g': 7.851,
     'mem_norm_g': 2.85,
     'b_router_c': 12.937,
     'b_router_f': 10.906,
     'final_norm_g': 8.192,
     'ln_moe_g': 7.349}
    for name, (base, spread) in spreads.items():
        noise = np.random.default_rng([zlib.crc32(name.encode()), seed]).standard_normal(out[name].shape)
        drawn = base * np.exp(spread * noise) if base else spread * noise
        out[name] = __import__('jax').numpy.asarray(drawn.astype(out[name].dtype))
    for name, factor in factors.items():
        out[name] = (out[name] * factor).astype(out[name].dtype)
    return out
```

```python
import math
from contextlib import ExitStack

import concourse.bass as bass
import numpy as np
from concourse import mybir

F32 = mybir.dt.float32
I32 = mybir.dt.int32
ALU = mybir.AluOpType
ACT = mybir.ActivationFunctionType
AX = mybir.AxisListType

D = 2048
DT = D // 128
SEQ, NB, ND = 256, 8, 8
TILE = (128, 128, NB * ND)
T = sum(TILE)
EPS = 1e-6
RW = 1024
RPROJ = 3 * RW + 96 + 96 + 256
QL, KVL, ROPE = 512, 256, 64
IN_PROJ = RPROJ + QL + KVL + ROPE
MH, NOPE, VD = 8, 128, 128
PAGE, NPG, NPHYS = 128, 16, 160
MLA_SCALE = (NOPE + ROPE) ** -0.5
MEM, MEMH = 256, 4
MEM_SCALE = 128 ** -0.5
NEG = -1e30
NG, EG = 4, 8
NE = NG * EG
FF = 512
SL = 64
SLOTS_MAX = T
ROWS = 2 * T
CH = 32
SUB = 16
NCH = SEQ // CH
HP = 8
HD = 64
DECAY = math.exp(-0.5)
GN_EPS = 64e-5
SEC = ((0, 128), (128, 128), (256, 64))

VECTORS = [("mu", 28), ("w0", 8), ("a0", 8), ("k_k", 8), ("k_a", 8), ("r_k", 8), ("gn_g", 8), ("gn_b", 8), ("ln_mix", 16),
           ("q_norm", 4), ("kv_norm", 2), ("ln_mem", 16), ("ln_moe", 16), ("mem_norm", 16)]
VECTOR_AT = {}
for _name, _n in VECTORS:
    _at = sum(n for _, n in VECTORS[:len(VECTOR_AT)])
    VECTOR_AT[_name] = (_at if _at < 106 else _at - 106 + 128, _n)

TABLES = [("ident", 128), ("headsum", 128), ("ones", 128), ("rot", 128), ("before16", T), ("after16", T), ("cross", T), ("before", T), ("upto", T),
          ("one", T), ("eye2", 64), ("own", 8), ("causal", 128), ("cos", T), ("sin", T), ("own_causal", NB * 64)]
TABLE_AT = {}
for _name, _n in TABLES:
    TABLE_AT[_name] = (sum(n for _, n in TABLES[:len(TABLE_AT)]), _n)
TABLE_W = sum(n for _, n in TABLES)


def tables():
    out = np.zeros((128, TABLE_W), np.float32)
    p = np.arange(128)[:, None]
    q = np.arange(128)[None, :]

    def put(name, value):
        at, n = TABLE_AT[name]
        out[:value.shape[0], at:at + value.shape[1]] = value

    def sections(same, order):
        a = (p // same == q // same) & order(p, q)
        b = ((p // ND == q // ND) & order(p, q))[:, :64] & (p < 64)
        return np.concatenate([a, a, b], 1)

    put("ident", p == q)
    put("headsum", p // 64 == q // 64)
    put("ones", np.ones((128, 128)))
    rot = np.zeros((128, 128))
    for b in (0, 64):
        for i in range(32):
            rot[b + 32 + i, b + i] = -1
            rot[b + i, b + 32 + i] = 1
    put("rot", rot)
    lt = lambda a, b: a < b
    put("before16", sections(SUB, lt))
    put("after16", sections(SUB, lambda a, b: a > b))
    cross = (p // CH == q // CH) & (p // SUB < q // SUB)
    put("cross", np.concatenate([cross, cross], 1))
    put("before", sections(CH, lt))
    put("upto", sections(CH, lambda a, b: a <= b))
    put("one", np.concatenate([p == q, p == q, (p == q)[:, :64]], 1))
    put("eye2", (p % 64 == q)[:, :64])
    put("own", (p // ND == q)[:64, :8])
    put("causal", np.where(q <= p, 0.0, NEG))
    inv = np.float32(10000.0) ** (-np.arange(32, dtype=np.float32) / np.float32(32))
    pos = np.concatenate([np.arange(SEQ), np.tile(NPG * PAGE + np.arange(ND), NB)]).astype(np.float32)
    ang = inv[:, None] * pos[None, :]
    put("cos", np.tile(np.cos(ang), (4, 1)))
    put("sin", np.tile(np.sin(ang), (4, 1)))
    own = np.full((64, NB, 64), NEG, np.float32)
    for b in range(NB):
        for h in range(MH):
            for t in range(ND):
                own[ND * h + t, b, ND * b:ND * b + t + 1] = 0
    put("own_causal", own.reshape(64, NB * 64))
    return out


class Shared:

    def __init__(self):
        self.finished = []

    def semaphore(self, nc, name):
        self.finished.append(nc.alloc_semaphore(name))
        return self.finished[-1]

    def recycle(self, nc):
        nc.clear_and_free_semaphores(self.finished)
        self.finished = []
        with nc.Block() as block:
            @block.gpsimd
            def _(pool):
                pool.nop()

    def vec(self, name):
        at, n = VECTOR_AT[name]
        return self.vectors[:, at:at + n]

    def table(self, name):
        at, n = TABLE_AT[name]
        return self.tables_sb[:, at:at + n]


def norm_steps(S, src, dst, gains, nt, width, bank, root, inv, sems):
    squared, summed, rooted, scaled = sems
    n = src.shape[2]

    def act_part(act):
        act.activation(dst, src, ACT.Square).then_inc(squared, 1)
        act.wait_ge(summed, 1)
        act.activation(root[:, 0:n], bank[:, 0:n], ACT.Sqrt, bias=S.eps[:, :], scale=1.0 / width).then_inc(rooted, 1)

    def pe_part(pe):
        pe.wait_ge(squared, 1)
        for t in range(nt):
            ins = pe.matmul(bank[:, 0:n], S.table("ones"), dst[:, t, :], start=(t == 0), stop=(t == nt - 1))
        ins.then_inc(summed, 1)

    def dve_part(dve):
        dve.wait_ge(rooted, 1)
        dve.reciprocal(inv[:, 0:n], root[:, 0:n]).then_inc(scaled, 1)
        dve.wait_ge(scaled, 1)
        for t in range(nt):
            ins = dve.scalar_tensor_tensor(dst[:, t, :], src[:, t, :], gains[:, t:t + 1], inv[:, 0:n], ALU.mult, ALU.mult)
        ins.then_inc(scaled, 1)

    return act_part, pe_part, dve_part


def feature_norm(nc, S, name, src, dst, gains, nt, width):
    with ExitStack() as ctx:
        sem = lambda n: S.semaphore(nc, n)
        root = ctx.enter_context(nc.sbuf_tensor(name + "_root", [128, T], F32)); inv = ctx.enter_context(nc.sbuf_tensor(name + "_inv", [128, T], F32))
        bank = ctx.enter_context(nc.psum_tensor(name + "_sum", [128, 512], F32))
        a, p, v = norm_steps(S, src, dst, gains, nt, width, bank, root, inv, [sem(name + x) for x in ("_squared", "_summed", "_rooted", "_scaled")])
        with nc.Block() as block:
            @block.scalar
            def _(act):
                a(act)

            @block.tensor
            def _(pe):
                p(pe)

            @block.vector
            def _(dve):
                v(dve)


def load_front(nc, d, S):
    with ExitStack() as ctx:
        sb = lambda n, s, t=F32: ctx.enter_context(nc.sbuf_tensor(n, s, t))
        ps = lambda n, s=(128, 512): ctx.enter_context(nc.psum_tensor(n, list(s), F32))
        sem = lambda n: S.semaphore(nc, n)
        rows = sb("vector_rows", [128, 2, 128]); x = sb("x_tokens", [128, 3, D]); prev = sb("prev_rows", [8, RPROJ])
        p_t = [ps(f"p_t{i}") for i in range(4)]; p_v = ps("p_v")
        cleared = sem("cleared"); rows_in = sem("vec_in"); x_in = [sem(f"x_in{i}") for i in range(3)]; prev_in = sem("prev_in"); tables_in = sem("tables_in")
        vec_turned = sem("vec_turned"); vec_done = sem("vec_done"); turned = sem("x_turned"); cv = sem("x_copied_v"); ca = sem("x_copied_a")
        prev_turned = sem("prev_turned"); prev_done = sem("prev_done"); parked = sem("x_parked"); xT = S.xT
        names = dict(w0='rwkv_w0', a0='rwkv_a0', k_k='rwkv_k_k', k_a='rwkv_k_a', gn_g='rwkv_gn_g', gn_b='rwkv_gn_b', ln_mix='ln_mix_g', q_norm='mla_q_norm_g',
                     kv_norm='mla_kv_norm_g', ln_mem='ln_mem_g', ln_moe='ln_moe_g', mem_norm='mem_norm_g')
        cols = [(128 * t, 128) for t in range(24)] + [(3072, 96), (3168, 96), (3264, 128), (3392, 128)]
        with nc.Block() as block:
            @block.sync
            def _(sp):
                sp.dma_start(S.tables_sb[:, :], d['tables']).then_inc(tables_in, 16)
                xp = d['x_prompt'][0].rearrange("(i p) n -> i p n", p=128)
                for i, n in enumerate(TILE):
                    sp.dma_start(x[0:n, i, :], xp[i] if i < 2 else d['x_sample'].rearrange("b t n -> (b t) n")).then_inc(x_in[i], 16)
                sp.dma_start(prev[:, :], d['state_rwkv_shift'][0]).then_inc(prev_in, 16)
                sp.wait_ge(cleared, 3)
                mu = d['rwkv_mu'][0]
                sp.dma_start(rows[0:24, 0, :], mu[0:3072].rearrange("(r n) -> r n", n=128)).then_inc(rows_in, 16)
                sp.dma_start(rows[24:26, 0, 0:96], mu[3072:3264].rearrange("(r n) -> r n", n=96)).then_inc(rows_in, 16)
                sp.dma_start(rows[26:28, 0, :], mu[3264:3520].rearrange("(r n) -> r n", n=128)).then_inc(rows_in, 16)
                for name, n in VECTORS[1:]:
                    at = VECTOR_AT[name][0]
                    src = d['rwkv_r_k'][0].rearrange("h n -> (h n)") if name == 'r_k' else d[names[name]][0]
                    sp.dma_start(rows[at % 128:at % 128 + n, at // 128, :], src.rearrange("(r n) -> r n", n=128)).then_inc(rows_in, 16)
                sp.wait_ge(cv, 6)
                sp.wait_ge(ca, 6)
                sp.dma_start(S.xT_dram, xT[:, :, :].rearrange("p t n -> p (t n)")).then_inc(parked, 16)
                sp.wait_ge(parked, 16)

            @block.gpsimd
            def _(pool):
                pool.memset(rows[:, :, :], 0.0).then_inc(cleared, 1)
                pool.memset(S.eps[:, :], EPS).then_inc(cleared, 1)
                pool.memset(S.P[:, :, :], 0.0).then_inc(cleared, 1)

            @block.tensor
            def _(pe):
                pe.wait_ge(tables_in, 16)
                pe.wait_ge(rows_in, 16 * (len(VECTORS) + 2))
                for i in range(2):
                    ins = pe.transpose(p_v[:, 128 * i:128 * i + 128], rows[:, i, :], S.ident)
                ins.then_inc(vec_turned, 1)
                pe.wait_ge(vec_done, 1)
                pe.wait_ge(prev_in, 16)
                for t, (c, n) in enumerate(cols):
                    ins = pe.transpose(p_v[0:n, 8 * t:8 * t + 8], prev[:, c:c + n], S.ident[0:8, 0:8])
                ins.then_inc(prev_turned, 1)
                k = 0
                for i, n in enumerate(TILE):
                    pe.wait_ge(x_in[i], 16)
                    for q in range(4):
                        if k >= 4:
                            pe.wait_ge((cv, ca)[k % 2], k // 2 - 1)
                        for t in range(4):
                            ins = pe.transpose(p_t[k % 4][:, n * t:n * t + n], x[0:n, i, 512 * q + 128 * t:512 * q + 128 * t + 128], S.ident[0:n, 0:n])
                        ins.then_inc(turned, 1)
                        k += 1

            def copies(eng, copy, parity, done):
                k = 0
                for i, n in enumerate(TILE):
                    for q in range(4):
                        if k % 2 == parity:
                            eng.wait_ge(turned, k + 1)
                            copy(S.xT[:, 4 * q:4 * q + 4, 128 * i:128 * i + n], p_t[k % 4][:, 0:4 * n].rearrange("p (t n) -> p t n", t=4)).then_inc(done, 1)
                        k += 1

            @block.vector
            def _(dve):
                dve.wait_ge(vec_turned, 1)
                dve.tensor_copy(S.vectors[:, :], p_v[:, 0:256]).then_inc(vec_done, 1)
                dve.wait_ge(prev_turned, 1)
                dve.wait_ge(cleared, 3)
                prev_cols = S.P[:, :, 257:329].rearrange("p t (b c) -> p t b c", c=9)[:, :, :, 0]
                src = p_v[:, 0:224].rearrange("p (t b) -> p t b", b=8)
                for lo, hi, n in ((0, 24, 128), (24, 26, 96), (26, 28, 128)):
                    dve.tensor_copy(prev_cols[0:n, lo:hi], src[0:n, lo:hi]).then_inc(prev_done, 1)
                copies(dve, dve.tensor_copy, 0, cv)

            @block.scalar
            def _(act):
                copies(act, act.copy, 1, ca)


def project_in(nc, d, S):
    with ExitStack() as ctx:
        ps = lambda n, s=(128, 512): ctx.enter_context(nc.psum_tensor(n, list(s), F32))
        sem = lambda n: S.semaphore(nc, n)
        w = [ctx.enter_context(nc.sbuf_tensor(f"w_in{i}", [128, DT, 256], F32)) for i in range(4)]
        acc = [ps(f"acc{i}") for i in range(4)]
        loaded = [sem(f"win_loaded{i}") for i in range(4)]
        done = sem("win_done"); bank_free = [sem("win_bank_v"), sem("win_bank_a")]
        src = d['w_in'][0].rearrange("(t p) n -> p t n", p=128)
        rest = [(3072, (96, 96)), (3264, (128, 128)), (3520, (128, 128)), (3776, (128, 128)), (4032, (128, 128)), (4288, (64,))]
        rest_dst = [S.P[0:96, 24], S.P[0:96, 25], S.P[:, 26], S.P[:, 27]]
        other = [S.qa[:, 0, :], S.qa[:, 1, :], S.qa[:, 2, :], S.qa[:, 3, :], S.kv[:, 0, :], S.kv[:, 1, :], S.kr[:, :]]
        with nc.Block() as block:
            @block.sync
            def _(sp):
                for s in range(4):
                    sp.dma_start(w[s][:, :, :], src[:, :, 256 * s:256 * s + 256]).then_inc(loaded[s], 16)
                with sp.Fori(1, 3) as it:
                    for s in range(4):
                        sp.wait_ge(done, 8 * it - 8 + 2 * s + 2)
                        sp.dma_start(w[s][:, :, :], src[:, :, bass.ds(1024 * it + 256 * s, 256)]).then_inc(loaded[s], 16)
                for n, (c, ms) in enumerate(rest):
                    s = n % 4
                    sp.wait_ge(done, 16 + 2 * s + 2 if n < 4 else 24 + 2 * (n - 3))
                    sp.dma_start(w[s][:, :, 0:sum(ms)], src[:, :, c:c + sum(ms)]).then_inc(loaded[s], 16)

            @block.tensor
            def _(pe):
                def tile(s, c, m, k, n_before, more=False):
                    pe.wait_ge(bank_free[k % 2], n_before + k // 2 + 1)
                    for t in range(DT):
                        ins = pe.matmul(acc[k % 4][0:m, 0:T], w[s][:, t, c:c + m], S.hT[:, t, :], start=(t == 0), stop=(t == DT - 1))
                    ins.then_inc(done, 1)

                with pe.Fori(0, 3) as it:
                    for s in range(4):
                        pe.wait_ge(loaded[s], 16 * (it + 1))
                        for m in range(2):
                            tile(s, 128 * m, 128, 2 * s + m, 4 * it)
                k = 0
                for n, (c, ms) in enumerate(rest):
                    pe.wait_ge(loaded[n % 4], 16 * (4 + n // 4))
                    o = 0
                    for m in ms:
                        tile(n % 4, o, m, k % 8, 12 + 4 * (k // 8))
                        o += m
                        k += 1

            def copy_out(eng, copy, parity):
                mine = bank_free[parity]
                eng.nop().then_inc(mine, 1)
                eng.nop().then_inc(mine, 1)

                def to_p(dst, k, m):
                    src_ = acc[k % 4][0:m, :]
                    copy(dst[:, 1:257], src_[:, 0:256])
                    return copy(dst[:, 257:329].rearrange("p (b c) -> p b c", c=9)[:, :, 1:9], src_[:, 256:320].rearrange("p (b c) -> p b c", c=8))

                with eng.Fori(0, 3) as it:
                    for k in range(parity, 8, 2):
                        eng.wait_ge(done, 8 * it + k + 1)
                        to_p(S.P[:, bass.ds(8 * it + k, 1), :].rearrange("p t n -> p (t n)"), k, 128).then_inc(mine, 1)
                for k in range(parity, 11, 2):
                    eng.wait_ge(done, 24 + k + 1)
                    if k < 4:
                        m = 96 if k < 2 else 128
                        to_p(rest_dst[k], k, m).then_inc(mine, 1)
                    else:
                        dst = other[k - 4]
                        copy(dst, acc[k % 4][0:dst.shape[0], 0:T]).then_inc(mine, 1)

            @block.vector
            def _(dve):
                copy_out(dve, dve.tensor_copy, 0)

            @block.scalar
            def _(act):
                copy_out(act, act.copy, 1)


def rwkv_mix(nc, d, S, outs):
    with ExitStack() as ctx:
        sb = lambda n, s, t=F32: ctx.enter_context(nc.sbuf_tensor(n, s, t))
        ps = lambda n, s=(128, 512): ctx.enter_context(nc.psum_tensor(n, list(s), F32))
        sem = lambda n: S.semaphore(nc, n)
        P = S.P
        diff = sb("diff", [128, 28, T])
        xw = sb("xw", [128, 4, T])
        w_w2 = sb("w_w2", [96, 1024]); w_a2 = sb("w_a2", [96, 1024])
        last = sb("last", [9, RPROJ])
        p_z = [ps("p_z0"), ps("p_z1")]; p_last = ps("p_last", (16, 512))
        lora_in = sem("lora_in"); chain = sem("mix_chain"); mixed = sem("mixed"); tanh_done = sem("tanh_done"); z_done = sem("z_done"); z_used = sem("z_used")
        last_turned = sem("last_turned"); last_copied = sem("last_copied"); last_out = sem("last_out"); lw_raw = sem("lw_raw")
        cols = [(t, 128) for t in range(24)] + [(24, 96), (25, 96), (26, 128), (27, 128)]
        starts = [128 * t for t in range(24)] + [3072, 3168, 3264, 3392]
        with nc.Block() as block:
            @block.sync
            def _(sp):
                sp.dma_start(w_w2[:, :], d['rwkv_w_w2'][0]).then_inc(lora_in, 16)
                sp.dma_start(w_a2[:, :], d['rwkv_w_a2'][0]).then_inc(lora_in, 16)
                sp.wait_ge(last_copied, 28)
                sp.dma_start(outs[7][0], last[0:1, :]).then_inc(last_out, 16)
                sp.dma_start(outs[11][0], last[1:9, :]).then_inc(last_out, 16)
                sp.wait_ge(last_out, 32)

            @block.tensor
            def _(pe):
                for n, (t, m) in enumerate(cols):
                    if n >= 1:
                        pe.wait_ge(last_copied, n)
                    pe.transpose(p_last[0:9, 0:m], P[0:m, t, 256:329:9], S.ident[0:m, 0:m]).then_inc(last_turned, 1)
                pe.wait_ge(lora_in, 32)
                pe.wait_ge(tanh_done, 1)
                pe.wait_ge(mixed, 2)
                for n in range(16):
                    if n >= 2:
                        pe.wait_ge(z_used, n - 1)
                    w = (w_w2, w_a2)[n // 8]
                    x = xw[0:96, 0, :] if n < 8 else S.xa[0:96, :]
                    pe.matmul(p_z[n % 2][:, 0:T], w[:, 128 * (n % 8):128 * (n % 8) + 128], x, start=True, stop=True).then_inc(z_done, 1)

            @block.scalar
            def _(act):
                for n, (t, m) in enumerate(cols):
                    act.wait_ge(last_turned, n + 1)
                    act.copy(last[:, starts[n]:starts[n] + m], p_last[0:9, 0:m]).then_inc(last_copied, 1)
                act.wait_ge(mixed, 2)
                act.activation(xw[0:96, 0, :], xw[0:96, 1, :], ACT.Tanh).then_inc(tanh_done, 1)
                act.activation(S.sg[:, :, :], xw[:, 2:4, :], ACT.Sigmoid).then_inc(tanh_done, 1)
                for n in range(16):
                    act.wait_ge(z_done, n + 1)
                    o, b = (S.lw, S.vec('w0')) if n < 8 else (S.a, S.vec('a0'))
                    act.activation(o[:, n % 8, :], p_z[n % 2][:, 0:T], ACT.Sigmoid, bias=b[:, n % 8:n % 8 + 1]).then_inc(z_used, 1)

            @block.vector
            def _(dve):
                sp_ = P[:, :, 257:329].rearrange("p t (b c) -> p t b c", c=9)
                dve.tensor_tensor(diff[:, :, 0:256], P[:, :, 0:256], P[:, :, 1:257], ALU.subtract).then_inc(chain, 1)
                dve.tensor_tensor(diff[:, :, 256:320].rearrange("p t (b c) -> p t b c", c=8), sp_[:, :, :, 0:8], sp_[:, :, :, 1:9], ALU.subtract).then_inc(chain, 1)
                dve.wait_ge(chain, 2)
                dst = [S.r[:, t, :] for t in range(8)] + [S.k[:, t, :] for t in range(8)] + [S.v[:, t, :] for t in range(8)] + [xw[:, 1, :], S.xa, xw[:, 2, :], xw[:, 3, :]]
                mu = S.vec('mu')
                for t in range(28):
                    dve.scalar_tensor_tensor(dst[t][:, 0:256], diff[:, t, 0:256], mu[:, t:t + 1], P[:, t, 1:257], ALU.mult, ALU.add)
                    i2 = dve.scalar_tensor_tensor(dst[t][:, 256:320].rearrange("p (b c) -> p b c", c=8), diff[:, t, 256:320].rearrange("p (b c) -> p b c", c=8),
                                                  mu[:, t:t + 1], sp_[:, t, :, 1:9], ALU.mult, ALU.add)
                    if t in (23, 27):
                        i2.then_inc(mixed, 1)
                dve.wait_ge(z_used, 8)
                dve.tensor_scalar(S.lw[:, :, :].rearrange("p t n -> p (t n)"), S.lw[:, :, :].rearrange("p t n -> p (t n)"), -DECAY, None, ALU.mult).then_inc(lw_raw, 1)


def rwkv_pairs(nc, d, S, outs):
    with ExitStack() as ctx:
        sb = lambda n, s, t=F32: ctx.enter_context(nc.sbuf_tensor(n, s, t))
        ps = lambda n, s=(128, 512): ctx.enter_context(nc.psum_tensor(n, list(s), F32))
        sem = lambda n: S.semaphore(nc, n)
        ident = S.ident
        cum = [sb("cum0", [128, T]), sb("cum1", [128, T])]
        lpm = sb("lpm", [128, T]); lpe = sb("lpe", [128, T])
        e_pos = sb("e_pos", [128, T]); e_prev = sb("e_prev", [128, T]); e_inv = sb("e_inv", [128, T]); e_end = sb("e_end", [128, T])
        e_all = sb("e_all", [128, NCH + NB])
        kn = sb("kn", [128, T]); sq = sb("sq_k", [128, T]); nrm = sb("nrm", [128, T]); kp = sb("kp", [128, T]); bb = sb("bb", [128, T])
        al = sb("al", [128, T]); rho = sb("rho", [128, T]); be = sb("be", [128, T]); ka = sb("ka", [128, T])
        bend = sb("bend", [128, T]); kend = sb("kend", [128, T]); vv = sb("vv", [128, T])
        be_t = sb("be_t", [128, 3, 128]); ke_t = sb("ke_t", [128, 3, 128]); v_t = sb("v_t", [128, 3, 128])
        X0 = sb("X0", [128, 2, 3, 128]); Y1 = sb("Y1", [128, 2, 3, 128]); Z = sb("Z", [128, 2, 2, 128]); X = sb("X", [128, 2, 3, 128])
        mat = lambda n: sb(n, [128, 2, T])
        M = {n: mat("m_" + n) for n in ("DT", "D", "D2T", "D2", "ET", "AkT", "RbT", "RkT", "TA", "TB")}
        M["D4T"], M["D4"], M["D8"] = M["DT"], M["D"], M["D2T"]
        b_exp = sb("b_exp", [64, 2, 512]); k_exp = sb("k_exp", [64, 2, 512])
        mts = sb("mts", [128, 512]); st_in = sb("st_in", [64, 8, 128]); sig0 = sb("sig0", [128, 512]); st_out = sb("st_out", [128, 512]); st_a = sb("st_a", [128, 512])
        B = [ps(f"b{i}", (128, 1024)) for i in range(4)]
        PE_ = {n: i + 1 for i, n in enumerate(["ss", "tok1", "tok2", "DT", "D", "AkT", "RbT", "RkT", "D2T", "D2", "T2", "D4T", "D4", "T4", "D8", "T8",
                                              "X0", "Y1", "Z", "W", "Rh", "sig0", "MN", "mts", "stA", "stB", "Ys"])}
        DV = {n: i + 1 for i, n in enumerate(["c0", "c1", "c2", "c3", "c4", "lp", "sq", "nrm", "kk", "rows", "DT", "D", "AkT", "RbT", "RkT", "T1", "T2", "T4", "T8",
                                             "W", "Rh", "MN", "exp", "mts", "stB"])}
        AC = {n: i + 1 for i, n in enumerate(["exps", "root", "tok1", "tok2", "D2T", "D2", "D4T", "D4", "D8", "X0", "Y1", "Z", "sig0", "stA", "Ys"])}
        mm = sem("pair_products"); dv = sem("pair_vector"); ac = sem("pair_scalar"); st_loaded = sem("st_loaded"); st_stored = sem("st_stored"); st_free = sem("st_free")
        vs = sem("pair_steps")
        NPE, NDV, NAC = len(PE_), len(DV), len(AC)
        s0, s1, s2 = SEC

        def secs(x, h):
            return [x[64 * h:64 * h + 64, c:c + n] for c, n in SEC]

        state = d['state_rwkv'][0]
        state_out = outs[10][0]
        with nc.Block() as block:
            @block.sync
            def _(sp):
                with sp.Fori(0, HP) as j:
                    sp.wait_ge(st_free, j + 1)
                    sp.nop(nofuse=True)
                    for h in range(2):
                        sp.dma_start(st_in[:, :, 64 * h:64 * h + 64], state[:, bass.ds(2 * j + h, 1), :, :].rearrange("b h v k -> v b (h k)")).then_inc(st_loaded, 16)
                    sp.wait_ge(dv, j * NDV + DV["stB"])
                    sp.nop(nofuse=True)
                    for h in range(2):
                        sp.dma_start(state_out[:, bass.ds(2 * j + h, 1), :, :].rearrange("b h v k -> v b (h k)"), st_out[64 * h:64 * h + 64, :].rearrange("v (b k) -> v b k", b=NB)).then_inc(st_stored, 16)
                    sp.wait_ge(st_stored, 32 * (j + 1))
                    sp.nop(nofuse=True)

            @block.gpsimd
            def _(pool):
                pool.nop().then_inc(st_free, 1)
                with pool.Fori(0, HP) as j:
                    pool.wait_ge(ac, j * NAC + AC["sig0"])
                    pool.nop().then_inc(st_free, 1)

            @block.tensor
            def _(pe):
                with pe.Fori(0, HP) as j:
                    V = lambda n: pe.wait_ge(dv, j * NDV + DV[n])
                    A = lambda n: pe.wait_ge(ac, j * NAC + AC[n])

                    def prods(b, lhs, rhs, name, cols=lambda c, n: (c, n)):
                        for h in range(2):
                            for i, (c, n) in enumerate(SEC):
                                l, r = lhs(h, i), rhs(h, i)
                                o, w = cols(c, n)
                                ins = pe.matmul(B[b][0:n, 512 * h + o:512 * h + o + w], l, r, start=True, stop=True)
                        ins.then_inc(mm, 1)

                    feat = lambda x: lambda h, i: x[64 * h:64 * h + 64, SEC[i][0]:SEC[i][0] + SEC[i][1]]
                    sq_ = lambda x: lambda h, i: x[0:SEC[i][1], h, SEC[i][0]:SEC[i][0] + SEC[i][1]]
                    V("sq")
                    pe.matmul(B[0][:, 0:T], S.table('headsum'), sq[:, :], start=True, stop=True)
                    pe.matmul(B[0][:, 512:512 + T], S.table('headsum'), nrm[:, :], start=True, stop=True).then_inc(mm, 1)
                    V("rows")
                    for b, name, srcs in ((1, "tok1", (al, bend)), (2, "tok2", (kend, vv))):
                        for x, src in enumerate(srcs):
                            for i, (c, n) in enumerate(SEC):
                                ins = pe.transpose(B[b][0:n, 512 * x + 128 * i:512 * x + 128 * i + 128], src[:, c:c + n], ident[:, :])
                        ins.then_inc(mm, 1)
                    prods(3, feat(be), feat(al), "DT")
                    prods(0, feat(al), feat(be), "D")
                    A("tok1"); prods(1, feat(ka), feat(al), "AkT")
                    A("tok2"); prods(2, feat(be), feat(rho), "RbT")
                    V("DT"); prods(3, feat(ka), feat(rho), "RkT")
                    V("D")
                    prods(0, sq_(M["D"]), sq_(M["DT"]), "D2T")
                    V("AkT"); prods(1, sq_(M["DT"]), sq_(M["D"]), "D2")
                    A("D2T"); A("D2"); V("T1"); V("RbT"); V("RkT")
                    prods(2, sq_(M["D2"]), sq_(M["TA"]), "T2")
                    prods(3, sq_(M["D2"]), sq_(M["D2T"]), "D4T")
                    prods(0, sq_(M["D2T"]), sq_(M["D2"]), "D4")
                    A("D4T"); A("D4"); V("T2")
                    prods(1, sq_(M["D4"]), sq_(M["TB"]), "T4")
                    prods(2, sq_(M["D4T"]), sq_(M["D4"]), "D8")
                    A("D8"); V("T4")
                    prods(3, sq_(M["D8"]), sq_(M["TA"]), "T8")
                    prods(0, sq_(M["AkT"]), lambda h, i: v_t[0:SEC[i][1], i, 64 * h:64 * h + 64], "X0", lambda c, n: (c // 2, 64))
                    A("X0"); V("T8")
                    wide = lambda x: lambda h, i: x[0:SEC[i][1], h, i, :]
                    prods(1, sq_(M["TB"]), wide(X0), "Y1", lambda c, n: (c, 128))
                    A("Y1")
                    for b, lhs, rhs, name in ((2, M["ET"], Y1, "Z"), (3, M["TB"], Z, "W")):
                        if name == "W":
                            A("Z")
                        for h in range(2):
                            for i, (c, n) in enumerate(SEC[:2]):
                                ins = pe.matmul(B[b][:, 512 * h + 128 * i:512 * h + 128 * i + 128], lhs[:, h, c:c + n], rhs[:, h, i, :], start=True, stop=True)
                        ins.then_inc(mm, 1)
                    V("W")
                    for h in range(2):
                        for i, (c, n) in enumerate(SEC):
                            pe.matmul(B[0][64 * h:64 * h + 64, c:c + n], X[0:n, h, i, 64:128], M["RbT"][0:n, h, c:c + n], start=True, stop=True)
                    for h in range(2):
                        for i, (c, n) in enumerate(SEC):
                            o = B[0][64 * h:64 * h + 64, 512 + c:512 + c + n]
                            pe.matmul(o, X[0:n, h, i, 0:64], M["RbT"][0:n, h, c:c + n], start=True, stop=False)
                            ins = pe.matmul(o, v_t[0:n, i, 64 * h:64 * h + 64], M["RkT"][0:n, h, c:c + n], start=False, stop=True)
                    ins.then_inc(mm, 1)
                    pe.wait_ge(st_loaded, 32 * (j + 1))
                    pe.nop(nofuse=True)
                    for b in range(NB):
                        ins = pe.transpose(B[1][:, 64 * b:64 * b + 64], st_in[:, b, :], ident[0:64, 0:64])
                    ins.then_inc(mm, 1)
                    V("W")
                    for c in range(NCH):
                        i, g = c // 4, c % 4
                        rows = slice(32 * g, 32 * g + 32)
                        bank = (B[2][:, 0:512], B[2][:, 512:1024], B[3][:, 0:512], B[3][:, 512:1024])[g]
                        for h in range(2):
                            hk = slice(64 * h, 64 * h + 64)
                            pe.matmul(bank[hk, 64 * i:64 * i + 64], X[rows, h, i, 64:128], be_t[rows, i, hk], start=True, stop=True)
                            o = bank[hk, 128 + 64 * i:128 + 64 * i + 64]
                            pe.matmul(o, be_t[rows, i, hk], X[rows, h, i, 0:64], start=True, stop=False)
                            ins = pe.matmul(o, ke_t[rows, i, hk], v_t[rows, i, hk], start=False, stop=True)
                    ins.then_inc(mm, 1)
                    V("exp"); A("sig0")
                    pe.nop(nofuse=True)
                    for h in range(2):
                        ins = pe.matmul(B[1][64 * h:64 * h + 64, 512:1024], X[0:64, h, 2, 64:128], b_exp[:, h, :], start=True, stop=True)
                    ins.then_inc(mm, 1)
                    V("Rh")
                    pe.nop(nofuse=True)
                    for h in range(2):
                        o = B[0][64 * h:64 * h + 64, 0:512]
                        pe.matmul(o, X[0:64, h, 2, 0:64], b_exp[:, h, :], start=True, stop=False)
                        ins = pe.matmul(o, v_t[0:64, 2, 64 * h:64 * h + 64], k_exp[:, h, :], start=False, stop=True)
                    ins.then_inc(mm, 1)
                    V("mts"); V("MN"); A("stA")
                    pe.nop(nofuse=True)
                    for h in range(2):
                        hk = slice(64 * h, 64 * h + 64)
                        for b in range(NB):
                            ins = pe.matmul(B[2][hk, 512 * h + 64 * b:512 * h + 64 * b + 64], sig0[hk, 64 * b:64 * b + 64], mts[hk, 64 * b:64 * b + 64], start=True, stop=True)
                    ins.then_inc(mm, 1)
                    for h in range(2):
                        hk = slice(64 * h, 64 * h + 64)
                        for b in range(NB):
                            ins = pe.matmul(B[3][hk, 512 * h + 8 * b:512 * h + 8 * b + 8], sig0[hk, 64 * b:64 * b + 64],
                                            rho[hk, 256 + 8 * b:256 + 8 * b + 8], start=True, stop=True)
                    ins.then_inc(mm, 1)
                    V("stB"); A("Ys")

            @block.scalar
            def _(act):
                with act.Fori(0, HP) as j:
                    V = lambda n: act.wait_ge(dv, j * NDV + DV[n])
                    Pm = lambda n: act.wait_ge(mm, j * NPE + PE_[n])
                    V("lp")
                    act.activation(e_pos[:, :], cum[1][:, :], ACT.Exp)
                    act.activation(e_prev[:, :], lpm[:, :], ACT.Exp)
                    act.activation(e_inv[:, :], cum[1][:, :], ACT.Exp, scale=-1.0)
                    act.activation(e_end[:, :], lpe[:, :], ACT.Exp)
                    act.activation(e_all[:, 0:NCH], cum[1][:, CH - 1:SEQ:CH], ACT.Exp)
                    act.activation(e_all[:, NCH:], cum[1][:, SEQ + 7:T:8], ACT.Exp).then_inc(ac, 1)
                    Pm("ss")
                    act.activation(kn[:, :], B[0][:, 0:T], ACT.Sqrt).then_inc(ac, 1)

                    def both(dst, b, name, w=128):
                        Pm(name)
                        src = B[b][:, :].rearrange("p (h n) -> p h n", h=2)
                        act.copy(dst[0:128, :, 0:256], src[0:128, :, 0:256])
                        act.copy(dst[0:64, :, 256:320], src[0:64, :, 256:320]).then_inc(ac, 1)

                    def two(dst0, dst1, b, name):
                        Pm(name)
                        act.copy(dst0[:, 0:2, :], B[b][:, 0:256].rearrange("p (i n) -> p i n", i=2))
                        act.copy(dst1[:, 0:2, :], B[b][:, 512:768].rearrange("p (i n) -> p i n", i=2))
                        act.copy(dst0[0:64, 2, :], B[b][0:64, 256:384])
                        return act.copy(dst1[0:64, 2, :], B[b][0:64, 768:896])

                    Pm("tok1")
                    for h in range(2):
                        act.copy(X0[:, h, 0:2, 64:128], B[1][:, 0:256].rearrange("p (i n) -> p i n", i=2)[:, :, 64 * h:64 * h + 64])
                        act.copy(X0[0:64, h, 2, 64:128], B[1][0:64, 256 + 64 * h:256 + 64 * h + 64])
                    act.copy(be_t[:, 0:2, :], B[1][:, 512:768].rearrange("p (i n) -> p i n", i=2))
                    act.copy(be_t[0:64, 2, :], B[1][0:64, 768:896]).then_inc(ac, 1)
                    two(ke_t, v_t, 2, "tok2").then_inc(ac, 1)
                    both(M["D2T"], 0, "D2T")
                    both(M["D2"], 1, "D2")
                    Pm("D4"); both(M["D4T"], 3, "D4T"); both(M["D4"], 0, "D4")
                    both(M["D8"], 2, "D8")
                    Pm("X0")
                    src = B[0][:, :].rearrange("p (h n) -> p h n", h=2)
                    for i, (c, n) in enumerate(SEC):
                        ins = act.copy(X0[0:n, :, i, 0:64], src[0:n, :, c // 2:c // 2 + 64])
                    ins.then_inc(ac, 1)
                    for dst, b, name in ((Y1, 1, "Y1"), (Z, 2, "Z")):
                        Pm(name)
                        src = B[b][:, :].rearrange("p (h n) -> p h n", h=2)
                        if name == "Y1":
                            act.copy(X[0:64, :, 2, :], src[0:64, :, 256:384])
                        act.copy(dst[:, :, 0:2, :].rearrange("p h i n -> p h (i n)"), src[:, :, 0:256]).then_inc(ac, 1)
                    Pm("sig0")
                    act.copy(sig0[:, :], B[1][:, 0:512]).then_inc(ac, 1)
                    Pm("stA")
                    act.copy(st_a[:, :], B[0][:, 0:512]).then_inc(ac, 1)
                    Pm("Ys")
                    V("stB")
                    act.copy(S.ys[0:64, bass.ds(j, 1), :].rearrange("p j n -> p (j n)"), B[3][0:64, 0:64])
                    act.copy(S.ys[64:128, bass.ds(j, 1), :].rearrange("p j n -> p (j n)"), B[3][64:128, 512:576]).then_inc(ac, 1)

            @block.vector
            def _(dve):
                steps = 9
                with dve.Fori(0, HP) as j:
                    k_ = [0, 0]

                    def done(ins, n=None):
                        k_[0] += 1
                        assert n is None or DV[n] == k_[0], n
                        ins.then_inc(dv, 1)
                        dve.wait_ge(dv, j * NDV + k_[0])

                    def step(ins):
                        k_[1] += 1
                        ins.then_inc(vs, 1)
                        dve.wait_ge(vs, j * steps + k_[1])

                    A = lambda n: dve.wait_ge(ac, j * NAC + AC[n])
                    Pm = lambda n: dve.wait_ge(mm, j * NPE + PE_[n])
                    at = lambda x: x[:, bass.ds(j, 1), :].rearrange("p j n -> p (j n)")
                    r, k, v, a, lw = at(S.r), at(S.k), at(S.v), at(S.a), at(S.lw)
                    src = lw
                    for n, s in enumerate((1, 2, 4, 8, 16)):
                        dst = cum[n % 2] if n < 5 else None
                        dst = cum[(n + 1) % 2]
                        pv = lambda x: x[:, 0:SEQ].rearrange("p (c t) -> p c t", t=CH)
                        sv = lambda x: x[:, SEQ:T].rearrange("p (c t) -> p c t", t=8)
                        dve.tensor_tensor(pv(dst)[:, :, s:CH], pv(src)[:, :, s:CH], pv(src)[:, :, 0:CH - s], ALU.add)
                        ins = dve.tensor_copy(pv(dst)[:, :, 0:s], pv(src)[:, :, 0:s])
                        if s < 8:
                            dve.tensor_tensor(sv(dst)[:, :, s:8], sv(src)[:, :, s:8], sv(src)[:, :, 0:8 - s], ALU.add)
                            ins = dve.tensor_copy(sv(dst)[:, :, 0:s], sv(src)[:, :, 0:s])
                        else:
                            ins = dve.tensor_copy(dst[:, SEQ:T], src[:, SEQ:T])
                        done(ins, f"c{n}")
                        src = dst
                    assert src is cum[1]
                    lp = cum[1]
                    dve.tensor_tensor(lpm[:, :], lp[:, :], lw, ALU.subtract)
                    dve.tensor_tensor(pv(lpe), pv(lp)[:, :, CH - 1:CH].to_broadcast([128, NCH, CH]), pv(lp), ALU.subtract)
                    done(dve.tensor_tensor(sv(lpe), sv(lp)[:, :, 7:8].to_broadcast([128, NB, 8]), sv(lp), ALU.subtract), "lp")
                    col = lambda n: S.vec(n)[:, bass.ds(j, 1)]
                    step(dve.tensor_scalar(kp[:, :], a, -1.0, col('k_a'), ALU.add, ALU.mult))
                    step(dve.scalar_tensor_tensor(kp[:, :], kp[:, :], 1.0, k, ALU.add, ALU.mult))
                    step(dve.tensor_scalar(bb[:, :], k, col('k_k'), None, ALU.mult))
                    step(dve.scalar_tensor_tensor(nrm[:, :], r, col('r_k'), kp[:, :], ALU.mult, ALU.mult))
                    done(dve.tensor_tensor(sq[:, :], bb[:, :], bb[:, :], ALU.mult), "sq")
                    Pm("ss"); A("root")
                    step(dve.tensor_tensor(k, B[0][:, 512:512 + T], v, ALU.mult))
                    step(dve.tensor_scalar(kn[:, :], kn[:, :], 1e-12, None, ALU.max))
                    done(dve.reciprocal(nrm[:, :], kn[:, :]), "nrm")
                    done(dve.tensor_tensor(kn[:, :], bb[:, :], nrm[:, :], ALU.mult), "kk")
                    step(dve.tensor_tensor(bb[:, :], kn[:, :], a, ALU.mult))
                    A("exps")
                    dve.scalar_tensor_tensor(al[:, :], kn[:, :], -1.0, e_prev[:, :], ALU.mult, ALU.mult)
                    dve.tensor_tensor(rho[:, :], r, e_pos[:, :], ALU.mult)
                    dve.tensor_tensor(be[:, :], bb[:, :], e_inv[:, :], ALU.mult)
                    dve.tensor_tensor(ka[:, :], kp[:, :], e_inv[:, :], ALU.mult)
                    dve.tensor_tensor(bend[:, :], bb[:, :], e_end[:, :], ALU.mult)
                    dve.tensor_tensor(kend[:, :], kp[:, :], e_end[:, :], ALU.mult)
                    done(dve.tensor_copy(vv[:, :], v), "rows")

                    def masked(dst, b, name, mask, last=True):
                        ps_ = B[b][:, :].rearrange("p (h n) -> p h n", h=2)
                        m = S.table(mask)
                        dve.tensor_tensor(dst[0:128, :, 0:256], ps_[0:128, :, 0:256], m[0:128, 0:256].unsqueeze(1).to_broadcast([128, 2, 256]), ALU.mult)
                        return dve.tensor_tensor(dst[0:64, :, 256:320], ps_[0:64, :, 256:320], m[0:64, 256:320].unsqueeze(1).to_broadcast([64, 2, 64]), ALU.mult)

                    Pm("DT")
                    masked(M["DT"], 3, "DT", "before16")
                    done(masked(M["ET"], 3, "DT", "cross"), "DT")
                    Pm("D"); done(masked(M["D"], 0, "D", "after16"), "D")
                    Pm("AkT"); done(masked(M["AkT"], 1, "AkT", "before"), "AkT")
                    Pm("RbT"); done(masked(M["RbT"], 2, "RbT", "upto"), "RbT")
                    Pm("RkT"); done(masked(M["RkT"], 3, "RkT", "upto"), "RkT")

                    def added(dst, x, b, name):
                        if b is None:
                            y = S.table('one')
                            y1 = y[0:128, 0:256].unsqueeze(1).to_broadcast([128, 2, 256]); y2 = y[0:64, 256:320].unsqueeze(1).to_broadcast([64, 2, 64])
                        else:
                            ps_ = B[b][:, :].rearrange("p (h n) -> p h n", h=2)
                            y1, y2 = ps_[0:128, :, 0:256], ps_[0:64, :, 256:320]
                        dve.tensor_tensor(dst[0:128, :, 0:256], x[0:128, :, 0:256], y1, ALU.add)
                        done(dve.tensor_tensor(dst[0:64, :, 256:320], x[0:64, :, 256:320], y2, ALU.add), name)

                    added(M["TA"], M["DT"], None, "T1")
                    Pm("T2"); added(M["TB"], M["TA"], 2, "T2")
                    Pm("T4"); added(M["TA"], M["TB"], 1, "T4")
                    Pm("T8"); added(M["TB"], M["TA"], 3, "T8")
                    Pm("W"); A("Y1")
                    done(dve.tensor_tensor(X[:, :, 0:2, :].rearrange("p h i n -> p h (i n)"), Y1[:, :, 0:2, :].rearrange("p h i n -> p h (i n)"),
                                           B[3][:, :].rearrange("p (h n) -> p h n", h=2)[:, :, 0:256], ALU.add), "W")
                    Pm("Rh")
                    step(dve.tensor_tensor(r, rho[:, :], B[0][:, 0:T], ALU.add))
                    dve.tensor_copy(rho[:, 256:320], r[:, 256:320])
                    done(dve.tensor_copy(a, B[0][:, 512:512 + T]), "Rh")
                    Pm("MN")
                    for g in range(4):
                        bank = (B[2][:, 0:512], B[2][:, 512:1024], B[3][:, 0:512], B[3][:, 512:1024])[g]
                        for i in range(2):
                            c = 4 * i + g
                            dve.scalar_tensor_tensor(S.mt[:, bass.ds(j, 1), c, :].rearrange("p j n -> p (j n)"), S.table('eye2'), e_all[:, c:c + 1], bank[:, 64 * i:64 * i + 64], ALU.mult, ALU.add)
                            ins = dve.tensor_copy(S.nn[:, c, bass.ds(j, 1), :].rearrange("p j n -> p (j n)"), bank[:, 128 + 64 * i:128 + 64 * i + 64])
                    done(ins, "MN")
                    A("tok2")
                    for dst, src in ((b_exp, be_t), (k_exp, ke_t)):
                        for h in range(2):
                            ins = dve.tensor_tensor(dst[:, h, :].rearrange("p (b k) -> p b k", b=NB), src[0:64, 2, 64 * h:64 * h + 64].unsqueeze(1).to_broadcast([64, NB, 64]),
                                                    S.table('own')[0:64, :].unsqueeze(2).to_broadcast([64, NB, 64]), ALU.mult)
                    done(ins, "exp")
                    Pm("mts")
                    step(dve.tensor_tensor(mts[:, :].rearrange("p (b k) -> p b k", b=NB), S.table('eye2').unsqueeze(1).to_broadcast([128, NB, 64]),
                                           e_all[:, NCH:].unsqueeze(2).to_broadcast([128, NB, 64]), ALU.mult))
                    done(dve.tensor_tensor(mts[:, :], mts[:, :], B[1][:, 512:1024], ALU.add), "mts")
                    Pm("stB"); A("stA")
                    for h in range(2):
                        hk = slice(64 * h, 64 * h + 64)
                        ins = dve.tensor_tensor(st_out[hk, :], st_a[hk, :], B[2][hk, 512 * h:512 * h + 512], ALU.add)
                    done(ins, "stB")
                    assert k_[0] == NDV
                    assert k_[1] == steps


def rwkv_chain(nc, d, S, outs):
    with ExitStack() as ctx:
        sb = lambda n, s, t=F32: ctx.enter_context(nc.sbuf_tensor(n, s, t))
        ps = lambda n, s=(128, 512): ctx.enter_context(nc.psum_tensor(n, list(s), F32))
        sem = lambda n: S.semaphore(nc, n)
        st = S.nn
        w_g2 = sb("w_g2", [128, 2, 1024])
        fin = sb("fin_state", [64, 16 * 64])
        mean = sb("gn_mean", [128, T]); cen = sb("gn_cen", [128, 2, T]); sqr = sb("gn_sq", [128, 2, T]); root = sb("gn_root", [128, 2, T]); inv = sb("gn_inv", [128, 2, T]); gate = sb("gn_gate", [128, 2, T])
        eps = sb("gn_eps", [128, 1])
        p_s = [ps("p_s0"), ps("p_s1")]
        p_y = [[ps("p_y00"), ps("p_y01")], [ps("p_y10"), ps("p_y11")]]
        p_a = ps("p_ga"); p_b = ps("p_gb")
        stepped = sem("stepped"); added_ = sem("state_added"); y_done = sem("prompt_y"); y_used = sem("prompt_y_added")
        fin_turned = sem("fin_turned"); fin_copied = sem("fin_copied"); fin_out = sem("fin_out"); g2_in = sem("g2_in")
        gp = sem("gn_products"); gv = sem("gn_vector"); ga = sem("gn_scalar"); gs = sem("gn_steps"); eps_set = sem("gn_eps_set")
        y = S.a
        with nc.Block() as block:
            @block.sync
            def _(sp):
                sp.dma_start(w_g2[:, :, :], d['rwkv_w_g2'][0].rearrange("(t p) n -> p t n", p=128)).then_inc(g2_in, 16)
                sp.wait_ge(fin_copied, 2)
                sp.dma_start(outs[6][0, 0].rearrange("h v k -> v h k"), fin[:, :].rearrange("v (h k) -> v h k", h=16)).then_inc(fin_out, 16)
                sp.wait_ge(fin_out, 16)

            @block.tensor
            def _(pe):
                for c in range(1, NCH):
                    if c >= 2:
                        pe.wait_ge(added_, 2 * (c - 1))
                    for h in range(2):
                        hk = slice(64 * h, 64 * h + 64)
                        for j in range(HP):
                            ins = pe.matmul(p_s[h][hk, 64 * j:64 * j + 64], S.mt[hk, j, c, :], st[hk, c - 1, j, :], start=True, stop=True)
                        ins.then_inc(stepped, 1)
                pe.wait_ge(added_, 2 * (NCH - 1))
                for q in range(4):
                    if q >= 2:
                        pe.wait_ge(y_used, 4 * (q - 1))
                    for jj in range(2):
                        j = 2 * q + jj
                        for h in range(2):
                            hk = slice(64 * h, 64 * h + 64)
                            for c in range(1, NCH):
                                ins = pe.matmul(p_y[q % 2][h][hk, 256 * jj + CH * c:256 * jj + CH * c + CH], st[hk, c - 1, j, :], S.r[hk, j, CH * c:CH * c + CH], start=True, stop=True)
                    ins.then_inc(y_done, 1)
                for j in range(HP):
                    ins = pe.transpose(p_s[j // 4][0:64, 128 * (j % 4):128 * (j % 4) + 128], st[:, NCH - 1, j, :], S.ident)
                    if j % 4 == 3:
                        ins.then_inc(fin_turned, 1)
                pe.wait_ge(g2_in, 16)
                pe.wait_ge(y_used, 16)
                pe.wait_ge(gs, 1)
                for j in range(HP):
                    if j >= 1:
                        pe.wait_ge(gv, 3 * j)
                    pe.matmul(p_a[:, 0:T], S.table('headsum'), y[:, j, :], start=True, stop=True).then_inc(gp, 1)
                    pe.wait_ge(gv, 3 * j + 1)
                    pe.matmul(p_b[:, 0:T], S.table('headsum'), sqr[:, 0, :], start=True, stop=True).then_inc(gp, 1)
                    for t in range(2):
                        ins = pe.matmul(p_a[:, 0:T], w_g2[:, t, 128 * j:128 * j + 128], S.sg[:, t, :], start=(t == 0), stop=(t == 1))
                    ins.then_inc(gp, 1)

            @block.scalar
            def _(act):
                for q in range(2):
                    act.wait_ge(fin_turned, q + 1)
                    act.copy(fin[:, 512 * q:512 * q + 512], p_s[q][0:64, :]).then_inc(fin_copied, 1)
                act.wait_ge(eps_set, 1)
                for j in range(HP):
                    act.wait_ge(gp, 3 * j + 2)
                    act.activation(root[:, 0, :], p_b[:, 0:T], ACT.Sqrt, bias=eps[:, :], scale=1.0 / HD).then_inc(ga, 1)

            @block.vector
            def _(dve):
                dve.memset(eps[:, :], GN_EPS).then_inc(eps_set, 1)
                for c in range(1, NCH):
                    for h in range(2):
                        hk = slice(64 * h, 64 * h + 64)
                        dve.wait_ge(stepped, 2 * (c - 1) + h + 1)
                        s = st[hk, c, :, :].rearrange("p j v -> p (j v)")
                        dve.tensor_tensor(s, s, p_s[h][hk, :], ALU.add).then_inc(added_, 1)
                k = 0
                for q in range(4):
                    dve.wait_ge(y_done, q + 1)
                    for jj in range(2):
                        for h in range(2):
                            hk = slice(64 * h, 64 * h + 64)
                            o = y[hk, 2 * q + jj, CH:SEQ]
                            dve.tensor_tensor(o, o, p_y[q % 2][h][hk, 256 * jj + CH:256 * jj + 256], ALU.add).then_inc(y_used, 1)
                ys = y[:, :, 256:320]
                dve.tensor_tensor(ys, ys, S.ys[:, :, :], ALU.add).then_inc(gs, 1)
                done = [1]

                def step(ins):
                    done[0] += 1
                    ins.then_inc(gs, 1)
                    dve.wait_ge(gs, done[0])

                dve.wait_ge(gs, 1)
                dve.wait_ge(y_used, 16)
                for j in range(HP):
                    dve.wait_ge(gp, 3 * j + 1)
                    step(dve.scalar_tensor_tensor(cen[:, 0, :], p_a[:, 0:T], -1.0 / HD, y[:, j, :], ALU.mult, ALU.add))
                    dve.tensor_tensor(sqr[:, 0, :], cen[:, 0, :], cen[:, 0, :], ALU.mult).then_inc(gv, 1)
                    dve.wait_ge(ga, j + 1)
                    step(dve.reciprocal(inv[:, 0, :], root[:, 0, :]))
                    step(dve.tensor_tensor(cen[:, 0, :], cen[:, 0, :], inv[:, 0, :], ALU.mult))
                    step(dve.tensor_scalar(cen[:, 0, :], cen[:, 0, :], S.vec('gn_g')[:, j:j + 1], S.vec('gn_b')[:, j:j + 1], ALU.mult, ALU.add))
                    dve.tensor_tensor(cen[:, 0, :], cen[:, 0, :], S.k[:, j, :], ALU.add).then_inc(gv, 1)
                    dve.wait_ge(gv, 3 * j + 2)
                    dve.wait_ge(gp, 3 * j + 3)
                    dve.tensor_tensor(S.mix[:, j, :], cen[:, 0, :], p_a[:, 0:T], ALU.mult).then_inc(gv, 1)
                    dve.wait_ge(gv, 3 * j + 3)


def mla_project(nc, d, S, outs):
    with ExitStack() as ctx:
        sb = lambda n, s, t=F32: ctx.enter_context(nc.sbuf_tensor(n, s, t))
        ps = lambda n, s=(128, 512): ctx.enter_context(nc.psum_tensor(n, list(s), F32))
        sem = lambda n: S.semaphore(nc, n)
        w_qb = sb("w_qb", [128, 4, MH * (NOPE + ROPE)])
        w_ukT = sb("w_ukT", [128, MH, KVL])
        q_nope = sb("q_nope", [128, MH, T]); q_raw = sb("q_raw", [64, MH, T])
        turned_q = sb("turned_q", [64, MH, T]); turned_k = sb("turned_k", [64, T]); sin_k = sb("sin_k", [64, T])
        bank = [ps(f"p_proj{i}") for i in range(4)]; p_rot = [ps("p_rot0"), ps("p_rot1")]; p_tok = [ps("p_tok0"), ps("p_tok1")]
        w_in = sem("qb_in"); produced = sem("q_produced"); copied = [sem("q_copied_v"), sem("q_copied_a")]
        rotated = sem("rotated"); rot_used = sem("rot_used"); steps = sem("rope_steps"); tok_turned = sem("tok_turned"); tok_copied = sem("tok_copied"); latents_out = sem("latents_out")
        cos, sin = S.table("cos")[0:64, :], S.table("sin")[0:64, :]
        with nc.Block() as block:
            @block.sync
            def _(sp):
                sp.dma_start(w_qb[:, :, :], d['mla_w_qb'][0].rearrange("(t p) n -> p t n", p=128)).then_inc(w_in, 16)
                sp.dma_start(S.w_kvb[:, :, :], d['mla_w_kvb'][0].rearrange("(t p) n -> p t n", p=128)).then_inc(w_in, 16)
                for i, n in enumerate(TILE):
                    sp.wait_ge(tok_copied, 2 * (i + 1))
                    for o, src in ((0, S.c_tok), (1, S.kp_tok)):
                        dst = outs[2 + o][0, 0, 128 * i:128 * i + 128, :] if i < 2 else outs[8 + o][0].rearrange("b t n -> (b t) n")
                        sp.dma_start(dst, src[0:n, i, :]).then_inc(latents_out, 16)
                sp.wait_ge(latents_out, 96)

            @block.tensor
            def _(pe):
                pe.wait_ge(w_in, 32)

                def free(k):
                    if k >= 4:
                        pe.wait_ge(copied[k % 2], k // 2 - 1)
                k = 0
                for g in range(4):
                    for hh in range(2):
                        for ci in range(2):
                            h = 2 * g + hh
                            ins = pe.transpose(bank[k % 4][:, 256 * hh + 128 * ci:256 * hh + 128 * ci + 128], S.w_kvb[:, ci, 256 * h:256 * h + 128], S.ident)
                    ins.then_inc(produced, 1)
                    k += 1
                for h in range(MH):
                    for m, c in ((128, 192 * h), (64, 192 * h + 128)):
                        free(k)
                        for t in range(4):
                            ins = pe.matmul(bank[k % 4][0:m, 0:T], w_qb[:, t, c:c + m], S.qn[:, t, :], start=(t == 0), stop=(t == 3))
                        ins.then_inc(produced, 1)
                        k += 1
                pe.wait_ge(copied[0], 10)
                pe.wait_ge(copied[1], 10)
                for h in range(MH):
                    for ci in range(2):
                        free(k)
                        pe.matmul(bank[k % 4][:, 0:T], w_ukT[:, h, 128 * ci:128 * ci + 128], q_nope[:, h, :], start=True, stop=True).then_inc(produced, 1)
                        k += 1
                for h in range(MH + 1):
                    if h >= 2:
                        pe.wait_ge(rot_used, h - 1)
                    src = q_raw[:, h, :] if h < MH else S.kr[:, :]
                    pe.matmul(p_rot[h % 2][0:64, 0:T], S.table("rot")[0:64, 0:64], src, start=True, stop=True).then_inc(rotated, 1)
                pe.wait_ge(steps, 4)
                for i, n in enumerate(TILE):
                    if i >= 2:
                        pe.wait_ge(tok_copied, 2 * (i - 1))
                    for ci in range(2):
                        pe.transpose(p_tok[i % 2][0:n, 128 * ci:128 * ci + 128], S.c[:, ci, 128 * i:128 * i + n], S.ident)
                    pe.transpose(p_tok[i % 2][0:n, 256:320], S.kp[:, 128 * i:128 * i + n], S.ident[0:64, 0:64]).then_inc(tok_turned, 1)

            def copies(eng, copy, parity):
                k = 0
                for g in range(4):
                    if k % 2 == parity:
                        eng.wait_ge(produced, k + 1)
                        copy(w_ukT[:, 2 * g:2 * g + 2, :].rearrange("p h n -> p (h n)"), bank[k % 4][:, :]).then_inc(copied[parity], 1)
                    k += 1
                for h in range(MH):
                    for m, dst in ((128, q_nope), (64, q_raw)):
                        if k % 2 == parity:
                            eng.wait_ge(produced, k + 1)
                            copy(dst[:, h, :], bank[k % 4][0:m, 0:T]).then_inc(copied[parity], 1)
                        k += 1
                for h in range(MH):
                    for ci in range(2):
                        if k % 2 == parity:
                            eng.wait_ge(produced, k + 1)
                            copy(S.q_lat[:, ci, h, :], bank[k % 4][:, 0:T]).then_inc(copied[parity], 1)
                        k += 1

            @block.vector
            def _(dve):
                copies(dve, dve.tensor_copy, 0)
                dve.wait_ge(copied[1], 10)
                dve.tensor_tensor(S.q_pe[:, :, :], q_raw[:, :, :], cos.unsqueeze(1).to_broadcast([64, MH, T]), ALU.mult).then_inc(steps, 1)
                dve.tensor_tensor(sin_k[:, :], S.kr[:, :], cos, ALU.mult).then_inc(steps, 1)
                for h in range(MH + 1):
                    dve.wait_ge(rotated, h + 1)
                    dst = turned_q[:, h, :] if h < MH else turned_k[:, :]
                    dve.tensor_tensor(dst, p_rot[h % 2][0:64, 0:T], sin, ALU.mult).then_inc(rot_used, 1)
                dve.wait_ge(rot_used, MH + 1)
                dve.wait_ge(steps, 2)
                dve.tensor_tensor(S.kp[:, :], sin_k[:, :], turned_k[:, :], ALU.add).then_inc(steps, 1)
                dve.tensor_tensor(S.q_pe[:, :, :], S.q_pe[:, :, :], turned_q[:, :, :], ALU.add).then_inc(steps, 1)

            @block.scalar
            def _(act):
                copies(act, act.copy, 1)
                for i, n in enumerate(TILE):
                    act.wait_ge(tok_turned, i + 1)
                    act.copy(S.c_tok[0:n, i, :], p_tok[i % 2][0:n, 0:256]).then_inc(tok_copied, 1)
                    act.copy(S.kp_tok[0:n, i, :], p_tok[i % 2][0:n, 256:320]).then_inc(tok_copied, 1)


def mla_prompt(nc, d, S):
    with ExitStack() as ctx:
        sb = lambda n, s, t=F32: ctx.enter_context(nc.sbuf_tensor(n, s, t))
        ps = lambda n, s=(128, 1024): ctx.enter_context(nc.psum_tensor(n, list(s), F32))
        sem = lambda n: S.semaphore(nc, n)
        score = sb("score_p", [128, 2, 4, SEQ]); prob = sb("prob_p", [128, 2, 4, SEQ]); probT = sb("probT_p", [128, 4, 2, 128])
        stat = sb("stat_p", [128, 4, 4, 4])
        p_s = [ps("pp_s0"), ps("pp_s1")]; p_t = ps("pp_t"); p_o = ps("pp_o")
        scored = sem("p_scored"); masked = sem("p_masked"); chain = sem("p_chain"); bias = sem("p_bias"); exped = sem("p_exped"); norm = sem("p_norm")
        turned = sem("p_turned"); tv = sem("p_turn_v"); ta = sem("p_turn_a"); made = sem("p_made"); ov = sem("p_out_v")
        GROUPS = [(i, q) for i in range(2) for q in range(2)]
        with nc.Block() as block:
            @block.tensor
            def _(pe):
                def scores(g):
                    i, q = GROUPS[g]
                    w = 128 * (i + 1)
                    if g >= 2:
                        pe.wait_ge(masked, g - 1)
                    for x in range(4):
                        h = 4 * q + x
                        o = p_s[g % 2][:, 256 * x:256 * x + w]
                        for ci in range(2):
                            pe.matmul(o, S.q_lat[:, ci, h, 128 * i:128 * i + 128], S.c[:, ci, 0:w], start=(ci == 0), stop=False)
                        ins = pe.matmul(o, S.q_pe[:, h, 128 * i:128 * i + 128], S.kp[:, 0:w], start=False, stop=True)
                    ins.then_inc(scored, 1)

                scores(0)
                for g, (i, q) in enumerate(GROUPS):
                    if g + 1 < 4:
                        scores(g + 1)
                    pe.wait_ge(norm, g + 1)
                    if g >= 1:
                        pe.wait_ge(tv, g)
                        pe.wait_ge(ta, g)
                    for x in range(4):
                        for b in range(i + 1):
                            ins = pe.transpose(p_t[:, 256 * x + 128 * b:256 * x + 128 * b + 128], prob[:, g % 2, x, 128 * b:128 * b + 128], S.ident)
                    ins.then_inc(turned, 1)
                    pe.wait_ge(tv, g + 1)
                    pe.wait_ge(ta, g + 1)
                    if g >= 1:
                        pe.wait_ge(ov, g)
                    for x in range(4):
                        for ci in range(2):
                            for b in range(i + 1):
                                ins = pe.matmul(p_o[:, 512 * ci + 128 * x:512 * ci + 128 * x + 128], S.c_tok[:, b, 128 * ci:128 * ci + 128], probT[:, x, b, :], start=(b == 0), stop=(b == i))
                    ins.then_inc(made, 1)

            @block.vector
            def _(dve):
                done = [0]

                def step(ins):
                    done[0] += 1
                    ins.then_inc(chain, 1)
                    dve.wait_ge(chain, done[0])

                for g, (i, q) in enumerate(GROUPS):
                    w = 128 * (i + 1)
                    dve.wait_ge(scored, g + 1)
                    src = p_s[g % 2][:, :].rearrange("p (x n) -> p x n", x=4)
                    if i == 1:
                        step(dve.tensor_copy(score[:, g % 2, :, 0:128], src[:, :, 0:128]))
                    dve.tensor_tensor(score[:, g % 2, :, w - 128:w], src[:, :, w - 128:w], S.table("causal").unsqueeze(1).to_broadcast([128, 4, 128]), ALU.add).then_inc(masked, 1)
                    dve.wait_ge(masked, g + 1)
                    step(dve.tensor_reduce(stat[:, 0, g, :], score[:, g % 2, :, 0:w], AX.X, ALU.max))
                    dve.tensor_scalar(stat[:, 1, g, :], stat[:, 0, g, :], -MLA_SCALE, None, ALU.mult).then_inc(bias, 1)
                    dve.wait_ge(exped, 4 * (g + 1))
                    step(dve.reciprocal(stat[:, 3, g, :], stat[:, 2, g, :]))
                    dve.tensor_tensor(prob[:, g % 2, :, 0:w], prob[:, g % 2, :, 0:w], stat[:, 3, g, :].unsqueeze(2).to_broadcast([128, 4, w]), ALU.mult).then_inc(norm, 1)
                    dve.wait_ge(turned, g + 1)
                    if g >= 1:
                        dve.wait_ge(made, g)
                    dve.tensor_copy(probT[:, 0:2, 0:i + 1, :], p_t[:, 0:512].rearrange("p (x b n) -> p x b n", x=2, b=2)[:, :, 0:i + 1, :]).then_inc(tv, 1)
                    dve.wait_ge(made, g + 1)
                    dve.tensor_copy(S.o_lat[:, :, 4 * q:4 * q + 4, 128 * i:128 * i + 128], p_o[:, :].rearrange("p (c x n) -> p c x n", c=2, x=4)).then_inc(ov, 1)

            @block.scalar
            def _(act):
                for g, (i, q) in enumerate(GROUPS):
                    w = 128 * (i + 1)
                    act.wait_ge(bias, g + 1)
                    if g >= 2:
                        act.wait_ge(turned, g - 1)
                    for x in range(4):
                        act.activation(prob[:, g % 2, x, 0:w], score[:, g % 2, x, 0:w], ACT.Exp, bias=stat[:, 1, g, x:x + 1], scale=MLA_SCALE,
                                       accum_out=stat[:, 2, g, x:x + 1]).then_inc(exped, 1)
                    act.wait_ge(turned, g + 1)
                    if g >= 1:
                        act.wait_ge(made, g)
                    act.copy(probT[:, 2:4, 0:i + 1, :], p_t[:, 512:1024].rearrange("p (x b n) -> p x b n", x=2, b=2)[:, :, 0:i + 1, :]).then_inc(ta, 1)


def mla_sample(nc, d, S):
    with ExitStack() as ctx:
        sb = lambda n, s, t=F32: ctx.enter_context(nc.sbuf_tensor(n, s, t))
        ps = lambda n, s=(128, 512): ctx.enter_context(nc.psum_tensor(n, list(s), F32))
        sem = lambda n: S.semaphore(nc, n)
        pages = sb("page_numbers", [1, NB * NPG], I32)
        lat = [sb(f"lat{i}", [128, NPG, KVL]) for i in range(2)]; rope = [sb(f"rope{i}", [128, NPG, ROPE]) for i in range(2)]
        kT = sb("kT", [128, 2, NPG * PAGE]); kpT = sb("kpT", [64, NPG * PAGE])
        qs = sb("q_of_sample", [128, 2, MH, ND]); qps = sb("qp_of_sample", [64, MH, ND])
        prob = sb("prob_s", [128, 1024]); probT = sb("probT_s", [128, 8, 128])
        new = sb("new_scores", [64, 64]); p_new = sb("p_new", [64, 64]); p_newT = sb("p_newT", [64, 64])
        stat = sb("stat_s", [128, 12]); o_rows = sb("o_rows", [128, KVL]); o_sum = sb("o_half", [128, 2, 64])
        p_s = ps("ps_s", (128, 1024)); p_t = [ps("ps_t0"), ps("ps_t1")]; p_n = ps("ps_n"); p_pt = ps("ps_pt", (128, 1024)); p_o = ps("ps_o")
        table_in = sem("page_table_in"); lat_in = [sem(f"lat_in{i}") for i in range(2)]; rope_in = [sem(f"rope_in{i}") for i in range(2)]
        turned = sem("k_turned"); kept = [sem("k_copied_v"), sem("k_copied_a")]; q_ready = sem("sq_ready"); scored = sem("s_scored"); chain = sem("s_chain"); bias = sem("s_bias")
        exped = sem("s_exped"); p_turned = sem("s_p_turned"); p_v = sem("s_pt_v"); p_a = sem("s_pt_a"); made = sem("s_made"); rows = sem("s_rows"); o_turned = sem("s_o_turned"); stored = sem("s_kept")
        NI = 12

        def samples(eng, first, body):
            first()
            with eng.Fori(0, 3) as it:
                for par in range(2):
                    body(2 * it + par, par, it)
            for par in range(2):
                body(6 + par, par, 3)

        with nc.Block() as block:
            def load_pages(eng, cache, dst, done):
                def one(b, par):
                    with eng.Fori(0, NPG) as p:
                        page = eng.value_load(pages[0:1, bass.ds(NPG * b + p, 1)], min_val=0, max_val=NPHYS - 1)
                        eng.dma_start(dst[par][:, bass.ds(p, 1), :], cache[bass.ds(page, 1), :, :].rearrange("i p n -> p i n")).then_inc(done[par], 16)
                one(0, 0)
                one(1, 1)
                with eng.Fori(1, NB // 2) as it:
                    for par in range(2):
                        eng.wait_ge(made, 2 * it + par - 1)
                        eng.nop(nofuse=True)
                        one(2 * it + par, par)

            @block.sync
            def _(sp):
                sp.dma_start(pages[:, :], d['page_table'].rearrange("b n -> (b n)").unsqueeze(0)).then_inc(table_in, 16)
                sp.wait_ge(table_in, 16)
                load_pages(sp, d['cache_kv_latent'][0], lat, lat_in)

            @block.gpsimd
            def _(pool):
                pool.wait_ge(table_in, 16)
                load_pages(pool, d['cache_k_rope'][0], rope, rope_in)

            @block.tensor
            def _(pe):
                def turn(b, par, it):
                    pe.wait_ge(lat_in[par], 16 * NPG * (it + 1))
                    pe.wait_ge(rope_in[par], 16 * NPG * (it + 1))
                    for k in range(NI):
                        pe.wait_ge(kept[k % 2], NI // 2 * b + k // 2)
                        if k < 8:
                            for ci in range(2):
                                for x in range(2):
                                    ins = pe.transpose(p_t[k % 2][:, 256 * ci + 128 * x:256 * ci + 128 * x + 128], lat[par][:, 2 * k + x, 128 * ci:128 * ci + 128], S.ident)
                        else:
                            pe.nop(nofuse=True)
                            for x in range(4):
                                ins = pe.transpose(p_t[k % 2][0:64, 128 * x:128 * x + 128], rope[par][:, 4 * (k - 8) + x, :], S.ident)
                        ins.then_inc(turned, 1)

                def body(b, par, it):
                    for e in range(2):
                        pe.wait_ge(kept[e], NI // 2 * (b + 1))
                    pe.wait_ge(q_ready, b + 1)
                    pe.wait_ge(exped, b)
                    pe.wait_ge(stored, b)
                    for kc in range(4):
                        o = p_s[64 * (kc // 2):64 * (kc // 2) + 64, 512 * (kc % 2):512 * (kc % 2) + 512]
                        for ci in range(2):
                            pe.matmul(o, qs[:, ci, :, :].rearrange("p h t -> p (h t)"), kT[:, ci, 512 * kc:512 * kc + 512], start=(ci == 0), stop=False)
                        pe.matmul(o, qps[:, :, :].rearrange("p h t -> p (h t)"), kpT[:, 512 * kc:512 * kc + 512], start=False, stop=True)
                    for ci in range(2):
                        pe.matmul(p_n[0:64, 0:64], qs[:, ci, :, :].rearrange("p h t -> p (h t)"), S.c[:, ci, SEQ:T], start=(ci == 0), stop=False)
                    pe.matmul(p_n[0:64, 0:64], qps[:, :, :].rearrange("p h t -> p (h t)"), S.kp[:, SEQ:T], start=False, stop=True).then_inc(scored, 1)
                    if not isinstance(b, int) or b + 1 < NB:
                        turn(b + 1, 1 - par, it + par)
                    pe.wait_ge(exped, b + 1)
                    for j in range(8):
                        pe.transpose(p_pt[:, 128 * j:128 * j + 128], prob[:, 128 * j:128 * j + 128], S.ident)
                    pe.transpose(p_n[0:64, 64:128], p_new[:, :], S.ident[0:64, 0:64]).then_inc(p_turned, 1)
                    pe.wait_ge(p_v, b + 1)
                    pe.wait_ge(p_a, b + 1)
                    for j in range(8):
                        for half in range(2):
                            ins = pe.matmul(p_o[64 * half:64 * half + 64, 0:KVL], probT[:, j, 64 * half:64 * half + 64], lat[par][:, 8 * half + j, :], start=(j == 0), stop=(j == 7 and half == 1))
                    pe.matmul(p_o[0:64, 0:KVL], p_newT[:, :], S.c_tok[0:64, 2, :], start=False, stop=True).then_inc(made, 1)
                    pe.wait_ge(rows, b + 1)
                    for ci in range(2):
                        ins = pe.transpose(p_n[:, 256 + 128 * ci:256 + 128 * ci + 128], o_rows[:, 128 * ci:128 * ci + 128], S.ident)
                    ins.then_inc(o_turned, 1)

                samples(pe, lambda: turn(0, 0, 0), body)

            def keep(eng, copy, parity, b):
                for k in range(parity, NI, 2):
                    eng.wait_ge(turned, NI * b + k + 1)
                    if k < 8:
                        ins = copy(kT[:, :, 256 * k:256 * k + 256], p_t[parity][:, :].rearrange("p (c n) -> p c n", c=2))
                    else:
                        ins = copy(kpT[:, 512 * (k - 8):512 * (k - 8) + 512], p_t[parity][0:64, :])
                    ins.then_inc(kept[parity], 1)

            @block.vector
            def _(dve):
                STEPS = 12

                def body(b, par, it):
                    done = [0]

                    def step(ins):
                        done[0] += 1
                        ins.then_inc(chain, 1)
                        dve.wait_ge(chain, STEPS * b + done[0])

                    dve.wait_ge(scored, b + 1)
                    st = lambda k, half=0: stat[64 * half:64 * half + 64, k:k + 1]
                    dve.tensor_reduce(stat[:, 0:1], p_s[:, :], AX.X, ALU.max)
                    step(dve.tensor_tensor(new[:, :], p_n[0:64, 0:64], S.table("own_causal")[0:64, bass.ds(64 * b, 64)], ALU.add))
                    dve.tensor_copy(st(1), st(0, 1))
                    step(dve.tensor_reduce(st(2), new[:, :], AX.X, ALU.max))
                    step(dve.tensor_tensor(st(3), st(0), st(2), ALU.max))
                    step(dve.tensor_tensor(st(3), st(3), st(1), ALU.max))
                    step(dve.tensor_scalar(st(4), st(3), -MLA_SCALE, None, ALU.mult))
                    dve.tensor_copy(st(4, 1), st(4)).then_inc(bias, 1)
                    if not isinstance(b, int) or b + 1 < NB:
                        keep(dve, dve.tensor_copy, 0, b + 1)
                    dve.wait_ge(exped, b + 1)
                    step(dve.tensor_copy(st(7), st(5, 1)))
                    step(dve.tensor_tensor(st(8), st(5), st(6), ALU.add))
                    step(dve.tensor_tensor(st(8), st(8), st(7), ALU.add))
                    step(dve.reciprocal(st(9), st(8)))
                    step(dve.tensor_copy(st(9, 1), st(9)))
                    dve.wait_ge(p_turned, b + 1)
                    dve.tensor_copy(probT[:, 0:4, :].rearrange("p j n -> p (j n)"), p_pt[:, 0:512]).then_inc(p_v, 1)
                    dve.wait_ge(made, b + 1)
                    dve.tensor_scalar(o_rows[:, :], p_o[:, 0:KVL], stat[:, 9:10], None, ALU.mult).then_inc(rows, 1)
                    dve.wait_ge(o_turned, b + 1)
                    src = p_n[:, 256:512].rearrange("p (c half n) -> p c half n", c=2, half=2)
                    step(dve.tensor_copy(o_sum[:, :, :], src[:, :, 0, :]))
                    for ci in range(2):
                        ins = dve.tensor_tensor(S.o_lat[:, ci, :, bass.ds(SEQ + ND * b, ND)], o_sum[:, ci, :].rearrange("p (h t) -> p h t", h=MH),
                                                src[:, ci, 1, :].rearrange("p (h t) -> p h t", h=MH), ALU.add)
                        if ci == 0:
                            step(ins)
                    ins.then_inc(stored, 1)
                    assert done[0] == 12

                samples(dve, lambda: keep(dve, dve.tensor_copy, 0, 0), body)

            @block.scalar
            def _(act):
                def queries(b):
                    act.copy(qs[:, :, :, :].rearrange("p c h t -> p (c h) t"), S.q_lat[:, :, :, bass.ds(SEQ + ND * b, ND)].rearrange("p c h t -> p (c h) t"))
                    act.copy(qps[:, :, :], S.q_pe[:, :, bass.ds(SEQ + ND * b, ND)]).then_inc(q_ready, 1)

                def first():
                    queries(0)
                    keep(act, act.copy, 1, 0)

                def body(b, par, it):
                    act.wait_ge(bias, b + 1)
                    act.activation(prob[:, :], p_s[:, :], ACT.Exp, bias=stat[:, 4:5], scale=MLA_SCALE, accum_out=stat[:, 5:6])
                    act.activation(p_new[:, :], new[:, :], ACT.Exp, bias=stat[0:64, 4:5], scale=MLA_SCALE, accum_out=stat[0:64, 6:7]).then_inc(exped, 1)
                    if not isinstance(b, int) or b + 1 < NB:
                        queries(b + 1)
                        keep(act, act.copy, 1, b + 1)
                    act.wait_ge(p_turned, b + 1)
                    act.copy(p_newT[:, :], p_n[0:64, 64:128])
                    act.copy(probT[:, 4:8, :].rearrange("p j n -> p (j n)"), p_pt[:, 512:1024]).then_inc(p_a, 1)
                    act.wait_ge(made, b + 1)

                samples(act, first, body)


def mla_out(nc, S):
    with ExitStack() as ctx:
        bank = [ctx.enter_context(nc.psum_tensor(f"p_uv{i}", [128, 512], F32)) for i in range(4)]
        made = S.semaphore(nc, "uv_made"); copied = [S.semaphore(nc, "uv_copied_v"), S.semaphore(nc, "uv_copied_a")]
        with nc.Block() as block:
            @block.tensor
            def _(pe):
                for h in range(MH):
                    if h >= 4:
                        pe.wait_ge(copied[h % 2], h // 2 - 1)
                    for ci in range(2):
                        ins = pe.matmul(bank[h % 4][:, 0:T], S.w_kvb[:, ci, 256 * h + 128:256 * h + 256], S.o_lat[:, ci, h, :], start=(ci == 0), stop=(ci == 1))
                    ins.then_inc(made, 1)

            def copies(eng, copy, parity):
                for h in range(parity, MH, 2):
                    eng.wait_ge(made, h + 1)
                    copy(S.mix[:, 8 + h, :], bank[h % 4][:, 0:T]).then_inc(copied[parity], 1)

            @block.vector
            def _(dve):
                copies(dve, dve.tensor_copy, 0)

            @block.scalar
            def _(act):
                copies(act, act.copy, 1)


def project_out(nc, d, S):
    with ExitStack() as ctx:
        ps = lambda n, s=(128, 512): ctx.enter_context(nc.psum_tensor(n, list(s), F32))
        sem = lambda n: S.semaphore(nc, n)
        w = [ctx.enter_context(nc.sbuf_tensor(f"w_out{i}", [128, DT, 256], F32)) for i in range(4)]
        acc = [ps(f"acc_out{i}") for i in range(4)]
        loaded = [sem(f"wout_loaded{i}") for i in range(4)]; x_in = sem("xT_in"); done = sem("wout_done"); added = sem("wout_added")
        src = d['w_out'][0].rearrange("(t p) n -> p t n", p=128)
        with nc.Block() as block:
            @block.sync
            def _(sp):
                for s in range(4):
                    sp.dma_start(w[s][:, :, :], src[:, :, 256 * s:256 * s + 256]).then_inc(loaded[s], 16)
                sp.dma_start(S.xT[:, :, :].rearrange("p t n -> p (t n)"), S.xT_dram).then_inc(x_in, 16)
                for s in range(4):
                    sp.wait_ge(done, 2 * s + 2)
                    sp.dma_start(w[s][:, :, :], src[:, :, 1024 + 256 * s:1024 + 256 * s + 256]).then_inc(loaded[s], 16)

            @block.tensor
            def _(pe):
                with pe.Fori(0, 2) as it:
                    for s in range(4):
                        pe.wait_ge(loaded[s], 16 * (it + 1))
                        for m in range(2):
                            k = 2 * s + m
                            pe.wait_ge(added, 8 * it + k + 1)
                            for t in range(DT):
                                ins = pe.matmul(acc[k % 4][:, 0:T], w[s][:, t, 128 * m:128 * m + 128], S.mix[:, t, :], start=(t == 0), stop=(t == DT - 1))
                            ins.then_inc(done, 1)

            @block.vector
            def _(dve):
                for _ in range(4):
                    dve.nop().then_inc(added, 1)
                dve.wait_ge(x_in, 16)
                with dve.Fori(0, 2) as it:
                    for k in range(8):
                        dve.wait_ge(done, 8 * it + k + 1)
                        x = S.xT[:, bass.ds(8 * it + k, 1), :].rearrange("p t n -> p (t n)")
                        dve.tensor_tensor(x, x, acc[k % 4][:, 0:T], ALU.add).then_inc(added, 1)


def memory_keys(nc, d, S, outs):
    with ExitStack() as ctx:
        sb = lambda n, s, t=F32: ctx.enter_context(nc.sbuf_tensor(n, s, t))
        sem = lambda n: S.semaphore(nc, n)
        mem_n = sb("mem_n", [128, DT, MEM])
        w = [sb("w_mk", [128, DT, 512]), sb("w_mv", [128, DT, 512])]
        w_in = [sem("wmk_in"), sem("wmv_in")]
        with ExitStack() as c1:
            mem = c1.enter_context(nc.sbuf_tensor("mem_tokens", [128, 2, D], F32)); memT = c1.enter_context(nc.sbuf_tensor("memT", [128, DT, MEM], F32))
            p_t = [c1.enter_context(nc.psum_tensor(f"pm_t{i}", [128, 512], F32)) for i in range(4)]
            mem_in = S.semaphore(nc, "mem_in"); turned = S.semaphore(nc, "mem_turned")
            copied = [S.semaphore(nc, "mem_copied_v"), S.semaphore(nc, "mem_copied_a")]
            with nc.Block() as block:
                @block.sync
                def _(sp):
                    sp.dma_start(mem[:, :, :], d['mem_prompt'][0].rearrange("(i p) n -> p i n", p=128)).then_inc(mem_in, 16)
                    for x, n in ((0, 'w_mk'), (1, 'w_mv')):
                        sp.dma_start(w[x][:, :, :], d[n][0].rearrange("(t p) n -> p t n", p=128)).then_inc(w_in[x], 16)

                @block.tensor
                def _(pe):
                    pe.wait_ge(mem_in, 16)
                    for k in range(8):
                        if k >= 4:
                            pe.wait_ge(copied[k % 2], k // 2 - 1)
                        for t in range(2):
                            for i in range(2):
                                ins = pe.transpose(p_t[k % 4][:, 256 * t + 128 * i:256 * t + 128 * i + 128], mem[:, i, 128 * (2 * k + t):128 * (2 * k + t) + 128], S.ident)
                        ins.then_inc(turned, 1)

                def copies(eng, copy, parity):
                    for k in range(parity, 8, 2):
                        eng.wait_ge(turned, k + 1)
                        copy(memT[:, 2 * k:2 * k + 2, :].rearrange("p t n -> p (t n)"), p_t[k % 4][:, :]).then_inc(copied[parity], 1)

                @block.vector
                def _(dve):
                    copies(dve, dve.tensor_copy, 0)

                @block.scalar
                def _(act):
                    copies(act, act.copy, 1)
            feature_norm(nc, S, "norm_memory", memT[:, :, :], mem_n[:, :, :], S.vec("mem_norm"), DT, D)
        mem_k = sb("mem_k", [128, 2, 512])
        bank = [ctx.enter_context(nc.psum_tensor(f"pm_kv{i}", [128, 512], F32)) for i in range(4)]; p_kt = [ctx.enter_context(nc.psum_tensor(f"pm_kt{i}", [128, 512], F32)) for i in range(2)]
        made = sem("mkv_made"); copied = sem("mkv_copied"); k_turned = sem("mk_turned"); k_kept = sem("mk_kept"); out = sem("mkv_out")
        with nc.Block() as block:
            @block.sync
            def _(sp):
                for x, buf in ((0, mem_k), (1, S.mem_v)):
                    for i in range(2):
                        sp.wait_ge(copied, 2 * x + i + 1)
                        sp.dma_start(outs[4 + x][0, 0, 128 * i:128 * i + 128].rearrange("p h n -> p (h n)"), buf[:, i, :]).then_inc(out, 16)
                sp.wait_ge(out, 64)

            @block.tensor
            def _(pe):
                for x in range(2):
                    pe.wait_ge(w_in[x], 16)
                    for i in range(2):
                        for t in range(DT):
                            ins = pe.matmul(bank[2 * x + i][:, :], mem_n[:, t, 128 * i:128 * i + 128], w[x][:, t, :], start=(t == 0), stop=(t == DT - 1))
                        ins.then_inc(made, 1)
                pe.wait_ge(copied, 2)
                for h in range(MEMH):
                    for i in range(2):
                        ins = pe.transpose(p_kt[h // 2][:, 256 * (h % 2) + 128 * i:256 * (h % 2) + 128 * i + 128], mem_k[:, i, 128 * h:128 * h + 128], S.ident)
                    if h % 2:
                        ins.then_inc(k_turned, 1)

            @block.vector
            def _(dve):
                for x, buf in ((0, mem_k), (1, S.mem_v)):
                    for i in range(2):
                        dve.wait_ge(made, 2 * x + i + 1)
                        dve.tensor_copy(buf[:, i, :], bank[2 * x + i][:, :]).then_inc(copied, 1)
                for q in range(2):
                    dve.wait_ge(k_turned, q + 1)
                    dve.tensor_copy(S.mem_kT[:, 2 * q:2 * q + 2, :].rearrange("p h n -> p (h n)"), p_kt[q][:, :]).then_inc(k_kept, 1)


def memory_queries(nc, d, S):
    with ExitStack() as ctx:
        w = ctx.enter_context(nc.sbuf_tensor("w_mq", [128, DT, 512], F32))
        bank = [ctx.enter_context(nc.psum_tensor(f"p_mq{i}", [128, 512], F32)) for i in range(MEMH)]
        w_in = S.semaphore(nc, "wmq_in"); made = S.semaphore(nc, "mq_made"); copied = S.semaphore(nc, "mq_copied")
        with nc.Block() as block:
            @block.sync
            def _(sp):
                sp.dma_start(w[:, :, :], d['w_mq'][0].rearrange("(t p) n -> p t n", p=128)).then_inc(w_in, 16)

            @block.tensor
            def _(pe):
                pe.wait_ge(w_in, 16)
                for h in range(MEMH):
                    for t in range(DT):
                        ins = pe.matmul(bank[h][:, 0:T], w[:, t, 128 * h:128 * h + 128], S.mix[:, t, :], start=(t == 0), stop=(t == DT - 1))
                    ins.then_inc(made, 1)

            @block.vector
            def _(dve):
                for h in range(MEMH):
                    dve.wait_ge(made, h + 1)
                    dve.tensor_copy(S.mem_q[:, h, :], bank[h][:, 0:T]).then_inc(copied, 1)


def memory_prompt(nc, S):
    with ExitStack() as ctx:
        sb = lambda n, s, t=F32: ctx.enter_context(nc.sbuf_tensor(n, s, t))
        ps = lambda n, s=(128, 1024): ctx.enter_context(nc.psum_tensor(n, list(s), F32))
        sem = lambda n: S.semaphore(nc, n)
        prob = sb("prob_m", [128, 2, MEMH, MEM]); probT = sb("probT_m", [128, 2, MEMH, 2, 128]); stat = sb("stat_m", [128, 4, 2, MEMH])
        p_s = [ps("pm_s0"), ps("pm_s1")]; p_t = ps("pm_turn"); p_o = ps("pm_o")
        scored = sem("mp_scored"); chain = sem("mp_chain"); bias = sem("mp_bias"); exped = sem("mp_exped"); norm = sem("mp_norm"); turned = sem("mp_turned"); kept = sem("mp_kept"); made = sem("mp_made"); out = sem("mp_out")
        with nc.Block() as block:
            @block.tensor
            def _(pe):
                for i in range(2):
                    for h in range(MEMH):
                        ins = pe.matmul(p_s[i][:, 256 * h:256 * h + 256], S.mem_q[:, h, 128 * i:128 * i + 128], S.mem_kT[:, h, :], start=True, stop=True)
                    ins.then_inc(scored, 1)
                for i in range(2):
                    pe.wait_ge(norm, i + 1)
                    if i:
                        pe.wait_ge(kept, 1)
                    for h in range(MEMH):
                        for b in range(2):
                            ins = pe.transpose(p_t[:, 256 * h + 128 * b:256 * h + 128 * b + 128], prob[:, i, h, 128 * b:128 * b + 128], S.ident)
                    ins.then_inc(turned, 1)
                    pe.wait_ge(kept, i + 1)
                    for h in range(MEMH):
                        for b in range(2):
                            ins = pe.matmul(p_o[:, 512 * i + 128 * h:512 * i + 128 * h + 128], S.mem_v[:, b, 128 * h:128 * h + 128], probT[:, i, h, b, :], start=(b == 0), stop=(b == 1))
                    ins.then_inc(made, 1)

            @block.vector
            def _(dve):
                done = [0]

                def step(ins):
                    done[0] += 1
                    ins.then_inc(chain, 1)
                    dve.wait_ge(chain, done[0])

                for i in range(2):
                    dve.wait_ge(scored, i + 1)
                    step(dve.tensor_reduce(stat[:, 0, i, :], p_s[i][:, :].rearrange("p (h n) -> p h n", h=MEMH), AX.X, ALU.max))
                    dve.tensor_scalar(stat[:, 1, i, :], stat[:, 0, i, :], -MEM_SCALE, None, ALU.mult).then_inc(bias, 1)
                for i in range(2):
                    dve.wait_ge(exped, MEMH * (i + 1))
                    step(dve.reciprocal(stat[:, 3, i, :], stat[:, 2, i, :]))
                    dve.tensor_tensor(prob[:, i, :, :], prob[:, i, :, :], stat[:, 3, i, :].unsqueeze(2).to_broadcast([128, MEMH, MEM]), ALU.mult).then_inc(norm, 1)
                for i in range(2):
                    dve.wait_ge(made, i + 1)
                    dve.tensor_copy(S.mem_o[:, :, 128 * i:128 * i + 128], p_o[:, 512 * i:512 * i + 512].rearrange("p (h n) -> p h n", h=MEMH)).then_inc(out, 1)

            @block.scalar
            def _(act):
                for i in range(2):
                    act.wait_ge(bias, i + 1)
                    for h in range(MEMH):
                        act.activation(prob[:, i, h, :], p_s[i][:, 256 * h:256 * h + 256], ACT.Exp, bias=stat[:, 1, i, h:h + 1], scale=MEM_SCALE, accum_out=stat[:, 2, i, h:h + 1]).then_inc(exped, 1)
                for i in range(2):
                    act.wait_ge(turned, i + 1)
                    act.copy(probT[:, i, :, :, :].rearrange("p h b n -> p (h b n)"), p_t[:, :]).then_inc(kept, 1)


def memory_sample(nc, d, S):
    with ExitStack() as ctx:
        sb = lambda n, s, t=F32: ctx.enter_context(nc.sbuf_tensor(n, s, t))
        sem = lambda n: S.semaphore(nc, n)
        kT = sb("mem_kT_s", [128, NB, MEMH, MEM]); v = sb("mem_v_s", [128, NB, 2, 512])
        q = sb("mem_q_s", [128, NB, MEMH, 32]); stat = sb("stat_ms", [128, 4, NB])
        k_in = sem("msk_in"); v_in = sem("msv_in"); q_ready = sem("ms_q")
        with ExitStack() as c1:
            k = c1.enter_context(nc.sbuf_tensor("mem_k_s", [128, NB, 2, 512], F32))
            p_t = [c1.enter_context(nc.psum_tensor(f"pms_t{i}", [128, 1024], F32)) for i in range(4)]
            turned = S.semaphore(nc, "msk_turned"); copied = [S.semaphore(nc, "msk_copied_v"), S.semaphore(nc, "msk_copied_a")]
            with nc.Block() as block:
                @block.sync
                def _(sp):
                    for b in range(NB):
                        sp.dma_start(k[:, b, :, :], d['cache_mem_k'][0, b].rearrange("(i p) h n -> p i (h n)", p=128)).then_inc(k_in, 16)
                    for b in range(NB):
                        sp.dma_start(v[:, b, :, :], d['cache_mem_v'][0, b].rearrange("(i p) h n -> p i (h n)", p=128)).then_inc(v_in, 16)
                    sp.wait_ge(v_in, 16 * NB)

                @block.tensor
                def _(pe):
                    pe.wait_ge(k_in, 16 * NB)
                    for b in range(NB):
                        if b >= 4:
                            pe.wait_ge(copied[b % 2], b // 2 - 1)
                        for h in range(MEMH):
                            for i in range(2):
                                ins = pe.transpose(p_t[b % 4][:, 256 * h + 128 * i:256 * h + 128 * i + 128], k[:, b, i, 128 * h:128 * h + 128], S.ident)
                        ins.then_inc(turned, 1)

                def copies(eng, copy, parity):
                    for b in range(parity, NB, 2):
                        eng.wait_ge(turned, b + 1)
                        copy(kT[:, b, :, :].rearrange("p h n -> p (h n)"), p_t[b % 4][:, :]).then_inc(copied[parity], 1)

                @block.gpsimd
                def _(pool):
                    pool.memset(q[:, :, :, :], 0.0).then_inc(q_ready, 1)
                    pool.wait_ge(q_ready, 1)
                    pool.tensor_copy(q[:, :, :, 0:ND].rearrange("p b h t -> p h b t"), S.mem_q[:, :, SEQ:T].rearrange("p h (b t) -> p h b t", b=NB)).then_inc(q_ready, 1)
                    pool.wait_ge(q_ready, 2)

                @block.vector
                def _(dve):
                    copies(dve, dve.tensor_copy, 0)

                @block.scalar
                def _(act):
                    copies(act, act.copy, 1)
        with ExitStack() as c1:
            prob = c1.enter_context(nc.sbuf_tensor("prob_ms", [128, NB, MEM], F32)); probT = c1.enter_context(nc.sbuf_tensor("probT_ms", [128, NB, 2, 128], F32))
            o_rows = c1.enter_context(nc.sbuf_tensor("o_rows_ms", [128, NB, 128], F32))
            pa = [c1.enter_context(nc.psum_tensor(f"pms_a{i}", [128, 1024], F32)) for i in range(2)]; pb = [c1.enter_context(nc.psum_tensor(f"pms_b{i}", [128, 1024], F32)) for i in range(2)]
            s1 = lambda n: S.semaphore(nc, n)
            scored = s1("ms_scored"); chain = s1("ms_chain"); ready = s1("ms_shifted"); exped = s1("ms_exped"); turned = s1("ms_turned"); kept = [s1("ms_kept_v"), s1("ms_kept_a")]
            made = s1("ms_made"); rows = s1("ms_rows"); o_turned = s1("ms_o_turned")
            with nc.Block() as block:
                @block.tensor
                def _(pe):
                    for b in range(NB):
                        for h in range(MEMH):
                            ins = pe.matmul(pa[b // 4][32 * h:32 * h + 32, 256 * (b % 4):256 * (b % 4) + 256], q[:, b, h, :], kT[:, b, h, :], start=True, stop=True)
                    ins.then_inc(scored, 1)
                    pe.wait_ge(exped, 1)
                    for b in range(NB):
                        for i in range(2):
                            ins = pe.transpose(pb[b // 4][:, 256 * (b % 4) + 128 * i:256 * (b % 4) + 128 * i + 128], prob[:, b, 128 * i:128 * i + 128], S.ident)
                        if b % 4 == 3:
                            ins.then_inc(turned, 1)
                    for e in range(2):
                        pe.wait_ge(kept[e], 1)
                    for b in range(NB):
                        for h in range(MEMH):
                            for i in range(2):
                                ins = pe.matmul(pa[0][32 * h:32 * h + 32, 128 * b:128 * b + 128], probT[:, b, i, 32 * h:32 * h + 32], v[:, b, i, 128 * h:128 * h + 128], start=(i == 0), stop=(i == 1))
                    ins.then_inc(made, 1)
                    pe.wait_ge(rows, 1)
                    for b in range(NB):
                        ins = pe.transpose(pa[1][:, 128 * b:128 * b + 128], o_rows[:, b, :], S.ident)
                    ins.then_inc(o_turned, 1)

                @block.vector
                def _(dve):
                    done = [0]

                    def step(ins):
                        done[0] += 1
                        ins.then_inc(chain, 1)
                        dve.wait_ge(chain, done[0])

                    dve.wait_ge(scored, 1)
                    sv = lambda x: pa[x][:, :].rearrange("p (b n) -> p b n", b=4)
                    for x in range(2):
                        ins = dve.tensor_reduce(stat[:, 0, 4 * x:4 * x + 4], sv(x), AX.X, ALU.max)
                    step(ins)
                    for x in range(2):
                        ins = dve.tensor_tensor(prob[:, 4 * x:4 * x + 4, :], sv(x), stat[:, 0, 4 * x:4 * x + 4].unsqueeze(2).to_broadcast([128, 4, MEM]), ALU.subtract)
                    ins.then_inc(ready, 1)
                    dve.wait_ge(exped, 1)
                    step(dve.tensor_reduce(stat[:, 1, :], prob[:, :, :], AX.X, ALU.add))
                    step(dve.reciprocal(stat[:, 2, :], stat[:, 1, :]))
                    dve.wait_ge(turned, 1)
                    dve.tensor_copy(probT[:, 0:4, :, :].rearrange("p b i n -> p (b i n)"), pb[0][:, :]).then_inc(kept[0], 1)
                    dve.wait_ge(made, 1)
                    dve.tensor_tensor(o_rows[:, :, :], pa[0][:, :].rearrange("p (b n) -> p b n", b=NB), stat[:, 2, :].unsqueeze(2).to_broadcast([128, NB, 128]), ALU.mult).then_inc(rows, 1)
                    dve.wait_ge(o_turned, 1)
                    step(dve.tensor_copy(S.mem_o[:, :, SEQ:T].rearrange("p h (b t) -> p b h t", b=NB), pa[1][:, :].rearrange("p (b h t) -> p b h t", b=NB, h=MEMH)[:, :, :, 0:ND]))

                @block.scalar
                def _(act):
                    act.wait_ge(ready, 1)
                    act.activation(prob[:, :, :], prob[:, :, :], ACT.Exp, scale=MEM_SCALE).then_inc(exped, 1)
                    act.wait_ge(turned, 2)
                    act.copy(probT[:, 4:8, :, :].rearrange("p b i n -> p (b i n)"), pb[1][:, :]).then_inc(kept[1], 1)


def memory_out(nc, d, S):
    with ExitStack() as ctx:
        w = ctx.enter_context(nc.sbuf_tensor("w_mo", [128, MEMH, D], F32))
        bank = [ctx.enter_context(nc.psum_tensor(f"p_mo{i}", [128, 512], F32)) for i in range(4)]
        w_in = [S.semaphore(nc, f"wmo_in{i}") for i in range(4)]; made = S.semaphore(nc, "mo_made"); added = S.semaphore(nc, "mo_added")
        with nc.Block() as block:
            @block.sync
            def _(sp):
                for q in range(4):
                    sp.dma_start(w[:, :, 512 * q:512 * q + 512], d['w_mo'][0, :, 512 * q:512 * q + 512].rearrange("(t p) n -> p t n", p=128)).then_inc(w_in[q], 16)

            @block.tensor
            def _(pe):
                for m in range(DT):
                    if m % 4 == 0:
                        pe.wait_ge(w_in[m // 4], 16)
                    if m >= 4:
                        pe.wait_ge(added, m - 3)
                    for t in range(MEMH):
                        ins = pe.matmul(bank[m % 4][:, 0:T], w[:, t, 128 * m:128 * m + 128], S.mem_o[:, t, :], start=(t == 0), stop=(t == MEMH - 1))
                    ins.then_inc(made, 1)

            @block.vector
            def _(dve):
                for m in range(DT):
                    dve.wait_ge(made, m + 1)
                    dve.tensor_tensor(S.xT[:, m, :], S.xT[:, m, :], bank[m % 4][:, 0:T], ALU.add).then_inc(added, 1)


def route_tokens(nc, d, S, h3T, x2T, ident):
    T = S.T
    with ExitStack() as ctx:
        sb = lambda n, s, t=F32: ctx.enter_context(nc.sbuf_tensor(n, s, t))
        ps = lambda n, s=(128, 512): ctx.enter_context(nc.psum_tensor(n, list(s), F32))
        sem = lambda n: S.semaphore(nc, n)
        w_router = sb("w_router", [128, DT, NG + NE])
        bias = sb("router_bias", [128, NG + NE])
        x2 = sb("x2_tokens", [128, 3, D])
        logits = sb("logits", [128, 3, NG + NE])
        lc = sb("lc", [128, 3, NG]); ec = sb("ec", [128, 3, NG])
        stat = sb("stat", [128, 12, 3])
        group_hot = sb("group_hot", [128, 3, NG])
        order = sb("order", [128, 8])
        prod = sb("prod", [128, 3, NG, EG])
        lf = sb("lf", [128, 3, EG]); pf = sb("pf", [128, 3, EG]); pf2 = sb("pf2", [128, 3, EG])
        score = sb("score", [128, 3, EG])
        hot1 = sb("hot1", [128, 3, EG]); hot2 = sb("hot2", [128, 3, EG])
        sel1 = sb("sel1", [128, 3, NG, EG]); sel2 = sb("sel2", [128, 3, NG, EG])
        sel = sb("sel", [128, 3, NE])
        valid = sb("valid", [128, 3])
        before = sb("before", [128, 128])
        ones = sb("ones_r", [128, 128])
        token = sb("token", [128, 3])
        count = sb("count", [128, 1])
        p_logit = ps("p_logit"); p_pos = ps("p_pos"); p_turn = [ps("p_turn0"), ps("p_turn1")]
        loaded = sem("router_loaded"); consts = sem("router_consts"); logit_ready = sem("logit_ready")
        turned = sem("turned"); turn_copied = sem("turn_copied"); exp_in = sem("exp_in"); exp_out = sem("exp_out")
        chain = sem("route_chain"); positions = sem("positions"); sel_ready = sem("sel_ready"); parked = sem("parked")
        with nc.Block() as block:
            @block.sync
            def _(sp):
                sp.dma_start(w_router[:, :, 0:NG], d['w_router_c'][0].rearrange("(t p) n -> p t n", p=128)).then_inc(loaded, 16)
                sp.dma_start(w_router[:, :, NG:], d['w_router_f'][0].rearrange("(t p) n -> p t n", p=128)).then_inc(loaded, 16)
                sp.dma_start(bias[:, 0:NG], d['b_router_c'].to_broadcast([128, NG])).then_inc(loaded, 16)
                sp.dma_start(bias[:, NG:], d['b_router_f'].to_broadcast([128, NE])).then_inc(loaded, 16)
                for i, n in enumerate(TILE):
                    sp.wait_ge(turn_copied, 16 // 4 * 2 * (i + 1))
                    sp.dma_start(S.x2_dram[128 * i:128 * i + n, :], x2[0:n, i, :]).then_inc(parked, 16)
                sp.wait_ge(parked, 48)

            @block.gpsimd
            def _(pool):
                done = [0]

                def step(ins):
                    done[0] += 1
                    ins.then_inc(consts, 1)
                    pool.wait_ge(consts, done[0])

                step(pool.memset(ones[:, :], 1.0))
                step(pool.affine_select(out=before[:, :], in_=ones[:, :], compare_op=ALU.is_gt, fill=0.0, base=0,
                                        pattern=[[1, 128]], channel_multiplier=-1))
                step(pool.iota(token[:, :], pattern=[[2 * 128, 3]], base=0, channel_multiplier=2,
                               allow_small_or_imprecise_dtypes=True))
                step(pool.iota(S.no_row[:, :], pattern=[[0, 1]], base=2 * ROWS, channel_multiplier=1,
                               allow_small_or_imprecise_dtypes=True))
                step(pool.memset(S.row_of[:, :, :, 1:2], 1.0))
                step(pool.iota(order[:, :], pattern=[[-1, 8]], base=8, channel_multiplier=0,
                               allow_small_or_imprecise_dtypes=True))
                step(pool.iota(S.slot_of[:, :], pattern=[[0, 2], [1, SL]], base=0, channel_multiplier=0,
                               allow_small_or_imprecise_dtypes=True))
                step(pool.memset(valid[:, :], 1.0))
                step(pool.memset(valid[64:128, 2:3], 0.0))
                step(pool.memset(logits[64:128, 2, :], 0.0))
                step(pool.memset(S.pos_of[:, :, NE:NE + 1], -1.0))
                step(pool.memset(S.h3[64:128, 2, :, :], 0.0))

            @block.tensor
            def _(pe):
                pe.wait_ge(loaded, 64)
                for i, n in enumerate(TILE):
                    for t in range(DT):
                        mm = pe.matmul(p_logit[0:n, 64 * i:64 * i + NG + NE], h3T[:, t, 128 * i:128 * i + n],
                                       w_router[:, t, :], start=(t == 0), stop=(t == DT - 1))
                    mm.then_inc(logit_ready, 1)
                k = 0
                for i, n in enumerate(TILE):
                    for src in (h3T, x2T):
                        for q in range(4):
                            if k >= 2:
                                pe.wait_ge(turn_copied, k - 1)
                            for j in range(4):
                                mm = pe.transpose(p_turn[k % 2][0:n, 128 * j:128 * j + 128],
                                                  src[:, 4 * q + j, 128 * i:128 * i + n], ident[:, :])
                            mm.then_inc(turned, 1)
                            k += 1
                pe.wait_ge(sel_ready, 1)
                for i, n in enumerate(TILE):
                    for ii in range(i):
                        pe.matmul(p_pos[:, 32 * i:32 * i + 32], ones[:, :], sel[:, ii, :], start=(ii == 0), stop=False)
                    pe.matmul(p_pos[:, 32 * i:32 * i + 32], before[:, :], sel[:, i, :], start=(i == 0), stop=True)
                for i in range(3):
                    mm = pe.matmul(p_pos[:, 96:128], ones[:, :], sel[:, i, :], start=(i == 0), stop=(i == 2))
                mm.then_inc(positions, 1)

            @block.scalar
            def _(act):
                k = 0
                for i, n in enumerate(TILE):
                    for src in (h3T, x2T):
                        for q in range(4):
                            act.wait_ge(turned, k + 1)
                            if src is h3T:
                                o = S.h3[0:n, i, :, 32 * q:32 * q + 32].rearrange("k t p -> k p t")
                                src_ps = p_turn[k % 2][0:n, :].rearrange("k (p t) -> k p t", t=DT)
                            else:
                                o = x2[0:n, i, 512 * q:512 * q + 512]
                                src_ps = p_turn[k % 2][0:n, :]
                            act.copy(o, src_ps).then_inc(turn_copied, 1)
                            k += 1
                for n in range(2):
                    act.wait_ge(exp_in, n + 1)
                    if n == 0:
                        act.activation(ec[:, :, :], lc[:, :, :], ACT.Exp).then_inc(exp_out, 1)
                    else:
                        act.activation(pf[:, :, :], lf[:, :, :], ACT.Exp).then_inc(exp_out, 1)

            @block.vector
            def _(dve):
                done = [0]

                def step(ins):
                    done[0] += 1
                    ins.then_inc(chain, 1)
                    dve.wait_ge(chain, done[0])

                def bc(a, n):
                    return a.unsqueeze(2).to_broadcast([128, 3, n])

                dve.wait_ge(consts, 12)
                dve.wait_ge(loaded, 64)
                dve.wait_ge(logit_ready, 3)
                for i, n in enumerate(TILE):
                    step(dve.tensor_tensor(logits[0:n, i, :], p_logit[0:n, 64 * i:64 * i + NG + NE], bias[0:n, :], ALU.add))
                step(dve.tensor_reduce(stat[:, 0, :], logits[:, :, 0:NG], AX.X, ALU.max))
                dve.tensor_tensor(lc[:, :, :], logits[:, :, 0:NG], bc(stat[:, 0, :], NG), ALU.subtract).then_inc(exp_in, 1)
                dve.wait_ge(exp_in, 1)
                step(dve.scalar_tensor_tensor(score[:, :, 0:NG], lc[:, :, :], 0.0, order[:, 0:NG].unsqueeze(1).to_broadcast([128, 3, NG]), ALU.is_ge, ALU.mult))
                step(dve.tensor_reduce(stat[:, 1, :], score[:, :, 0:NG], AX.X, ALU.max))
                step(dve.tensor_tensor(group_hot[:, :, :], score[:, :, 0:NG], bc(stat[:, 1, :], NG), ALU.is_equal))
                for i in range(3):
                    fine = logits[:, i, NG:].rearrange("p (g e) -> p g e", g=NG)
                    step(dve.tensor_tensor(prod[:, i, :, :], fine, group_hot[:, i, :].unsqueeze(2).to_broadcast([128, NG, EG]), ALU.mult))
                    step(dve.tensor_reduce(lf[:, i, :], prod[:, i, :, :].rearrange("p g e -> p e g"), AX.X, ALU.add))
                step(dve.tensor_reduce(stat[:, 2, :], lf[:, :, :], AX.X, ALU.max))
                dve.tensor_tensor(lf[:, :, :], lf[:, :, :], bc(stat[:, 2, :], EG), ALU.subtract).then_inc(exp_in, 1)
                dve.wait_ge(exp_out, 1)
                step(dve.tensor_reduce(stat[:, 3, :], ec[:, :, :], AX.X, ALU.add))
                step(dve.reciprocal(stat[:, 4, :], stat[:, 3, :]))
                dve.wait_ge(exp_out, 2)
                order3 = order[:, :].unsqueeze(1).to_broadcast([128, 3, EG])
                for src, hot, m in ((pf, hot1, 5), (pf2, hot2, 6)):
                    step(dve.tensor_reduce(stat[:, m, :], src[:, :, :], AX.X, ALU.max))
                    step(dve.tensor_tensor(score[:, :, :], src[:, :, :], bc(stat[:, m, :], EG), ALU.is_equal))
                    step(dve.tensor_tensor(score[:, :, :], score[:, :, :], order3, ALU.mult))
                    step(dve.tensor_reduce(stat[:, 7, :], score[:, :, :], AX.X, ALU.max))
                    step(dve.tensor_tensor(hot[:, :, :], score[:, :, :], bc(stat[:, 7, :], EG), ALU.is_equal))
                    if src is pf:
                        step(dve.scalar_tensor_tensor(pf2[:, :, :], hot1[:, :, :], -2.0, pf[:, :, :], ALU.mult, ALU.add))
                step(dve.tensor_tensor(stat[:, 8, :], stat[:, 5, :], stat[:, 6, :], ALU.add))
                step(dve.reciprocal(stat[:, 9, :], stat[:, 8, :]))
                step(dve.tensor_tensor(stat[:, 10, :], stat[:, 9, :], stat[:, 4, :], ALU.mult))
                step(dve.tensor_tensor(S.weight[:, 0, :], stat[:, 5, :], stat[:, 10, :], ALU.mult))
                step(dve.tensor_tensor(S.weight[:, 1, :], stat[:, 6, :], stat[:, 10, :], ALU.mult))
                step(dve.tensor_tensor(group_hot[:, :, :], group_hot[:, :, :], bc(valid[:, :], NG), ALU.mult))
                for hot, s in ((hot1, sel1), (hot2, sel2)):
                    for i in range(3):
                        step(dve.tensor_tensor(s[:, i, :, :], group_hot[:, i, :].unsqueeze(2).to_broadcast([128, NG, EG]),
                                               hot[:, i, :].unsqueeze(1).to_broadcast([128, NG, EG]), ALU.mult))
                s1 = sel1[:, :, :, :].rearrange("p a g e -> p a (g e)")
                s2 = sel2[:, :, :, :].rearrange("p a g e -> p a (g e)")
                dve.tensor_tensor(sel[:, :, :], s1, s2, ALU.add).then_inc(sel_ready, 1)
                dve.wait_ge(sel_ready, 1)
                dve.wait_ge(positions, 1)
                pos = p_pos[:, 0:96].rearrange("p (a e) -> p a e", a=3)
                step(dve.tensor_tensor(S.pos_of[:, :, 0:NE], pos, sel[:, :, :], ALU.mult))
                step(dve.tensor_tensor(S.pos_of[:, :, 0:NE], S.pos_of[:, :, 0:NE], sel[:, :, :], ALU.add))
                step(dve.tensor_scalar(S.pos_of[:, :, 0:NE], S.pos_of[:, :, 0:NE], -1.0, None, ALU.add))
                for i in range(3):
                    step(dve.tensor_scalar(S.row_of[:, i, :, 0], s2[:, i, :], float(2 * T), token[:, i:i + 1], ALU.mult, ALU.add))
                step(dve.tensor_scalar(S.row_base[:, :], S.no_row[:, :], 0.0, None, ALU.add))
                step(dve.tensor_scalar(S.row_base[64:128, :], S.no_row[64:128, :], 1.0, None, ALU.add))
                step(dve.tensor_reduce(count[:, :], p_pos[:, 96:128], AX.X, ALU.max))
                step(dve.tensor_copy(S.most[:, :], count[:, :]))


def experts(nc, d, S, ident):
    with ExitStack() as ctx:
        sb = lambda n, s, t=F32: ctx.enter_context(nc.sbuf_tensor(n, s, t))
        ps = lambda n, s=(128, 512): ctx.enter_context(nc.psum_tensor(n, list(s), F32))
        sem = lambda n: S.semaphore(nc, n)
        sel = sb("slot_sel", [128, 3, 2 * SL]); rowf = sb("rowf", [128, 1]); row = sb("row", [128, 1], I32)
        xg = sb("xg", [128, 8, 128])
        xgT = sb("xgT", [128, 8, 2, SL])
        act_g = sb("act_g", [128, FF // 2]); hid = sb("hid", [128, FF // 2])
        hidT = sb("hidT", [128, 2, 2, SL])
        y = sb("y_slots", [128, D // 2])
        p_xg = ps("p_xg", (128, 1024)); p_xgT = ps("p_xgT", (128, 1024)); p_g = ps("p_g"); p_u = ps("p_u"); p_y = ps("p_y", (128, 1024))
        w = S.w
        w_free = [sem(f"w_free{g}") for g in range(6)]
        w_in = S.w_in
        sel_made = sem("sel_made"); gathered = sem("gathered")
        xg_v = sem("xg_v"); xg_a = sem("xg_a"); xgT_done = sem("xgT_done"); xgT_v = sem("xgT_v"); xgT_a = sem("xgT_a")
        gate_up = sem("gate_up"); silu_done = sem("silu_done"); hid_done = sem("hid_done"); hid_turned = sem("hid_turned")
        hidT_done = sem("hidT_done"); y_done = sem("y_done"); y_v = sem("y_v"); y_a = sem("y_a"); y_out = sem("y_out"); y_free = sem("y_free")
        ybuf = S.ybuf
        row_sum = sem("row_sum"); row_made = sem("row_made")

        def rounds(eng, body):
            body(0)
            most = eng.value_load(S.most[0:1, 0:1], min_val=0, max_val=SLOTS_MAX)
            with eng.Fori(1, SLOTS_MAX // SL) as r:
                with eng.If(most > r * SL):
                    body(r)
                eng.nop()

        with nc.Block() as block:
            @block.sync
            def _(sp):
                def load(e, r_e, first):
                    for g in range(6):
                        if not first:
                            sp.wait_ge(w_free[g], r_e)
                        sp.dma_start(w[g][:, :], S.w_src(d, g, e)).then_inc(w_in[g], 16)

                def body(r):
                    if not isinstance(r, int):
                        load(0, NE * r, False)
                    with sp.Fori(1, NE) as e:
                        load(e, NE * r + e, False)
                rounds(sp, body)

            @block.tensor
            def _(pe):
                def gather(k, r):
                    pe.wait_ge(sel_made, (NE + 1) * r + k + 1)
                    for b in range(2):
                        for i in range(3):
                            for h in range(2):
                                mm = pe.matmul(p_xg[SL * h:SL * h + SL, 512 * b:512 * b + 512], sel[:, i, SL * h:SL * h + SL],
                                               S.h3[:, i, 8 * h + 4 * b:8 * h + 4 * b + 4, :].rearrange("k t p -> k (t p)"),
                                               start=(i == 0), stop=(i == 2))
                    mm.then_inc(gathered, 1)

                def body(r):
                    if not isinstance(r, int):
                        pe.wait_ge(xg_v, (NE + 1) * r)
                        pe.wait_ge(xg_a, (NE + 1) * r)
                    gather(0, r)
                    with pe.Fori(0, NE) as e:
                        n = NE * r + e + 1
                        pe.wait_ge(xg_v, (NE + 1) * r + e + 1)
                        pe.wait_ge(xg_a, (NE + 1) * r + e + 1)
                        for t in range(8):
                            mm = pe.transpose(p_xgT[:, 128 * t:128 * t + 128], xg[:, t, :], ident[:, :])
                        for i in range(3):
                            mm = pe.matmul(p_g[:, 256:258], sel[:, i, :], S.row_of[:, i, bass.ds(e, 1), :].rearrange("k e c -> k (e c)"),
                                           start=(i == 0), stop=(i == 2))
                        mm.then_inc(xgT_done, 1)
                        pe.wait_ge(xgT_v, n)
                        pe.wait_ge(xgT_a, n)
                        for g in range(4):
                            pe.wait_ge(w_in[g], 16 * n)
                            acc = (p_g, p_u)[g % 2]
                            for t in range(8):
                                for h in range(2):
                                    mm = pe.matmul(acc[SL * h:SL * h + SL, 0:FF // 2], xgT[:, t, g // 2, :],
                                                   w[g][:, FF * t + FF // 2 * h:FF * t + FF // 2 * h + FF // 2],
                                                   start=(g < 2 and t == 0), stop=(g >= 2 and t == 7))
                            mm.then_inc(w_free[g], 1)
                        gather(e + 1, r)
                        pe.wait_ge(hid_done, n)
                        for j in range(2):
                            mm = pe.transpose(p_xgT[:, 128 * j:128 * j + 128], hid[:, 128 * j:128 * j + 128], ident[:, :])
                        mm.then_inc(hid_turned, 1)
                        pe.wait_ge(hidT_done, n)
                        pe.wait_ge(y_free, n)
                        for k in range(4):
                            if k % 2 == 0:
                                pe.wait_ge(w_in[4 + k // 2], 16 * n)
                            for b in range(2):
                                for h in range(2):
                                    mm = pe.matmul(p_y[SL * h:SL * h + SL, 512 * b:512 * b + 512],
                                                   hidT[:, k % 2, k // 2, :],
                                                   w[4 + k // 2][:, D * (k % 2) + 1024 * h + 512 * b:D * (k % 2) + 1024 * h + 512 * b + 512],
                                                   start=(k == 0), stop=(k == 3))
                            if k % 2 == 1:
                                mm.then_inc(w_free[4 + k // 2], 1)
                rounds(pe, body)

            @block.vector
            def _(dve):
                def select(k, r):
                    for i in range(3):
                        ins = dve.tensor_scalar(sel[:, i, :], S.slot_of[:, :], slot_shift, S.pos_of[:, i, bass.ds(k, 1)], ALU.add, ALU.is_equal)
                    ins.then_inc(sel_made, 1)

                def copy_xg(k, r):
                    dve.wait_ge(gathered, (NE + 1) * r + k + 1)
                    dve.tensor_copy(xg[:, 0:4, :].rearrange("p t q -> p (t q)"), p_xg[:, 0:512]).then_inc(xg_v, 1)

                slot_shift = S.shift[:, 0:1]

                def body(r):
                    if isinstance(r, int):
                        dve.memset(S.shift[:, :], 0.0).then_inc(S.shifted, 1)
                        dve.wait_ge(S.shifted, 1)
                    else:
                        dve.tensor_scalar(S.shift[:, :], S.shift[:, :], float(SL), None, ALU.add).then_inc(S.shifted, 1)
                        dve.wait_ge(S.shifted, r + 1)
                    select(0, r)
                    copy_xg(0, r)
                    with dve.Fori(0, NE) as e:
                        n = NE * r + e + 1
                        dve.wait_ge(xgT_done, n)
                        dve.tensor_scalar(rowf[:, :], p_g[:, 257:258], S.no_row[:, :], None, ALU.mult).then_inc(row_sum, 1)
                        dve.wait_ge(row_sum, 2 * n - 1)
                        dve.scalar_tensor_tensor(rowf[:, :], p_g[:, 256:257], S.row_base[:, :], rowf[:, :], ALU.add, ALU.subtract).then_inc(row_sum, 1)
                        dve.tensor_copy(xgT[:, 0:4, :, :].rearrange("p t h s -> p (t h s)"), p_xgT[:, 0:512]).then_inc(xgT_v, 1)
                        select(e + 1, r)
                        dve.wait_ge(y_free, n)
                        dve.wait_ge(row_sum, 2 * n)
                        dve.tensor_copy(row[:, :], rowf[:, :]).then_inc(row_made, 1)
                        dve.wait_ge(silu_done, n)
                        dve.tensor_tensor(hid[:, :], act_g[:, :], p_u[:, 0:FF // 2], ALU.mult).then_inc(hid_done, 1)
                        copy_xg(e + 1, r)
                        dve.wait_ge(hid_turned, n)
                        dve.tensor_copy(hidT[:, :, :, :].rearrange("p j h s -> p (j h s)"), p_xgT[:, 0:256]).then_inc(hidT_done, 1)
                        dve.wait_ge(w_free[5], n)
                        dve.tensor_copy(y[:, 0:512], p_y[:, 0:512]).then_inc(y_v, 1)
                rounds(dve, body)

            @block.scalar
            def _(act):
                def copy_xg(k, r):
                    act.wait_ge(gathered, (NE + 1) * r + k + 1)
                    act.copy(xg[:, 4:8, :].rearrange("p t q -> p (t q)"), p_xg[:, 512:1024]).then_inc(xg_a, 1)

                def body(r):
                    copy_xg(0, r)
                    with act.Fori(0, NE) as e:
                        n = NE * r + e + 1
                        act.wait_ge(xgT_done, n)
                        act.copy(xgT[:, 4:8, :, :].rearrange("p t h s -> p (t h s)"), p_xgT[:, 512:1024]).then_inc(xgT_a, 1)
                        act.wait_ge(w_free[3], n)
                        act.activation(act_g[:, :], p_g[:, 0:FF // 2], ACT.Silu).then_inc(silu_done, 1)
                        copy_xg(e + 1, r)
                        act.wait_ge(w_free[5], n)
                        act.copy(y[:, 512:1024], p_y[:, 512:1024]).then_inc(y_a, 1)
                rounds(act, body)

            @block.gpsimd
            def _(pool):
                last_row = pool.to_reg(2 * ROWS - 1)
                pool.nop().then_inc(y_free, 1)

                def body(r):
                    with pool.Fori(0, NE) as e:
                        n = NE * r + e + 1
                        pool.wait_ge(row_made, n)
                        pool.wait_ge(y_v, n)
                        pool.wait_ge(y_a, n)
                        pool.nop(nofuse=True)
                        pool.indirect_dma_start(out=ybuf[:, :], out_offset=bass.IndirectOffsetOnAxis(ap=row[:, 0:1], axis=0),
                                                in_=y[:, :], in_offset=None, bounds_check=last_row, oob_is_err=False).then_inc(y_out, 16)
                        pool.wait_ge(y_out, 16 * n)
                        pool.nop().then_inc(y_free, 1)
                rounds(pool, body)


def combine(nc, d, S, outs):
    with ExitStack() as ctx:
        sb = lambda n, s, t=F32: ctx.enter_context(nc.sbuf_tensor(n, s, t))
        sem = lambda n: S.semaphore(nc, n)
        xo = sb("xo", [128, 3, D]); r1 = sb("r1", [128, 3, D]); r2 = sb("r2", [128, 3, D]); g = sb("final_g", [128, D])
        ss = sb("final_ss", [128, 3, 4]); sq = sb("final_sq", [128, D])
        x_in = sem("xo_in"); rows_in = [sem(f"rows_in{i}") for i in range(3)]; results = S.ybuf.rearrange("(r h) n -> r (h n)", h=2); chain = sem("combine_chain"); squared = sem("final_squared"); root = sem("final_root"); stored = sem("stored")
        ready = sem("out_ready")
        eps = sb("eps_f", [128, 1]); eps_set = sem("eps_set")
        with nc.Block() as block:
            @block.sync
            def _(sp):
                sp.dma_start(g[:, :], d['final_norm_g'].unsqueeze(0).to_broadcast([128, D])).then_inc(x_in, 16)
                for i, n in enumerate(TILE):
                    sp.dma_start(xo[0:n, i, :], S.x2_dram[128 * i:128 * i + n, :]).then_inc(x_in, 16)
                    for c, r in ((0, r1), (1, r2)):
                        sp.dma_start(r[0:n, i, :], results[T * c + 128 * i:T * c + 128 * i + n, :]).then_inc(rows_in[i], 16)
                for i, n in enumerate(TILE):
                    sp.wait_ge(ready, i + 1)
                    dst = outs[0][0, 128 * i:128 * i + 128, :] if i < 2 else outs[1].rearrange("b t n -> (b t) n")
                    sp.dma_start(dst, xo[0:n, i, :]).then_inc(stored, 16)
                sp.wait_ge(stored, 48)

            @block.scalar
            def _(act):
                act.wait_ge(eps_set, 1)
                for i, n in enumerate(TILE):
                    act.wait_ge(chain, 4 * i + 2)
                    act.activation(sq[0:n, :], xo[0:n, i, :], ACT.Square, accum_out=ss[0:n, i, 0:1]).then_inc(squared, 1)
                    act.wait_ge(squared, i + 1)
                    act.activation(ss[0:n, i, 1:2], ss[0:n, i, 0:1], ACT.Sqrt, bias=eps[0:n, :], scale=1.0 / D).then_inc(root, 1)

            @block.vector
            def _(dve):
                dve.memset(eps[:, :], EPS).then_inc(eps_set, 1)
                dve.wait_ge(x_in, 64)
                for i, n in enumerate(TILE):
                    dve.wait_ge(rows_in[i], 32)
                    dve.scalar_tensor_tensor(xo[0:n, i, :], r1[0:n, i, :], S.weight[0:n, 0, i:i + 1], xo[0:n, i, :], ALU.mult, ALU.add).then_inc(chain, 1)
                    dve.wait_ge(chain, 4 * i + 1)
                    dve.scalar_tensor_tensor(xo[0:n, i, :], r2[0:n, i, :], S.weight[0:n, 1, i:i + 1], xo[0:n, i, :], ALU.mult, ALU.add).then_inc(chain, 1)
                    dve.wait_ge(root, i + 1)
                    dve.reciprocal(ss[0:n, i, 2:3], ss[0:n, i, 1:2]).then_inc(chain, 1)
                    dve.wait_ge(chain, 4 * i + 3)
                    dve.scalar_tensor_tensor(xo[0:n, i, :], xo[0:n, i, :], ss[0:n, i, 2:3], g[0:n, :], ALU.mult, ALU.mult).then_inc(ready, 1)
                    dve.nop().then_inc(chain, 1)


def build(nc, d, outs):
    with ExitStack() as ctx:
        sb = lambda n, s, t=F32: ctx.enter_context(nc.sbuf_tensor(n, s, t))
        sem = lambda n: ctx.enter_context(nc.semaphore(n))
        S = Shared()
        S.T = T
        S.x2_dram = nc.dram_tensor("x2_dram", [T, D], F32).ap()
        S.xT_dram = nc.dram_tensor("xT_dram", [128, DT * T], F32).ap()
        S.ybuf = nc.dram_tensor("ybuf", [2 * ROWS, D // 2], F32).ap()
        S.tables_sb = sb("tables_sb", [128, TABLE_W]); S.vectors = sb("vectors", [128, 256]); S.eps = sb("eps", [128, 1])
        S.ident = S.table("ident")
        S.slot_of = sb("slot_of", [128, 2 * SL]); S.no_row = sb("no_row", [128, 1]); S.row_base = sb("row_base", [128, 1]); S.row_of = sb("row_of", [128, 3, NE, 2])
        S.pos_of = sb("pos_of", [128, 3, NE + 1]); S.weight = sb("weight", [128, 2, 3]); S.most = sb("most", [128, 1], I32); S.shift = sb("shift", [128, 1])
        S.shifted = sem("shifted"); S.w_in = [sem(f"w_in_e{g}") for g in range(6)]
        low = sb("low", [128, 3 * D])
        at = [0]

        def part(n, *shape):
            size = math.prod(shape)
            out = low[0:n, at[0]:at[0] + size]
            at[0] += size
            assert at[0] <= 3 * D
            return out.rearrange("p (a b) -> p a b", a=shape[0]) if len(shape) == 2 else out

        S.qa, S.kv, S.kr, S.k, S.sg, S.ys = part(128, 4, T), part(128, 2, T), part(64, T), part(128, 8, T), part(128, 2, T), part(128, HP, 64)
        at[0] = 0
        S.mem_kT, S.mem_v, S.mem_q, S.mem_o = part(128, MEMH, MEM), part(128, 2, 512), part(128, MEMH, T), part(128, MEMH, T)
        S.o_lat = low[:, 0:2 * MH * T].rearrange("p (c h n) -> p c h n", c=2, h=MH)
        S.h3 = low[:, :].rearrange("p (i t q) -> p i t q", i=3, t=DT)
        with ExitStack() as c1:
            sb1 = lambda n, s, t=F32: c1.enter_context(nc.sbuf_tensor(n, s, t))
            mix = sb1("mix", [128, DT, T])
            S.mix, S.r, S.lw = mix, mix[:, 0:8, :], mix[:, 8:16, :]
            with ExitStack() as c2:
                sb2 = lambda n, s, t=F32: c2.enter_context(nc.sbuf_tensor(n, s, t))
                S.v = sb2("rw_v", [128, 8, T]); S.a = sb2("rw_a", [128, 8, T]); S.xa = sb2("rw_xa", [128, T])
                with ExitStack() as c3:
                    S.P = c3.enter_context(nc.sbuf_tensor("P", [128, 28, SEQ + 1 + 9 * NB], F32))
                    with ExitStack() as c4:
                        S.hT = c4.enter_context(nc.sbuf_tensor("hT", [128, DT, T], F32))
                        with ExitStack() as c5:
                            S.xT = c5.enter_context(nc.sbuf_tensor("xT", [128, DT, T], F32))
                            load_front(nc, d, S)
                            feature_norm(nc, S, "norm_mix", S.xT[:, :, :], S.hT[:, :, :], S.vec("ln_mix"), DT, D)
                        project_in(nc, d, S)
                    rwkv_mix(nc, d, S, outs)
                with ExitStack() as c3:
                    sb3 = lambda n, s, t=F32: c3.enter_context(nc.sbuf_tensor(n, s, t))
                    S.mt = sb3("maps_m", [128, HP, NCH, 64]); S.nn = sb3("maps_n", [128, NCH, HP, 64])
                    rwkv_pairs(nc, d, S, outs)
                    rwkv_chain(nc, d, S, outs)
            S.recycle(nc)
            with ExitStack() as c2:
                sb2 = lambda n, s, t=F32: c2.enter_context(nc.sbuf_tensor(n, s, t))
                S.c = sb2("latent", [128, 2, T]); S.kp = sb2("rot_key", [64, T]); S.c_tok = sb2("c_tok", [128, 3, KVL]); S.kp_tok = sb2("kp_tok", [128, 3, ROPE])
                S.w_kvb = sb2("w_kvb", [128, 2, MH * (NOPE + VD)]); S.q_lat = sb2("q_lat", [128, 2, MH, T]); S.q_pe = sb2("q_pe", [64, MH, T])
                with ExitStack() as c3:
                    S.qn = c3.enter_context(nc.sbuf_tensor("qn", [128, 4, T], F32))
                    feature_norm(nc, S, "norm_q", S.qa, S.qn[:, :, :], S.vec("q_norm"), 4, QL)
                    feature_norm(nc, S, "norm_kv", S.kv, S.c[:, :, :], S.vec("kv_norm"), 2, KVL)
                    mla_project(nc, d, S, outs)
                mla_prompt(nc, d, S)
                mla_sample(nc, d, S)
                mla_out(nc, S)
            S.xT = sb1("xT_again", [128, DT, T])
            project_out(nc, d, S)
            S.recycle(nc)
            memory_keys(nc, d, S, outs)
            feature_norm(nc, S, "norm_mem", S.xT[:, :, :], mix[:, :, :], S.vec("ln_mem"), DT, D)
            memory_queries(nc, d, S)
            memory_prompt(nc, S)
            memory_sample(nc, d, S)
            memory_out(nc, d, S)
            S.recycle(nc)
            feature_norm(nc, S, "norm_moe", S.xT[:, :, :], mix[:, :, :], S.vec("ln_moe"), DT, D)
            route_tokens(nc, d, S, mix, S.xT, S.ident)
        with ExitStack() as c1:
            S.w = [c1.enter_context(nc.sbuf_tensor(f"w_expert{g}", [128, 4096], F32)) for g in range(6)]

            def w_src(d, g, e):
                if g < 4:
                    return d[('w_gate', 'w_up')[g % 2]][0][bass.ds(e, 1)].rearrange("e (p t) n -> p (e t n)", t=DT)[:, 8 * FF * (g // 2):8 * FF * (g // 2) + 8 * FF]
                return d['w_down'][0][bass.ds(e, 1), 256 * (g - 4):256 * (g - 4) + 256, :].rearrange("e (k p) n -> p (e k) n", p=128)

            S.w_src = w_src
            with nc.Block() as block:
                @block.sync
                def _(sp):
                    for g in range(6):
                        sp.dma_start(S.w[g][:, :] if g < 4 else S.w[g][:, :].rearrange("p (k n) -> p k n", k=2), w_src(d, g, 0)).then_inc(S.w_in[g], 16)
            experts(nc, d, S, S.ident)
        combine(nc, d, S, outs)


OUTPUTS = [(1, SEQ, D), (NB, ND, D), (1, 1, SEQ, KVL), (1, 1, SEQ, ROPE), (1, 1, MEM, MEMH, 128), (1, 1, MEM, MEMH, 128), (1, 1, 2 * HP, HD, HD),
           (1, 1, RPROJ), (1, NB, ND, KVL), (1, NB, ND, ROPE), (1, NB, 2 * HP, HD, HD), (1, NB, RPROJ)]


def kernel(**inputs):
    import concourse.bacc as _bacc
    from concourse.bass_utils import run_bass_kernel_spmd as _run

    nc = _bacc.Bacc("TRN2", target_bir_lowering=False, num_devices=1)
    arrays, d = {}, {}
    for name, value in list(inputs.items()) + [("tables", tables())]:
        a = np.ascontiguousarray(value)
        arrays[f"in_{name}_dram"] = a
        d[name] = nc.dram_tensor(f"in_{name}_dram", a.shape, mybir.dt.from_np(a.dtype), kind="ExternalInput").ap()
    outs = [nc.dram_tensor(f"out_{i}_dram", shape, F32, kind="ExternalOutput").ap() for i, shape in enumerate(OUTPUTS)]
    build(nc, d, outs)
    results = _run(nc, [arrays], core_ids=[0]).results[0]
    return tuple(results[f"out_{i}_dram"] for i in range(len(OUTPUTS)))
```

```python
import math
from contextlib import ExitStack

import concourse.bass as bass
import numpy as np
from concourse import mybir

F32 = mybir.dt.float32
I32 = mybir.dt.int32
ALU = mybir.AluOpType
ACT = mybir.ActivationFunctionType
AX = mybir.AxisListType

D = 2048
DT = D // 128
SEQ, NB, ND = 256, 8, 8
TILE = (128, 128, NB * ND)
T = sum(TILE)
EPS = 1e-6
RW = 1024
RPROJ = 3 * RW + 96 + 96 + 256
QL, KVL, ROPE = 512, 256, 64
IN_PROJ = RPROJ + QL + KVL + ROPE
MH, NOPE, VD = 8, 128, 128
PAGE, NPG, NPHYS = 128, 16, 160
MLA_SCALE = (NOPE + ROPE) ** -0.5
MEM, MEMH = 256, 4
MEM_SCALE = 128 ** -0.5
NEG = -1e30
NG, EG = 4, 8
NE = NG * EG
FF = 512
SL = 64
SLOTS_MAX = T
ROWS = 2 * T
CH = 32
SUB = 16
NCH = SEQ // CH
HP = 8
HD = 64
DECAY = math.exp(-0.5)
GN_EPS = 64e-5
SEC = ((0, 128), (128, 128), (256, 64))

VECTORS = [("mu", 28), ("w0", 8), ("a0", 8), ("k_k", 8), ("k_a", 8), ("r_k", 8), ("gn_g", 8), ("gn_b", 8), ("ln_mix", 16),
           ("q_norm", 4), ("kv_norm", 2), ("ln_mem", 16), ("ln_moe", 16), ("mem_norm", 16)]
VECTOR_AT = {}
for _name, _n in VECTORS:
    _at = sum(n for _, n in VECTORS[:len(VECTOR_AT)])
    VECTOR_AT[_name] = (_at if _at < 106 else _at - 106 + 128, _n)

TABLES = [("ident", 128), ("headsum", 128), ("ones", 128), ("rot", 128), ("before16", T), ("after16", T), ("cross", T), ("before", T), ("upto", T),
          ("one", T), ("eye2", 64), ("own", 8), ("causal", 128), ("cos", T), ("sin", T), ("own_causal", NB * 64)]
TABLE_AT = {}
for _name, _n in TABLES:
    TABLE_AT[_name] = (sum(n for _, n in TABLES[:len(TABLE_AT)]), _n)
TABLE_W = sum(n for _, n in TABLES)


def tables():
    out = np.zeros((128, TABLE_W), np.float32)
    p = np.arange(128)[:, None]
    q = np.arange(128)[None, :]

    def put(name, value):
        at, n = TABLE_AT[name]
        out[:value.shape[0], at:at + value.shape[1]] = value

    def sections(same, order):
        a = (p // same == q // same) & order(p, q)
        b = ((p // ND == q // ND) & order(p, q))[:, :64] & (p < 64)
        return np.concatenate([a, a, b], 1)

    put("ident", p == q)
    put("headsum", p // 64 == q // 64)
    put("ones", np.ones((128, 128)))
    rot = np.zeros((128, 128))
    for b in (0, 64):
        for i in range(32):
            rot[b + 32 + i, b + i] = -1
            rot[b + i, b + 32 + i] = 1
    put("rot", rot)
    lt = lambda a, b: a < b
    put("before16", sections(SUB, lt))
    put("after16", sections(SUB, lambda a, b: a > b))
    cross = (p // CH == q // CH) & (p // SUB < q // SUB)
    put("cross", np.concatenate([cross, cross], 1))
    put("before", sections(CH, lt))
    put("upto", sections(CH, lambda a, b: a <= b))
    put("one", np.concatenate([p == q, p == q, (p == q)[:, :64]], 1))
    put("eye2", (p % 64 == q)[:, :64])
    put("own", (p // ND == q)[:64, :8])
    put("causal", np.where(q <= p, 0.0, NEG))
    inv = np.float32(10000.0) ** (-np.arange(32, dtype=np.float32) / np.float32(32))
    pos = np.concatenate([np.arange(SEQ), np.tile(NPG * PAGE + np.arange(ND), NB)]).astype(np.float32)
    ang = inv[:, None] * pos[None, :]
    put("cos", np.tile(np.cos(ang), (4, 1)))
    put("sin", np.tile(np.sin(ang), (4, 1)))
    own = np.full((64, NB, 64), NEG, np.float32)
    for b in range(NB):
        for h in range(MH):
            for t in range(ND):
                own[ND * h + t, b, ND * b:ND * b + t + 1] = 0
    put("own_causal", own.reshape(64, NB * 64))
    return out


class Shared:

    def __init__(self):
        self.finished = []

    def semaphore(self, nc, name):
        self.finished.append(nc.alloc_semaphore(name))
        return self.finished[-1]

    def recycle(self, nc):
        nc.clear_and_free_semaphores(self.finished)
        self.finished = []
        with nc.Block() as block:
            @block.gpsimd
            def _(pool):
                pool.nop()

    def vec(self, name):
        at, n = VECTOR_AT[name]
        return self.vectors[:, at:at + n]

    def table(self, name):
        at, n = TABLE_AT[name]
        return self.tables_sb[:, at:at + n]


def feature_norm(nc, S, name, src, dst, gains, nt, width):
    n, half = src.shape[2], nt // 2
    pool_tiles = max(1, nt // 4)
    with ExitStack() as ctx:
        sem = lambda x: S.semaphore(nc, name + x)
        root = ctx.enter_context(nc.sbuf_tensor(name + "_root", [128, T], F32)); inv = ctx.enter_context(nc.sbuf_tensor(name + "_inv", [128, T], F32))
        bank = ctx.enter_context(nc.psum_tensor(name + "_sum", [128, 512], F32))
        squared = [sem("_squared_v"), sem("_squared_a")]; summed = sem("_summed"); rooted = sem("_rooted"); inverted = sem("_inverted"); scaled = [sem("_scaled_v"), sem("_scaled_a")]; divided = sem("_divided")
        parts = max(1, half // 2)
        with nc.Block() as block:
            @block.scalar
            def _(act):
                for t in range(half, nt, half // parts):
                    act.activation(dst[:, t:t + half // parts, :], src[:, t:t + half // parts, :], ACT.Square).then_inc(squared[1], 1)
                act.wait_ge(summed, 1)
                act.activation(root[:, 0:n], bank[:, 0:n], ACT.Sqrt, bias=S.eps[:, :], scale=1.0 / width).then_inc(rooted, 1)
                act.wait_ge(divided, 1)
                for t in range(nt - pool_tiles, nt):
                    act.activation(dst[:, t, :], dst[:, t, :], ACT.Copy, scale=gains[:, t:t + 1]).then_inc(scaled[1], 1)

            @block.tensor
            def _(pe):
                for k in range(half):
                    for x in range(2):
                        if k % (half // parts) == 0:
                            pe.wait_ge(squared[x], k // (half // parts) + 1)
                        ins = pe.matmul(bank[:, 0:n], S.table("ones"), dst[:, half * x + k, :], start=(k == 0 and x == 0), stop=(k == half - 1 and x == 1))
                ins.then_inc(summed, 1)

            @block.vector
            def _(dve):
                for t in range(0, half, half // parts):
                    dve.tensor_tensor(dst[:, t:t + half // parts, :], src[:, t:t + half // parts, :], src[:, t:t + half // parts, :], ALU.mult).then_inc(squared[0], 1)
                dve.wait_ge(rooted, 1)
                dve.reciprocal(inv[:, 0:n], root[:, 0:n]).then_inc(inverted, 1)
                dve.wait_ge(inverted, 1)
                for t in range(nt - pool_tiles):
                    dve.scalar_tensor_tensor(dst[:, t, :], src[:, t, :], gains[:, t:t + 1], inv[:, 0:n], ALU.mult, ALU.mult).then_inc(scaled[0], 1)

            @block.gpsimd
            def _(pool):
                pool.wait_ge(inverted, 1)
                t = slice(nt - pool_tiles, nt)
                pool.tensor_tensor(dst[:, t, :], src[:, t, :], inv[:, 0:n].unsqueeze(1).to_broadcast([128, pool_tiles, n]), ALU.mult).then_inc(divided, 1)


def load_front(nc, d, S):
    with ExitStack() as ctx:
        sb = lambda n, s, t=F32: ctx.enter_context(nc.sbuf_tensor(n, s, t))
        ps = lambda n, s=(128, 512): ctx.enter_context(nc.psum_tensor(n, list(s), F32))
        sem = lambda n: S.semaphore(nc, n)
        rows = sb("vector_rows", [128, 2, 128]); x = sb("x_tokens", [128, 3, D]); prev = sb("prev_rows", [8, RPROJ])
        p_t = [ps(f"p_t{i}") for i in range(4)]; p_v = ps("p_v")
        cleared = sem("cleared"); rows_in = sem("vec_in"); x_in = [sem(f"x_in{i}") for i in range(3)]; prev_in = sem("prev_in"); tables_in = sem("tables_in"); ident_in = sem("ident_in")
        vec_turned = sem("vec_turned"); vec_done = sem("vec_done"); turned = sem("x_turned"); cv = sem("x_copied_v"); ca = sem("x_copied_a")
        prev_turned = sem("prev_turned"); prev_done = sem("prev_done"); parked = sem("x_parked"); xT = S.xT
        names = dict(w0='rwkv_w0', a0='rwkv_a0', k_k='rwkv_k_k', k_a='rwkv_k_a', gn_g='rwkv_gn_g', gn_b='rwkv_gn_b', ln_mix='ln_mix_g', q_norm='mla_q_norm_g',
                     kv_norm='mla_kv_norm_g', ln_mem='ln_mem_g', ln_moe='ln_moe_g', mem_norm='mem_norm_g')
        cols = [(128 * t, 128) for t in range(24)] + [(3072, 96), (3168, 96), (3264, 128), (3392, 128)]
        with nc.Block() as block:
            @block.sync
            def _(sp):
                sp.dma_start(S.tables_sb[:, 0:128], d['tables'][:, 0:128]).then_inc(ident_in, 16)
                xp = d['x_prompt'][0].rearrange("(i p) n -> i p n", p=128)
                for i, n in enumerate(TILE):
                    sp.dma_start(x[0:n, i, :], xp[i] if i < 2 else d['x_sample'].rearrange("b t n -> (b t) n")).then_inc(x_in[i], 16)
                sp.dma_start(prev[:, :], d['state_rwkv_shift'][0]).then_inc(prev_in, 16)
                sp.dma_start(S.tables_sb[:, 128:], d['tables'][:, 128:]).then_inc(tables_in, 16)
                sp.wait_ge(cleared, 3)
                mu = d['rwkv_mu'][0]
                sp.dma_start(rows[0:24, 0, :], mu[0:3072].rearrange("(r n) -> r n", n=128)).then_inc(rows_in, 16)
                sp.dma_start(rows[24:26, 0, 0:96], mu[3072:3264].rearrange("(r n) -> r n", n=96)).then_inc(rows_in, 16)
                sp.dma_start(rows[26:28, 0, :], mu[3264:3520].rearrange("(r n) -> r n", n=128)).then_inc(rows_in, 16)
                for name, n in VECTORS[1:]:
                    at = VECTOR_AT[name][0]
                    src = d['rwkv_r_k'][0].rearrange("h n -> (h n)") if name == 'r_k' else d[names[name]][0]
                    sp.dma_start(rows[at % 128:at % 128 + n, at // 128, :], src.rearrange("(r n) -> r n", n=128)).then_inc(rows_in, 16)
                sp.wait_ge(cv, 6)
                sp.wait_ge(ca, 6)
                sp.dma_start(S.xT_dram, xT[:, :, :].rearrange("p t n -> p (t n)")).then_inc(parked, 16)
                sp.wait_ge(parked, 16)
                sp.wait_ge(tables_in, 16)

            @block.gpsimd
            def _(pool):
                pool.memset(rows[:, :, :], 0.0).then_inc(cleared, 1)
                pool.memset(S.eps[:, :], EPS).then_inc(cleared, 1)
                pool.memset(S.P[:, :, :], 0.0).then_inc(cleared, 1)

            @block.tensor
            def _(pe):
                pe.wait_ge(ident_in, 16)
                k = 0
                for i, n in enumerate(TILE):
                    pe.wait_ge(x_in[i], 16)
                    for q in range(4):
                        if k >= 4:
                            pe.wait_ge((cv, ca)[k % 2], k // 2 - 1)
                        for t in range(4):
                            ins = pe.transpose(p_t[k % 4][:, n * t:n * t + n], x[0:n, i, 512 * q + 128 * t:512 * q + 128 * t + 128], S.ident[0:n, 0:n])
                        ins.then_inc(turned, 1)
                        k += 1
                pe.wait_ge(rows_in, 16 * (len(VECTORS) + 2))
                for i in range(2):
                    ins = pe.transpose(p_v[:, 128 * i:128 * i + 128], rows[:, i, :], S.ident)
                ins.then_inc(vec_turned, 1)
                pe.wait_ge(vec_done, 1)
                pe.wait_ge(prev_in, 16)
                for t, (c, n) in enumerate(cols):
                    ins = pe.transpose(p_v[0:n, 8 * t:8 * t + 8], prev[:, c:c + n], S.ident[0:8, 0:8])
                ins.then_inc(prev_turned, 1)

            def copies(eng, copy, parity, done):
                k = 0
                for i, n in enumerate(TILE):
                    for q in range(4):
                        if k % 2 == parity:
                            eng.wait_ge(turned, k + 1)
                            copy(S.xT[:, 4 * q:4 * q + 4, 128 * i:128 * i + n], p_t[k % 4][:, 0:4 * n].rearrange("p (t n) -> p t n", t=4)).then_inc(done, 1)
                        k += 1

            @block.vector
            def _(dve):
                copies(dve, dve.tensor_copy, 0, cv)
                dve.wait_ge(vec_turned, 1)
                dve.tensor_copy(S.vectors[:, :], p_v[:, 0:256]).then_inc(vec_done, 1)
                dve.wait_ge(prev_turned, 1)
                dve.wait_ge(cleared, 3)
                prev_cols = S.P[:, :, 257:329].rearrange("p t (b c) -> p t b c", c=9)[:, :, :, 0]
                src = p_v[:, 0:224].rearrange("p (t b) -> p t b", b=8)
                for lo, hi, n in ((0, 24, 128), (24, 26, 96), (26, 28, 128)):
                    dve.tensor_copy(prev_cols[0:n, lo:hi], src[0:n, lo:hi]).then_inc(prev_done, 1)

            @block.scalar
            def _(act):
                copies(act, act.copy, 1, ca)


FR = mybir.dt.float32r


def project(nc, S, name, x, w_of, turns, rest, raw, put, both, load_too=None):
    R = len(raw)
    assert R == 4 and rest
    total = R * turns + len(rest)
    PIECE = 4
    with ExitStack() as ctx:
        sem = lambda n: S.semaphore(nc, name + n)
        buf = lambda n, s: ctx.enter_context(nc.sbuf_tensor(name + n, s, FR))
        xh, xl = buf("_x_high", [128, DT, T]), buf("_x_low", [128, DT, T])
        wh = [buf(f"_w_high{i}", [128, DT, 128]) for i in range(2)]; wl = [buf(f"_w_low{i}", [128, DT, 128]) for i in range(2)]
        acc = [ctx.enter_context(nc.psum_tensor(f"{name}_acc{i}", [128, 512], F32)) for i in range(4)]
        loaded = [sem(f"_loaded{i}") for i in range(R)]; high, low, done = sem("_high"), sem("_low"), sem("_done"); x_high, x_low = sem("_x_high_made"), sem("_x_low_made")
        taken = [sem("_taken_v"), sem("_taken_a")]

        def columns(k):
            return rest[k - R * turns] if isinstance(k, int) and k >= R * turns else (128 * k, 128)

        def tiles(eng, body):
            if turns:
                with eng.Fori(0, turns) as it:
                    for s in range(R):
                        body(R * it + s, s, it)
            for k in range(R * turns, total):
                body(k, k % R, k // R)

        with nc.Block() as block:
            @block.sync
            def _(sp):
                def load(k, s):
                    c, m = columns(k)
                    sp.dma_start(raw[s][:, :, 0:m], w_of(c, m)).then_inc(loaded[s], 16)

                def reload(k, s):
                    sp.wait_ge(low, k - R + 1)
                    load(k, s)

                for k in range(R):
                    load(k, k)
                if load_too:
                    load_too(sp)
                if turns > 1:
                    with sp.Fori(1, turns) as it:
                        for s in range(R):
                            reload(R * it + s, s)
                for k in range(max(R, R * turns), total):
                    reload(k, k % R)

            @block.tensor
            def _(pe):
                def tile(k, s, it):
                    m = columns(k)[1]
                    pe.wait_ge(high, k + 1)
                    pe.wait_ge(low, k + 1)
                    if both:
                        pe.wait_ge(taken[s % 2], 2 * it + s // 2 + 1)
                    else:
                        pe.wait_ge(taken[0], k + 1)
                    o = acc[s][0:m, 0:T]
                    for t in range(DT):
                        pe.matmul(o, wh[s % 2][:, t, 0:m], xh[:, t, :], start=(t == 0), stop=False)
                        pe.matmul(o, wh[s % 2][:, t, 0:m], xl[:, t, :], start=False, stop=False)
                        ins = pe.matmul(o, wl[s % 2][:, t, 0:m], xh[:, t, :], start=False, stop=(t == DT - 1))
                    ins.then_inc(done, 1)

                pe.wait_ge(x_high, DT // PIECE)
                pe.wait_ge(x_low, DT // PIECE)
                tiles(pe, tile)

            def parts_free(eng, k):
                if not isinstance(k, int) or k >= 2:
                    eng.wait_ge(done, k - 1)

            def run(eng, copy, split, mine):
                for _ in range(2 if both else 4 if mine == 0 else 0):
                    eng.nop().then_inc(taken[mine], 1)

                def body(k, s, it):
                    if not isinstance(k, int) or k + 1 < total:
                        split(k + 1, (s + 1) % R, it + (s + 1) // R)
                    if s % 2 == mine if both else mine == 0:
                        eng.wait_ge(done, k + 1)
                        put(eng, copy, k, acc[s]).then_inc(taken[mine], 1)

                split(0, 0, 0)
                tiles(eng, body)

            @block.scalar
            def _(act):
                for q in range(DT // PIECE):
                    t = slice(PIECE * q, PIECE * q + PIECE)
                    act.copy(xh[:, t, :], x[:, t, :]).then_inc(x_high, 1)

                def split(k, s, it):
                    m = columns(k)[1]
                    act.wait_ge(loaded[s], 16 * (it + 1))
                    parts_free(act, k)
                    act.copy(wh[s % 2][:, :, 0:m], raw[s][:, :, 0:m]).then_inc(high, 1)
                run(act, act.copy, split, 1)

            @block.vector
            def _(dve):
                for q in range(DT // PIECE):
                    t = slice(PIECE * q, PIECE * q + PIECE)
                    dve.wait_ge(x_high, q + 1)
                    dve.tensor_tensor(xl[:, t, :], x[:, t, :], xh[:, t, :], ALU.subtract).then_inc(x_low, 1)

                def split(k, s, it):
                    m = columns(k)[1]
                    dve.wait_ge(high, k + 1)
                    parts_free(dve, k)
                    dve.tensor_tensor(wl[s % 2][:, :, 0:m], raw[s][:, :, 0:m], wh[s % 2][:, :, 0:m], ALU.subtract).then_inc(low, 1)
                run(dve, dve.tensor_copy, split, 0)


def project_in(nc, d, S):
    w = d['w_in'][0].rearrange("(t p) n -> p t n", p=128)
    rest = [(3072, 96), (3168, 96), (3264, 128), (3392, 128)] + [(3520 + 128 * i, 128) for i in range(6)] + [(4288, 64)]
    other = [S.qa[:, 0, :], S.qa[:, 1, :], S.qa[:, 2, :], S.qa[:, 3, :], S.kv[:, 0, :], S.kv[:, 1, :], S.kr]

    def put(eng, copy, k, bank):
        if isinstance(k, int) and k >= 28:
            dst = other[k - 28]
            return copy(dst, bank[0:dst.shape[0], 0:T])
        m = 96 if isinstance(k, int) and k in (24, 25) else 128
        dst = S.P[0:m, bass.ds(k, 1), :].rearrange("p t n -> p (t n)")
        copy(dst[:, 1:257], bank[0:m, 0:256])
        return copy(dst[:, 257:329].rearrange("p (b c) -> p b c", c=9)[:, :, 1:9], bank[0:m, 256:320].rearrange("p (b c) -> p b c", c=8))

    with nc.sbuf_tensor("w_in_raw", [128, DT, 128], F32) as own:
        project(nc, S, "w_in", S.hT, lambda c, m: w[:, :, bass.ds(c, m)], 6, rest, S.spare + [own], put, True)


def project_out(nc, d, S):
    w = d['w_out'][0].rearrange("(t p) n -> p t n", p=128)
    x_in = S.semaphore(nc, "xT_in")

    def put(eng, copy, k, bank):
        eng.wait_ge(x_in, 16)
        eng.nop(nofuse=True)
        x = S.xT[:, bass.ds(k, 1), :].rearrange("p t n -> p (t n)")
        return eng.tensor_tensor(x, x, bank[:, 0:T], ALU.add)

    with ExitStack() as ctx:
        raw = [ctx.enter_context(nc.sbuf_tensor(f"w_out_raw{i}", [128, DT, 128], F32)) for i in range(4)]
        project(nc, S, "w_out", S.mix, lambda c, m: w[:, :, bass.ds(c, m)], 3, [(128 * k, 128) for k in range(12, 16)], raw, put, False,
                lambda sp: sp.dma_start(S.xT[:, :, :].rearrange("p t n -> p (t n)"), S.xT_dram).then_inc(x_in, 16))


def memory_queries(nc, d, S):
    w = d['w_mq'][0].rearrange("(t p) n -> p t n", p=128)
    with ExitStack() as ctx:
        raw = S.spare_late + [ctx.enter_context(nc.sbuf_tensor(f"w_mq_raw{i}", [128, DT, 128], F32)) for i in range(2)]
        project(nc, S, "w_mq", S.mix, lambda c, m: w[:, :, c:c + m], 0, [(128 * k, 128) for k in range(MEMH)], raw,
                lambda eng, copy, k, bank: copy(S.mem_q[:, k, :], bank[:, 0:T]), True)


def rwkv_mix(nc, d, S, outs):
    with ExitStack() as ctx:
        sb = lambda n, s, t=F32: ctx.enter_context(nc.sbuf_tensor(n, s, t))
        ps = lambda n, s=(128, 512): ctx.enter_context(nc.psum_tensor(n, list(s), F32))
        sem = lambda n: S.semaphore(nc, n)
        P = S.P
        diff = sb("diff", [128, 28, T])
        xw = sb("xw", [128, 4, T])
        w_w2 = sb("w_w2", [96, 1024]); w_a2 = sb("w_a2", [96, 1024])
        last = sb("last", [9, RPROJ])
        p_z = [ps("p_z0"), ps("p_z1")]; p_last = ps("p_last", (16, 512))
        lora_in = sem("lora_in"); chain = sem("mix_chain"); mixed = sem("mixed"); tanh_done = sem("tanh_done"); z_done = sem("z_done"); z_used = sem("z_used")
        last_turned = sem("last_turned"); last_copied = sem("last_copied"); last_out = sem("last_out"); lw_raw = sem("lw_raw")
        cols = [(t, 128) for t in range(24)] + [(24, 96), (25, 96), (26, 128), (27, 128)]
        starts = [128 * t for t in range(24)] + [3072, 3168, 3264, 3392]
        HALF = 14
        diff_p = sem("mix_diff_pool")

        def differences(eng, t, done):
            eng.tensor_tensor(diff[:, t, 0:256], P[:, t, 0:256], P[:, t, 1:257], ALU.subtract).then_inc(done, 1)
            x = P[:, t, 257:329].rearrange("p t (b c) -> p t b c", c=9)
            eng.tensor_tensor(diff[:, t, 256:320].rearrange("p t (b c) -> p t b c", c=8), x[:, :, :, 0:8], x[:, :, :, 1:9], ALU.subtract).then_inc(done, 1)

        with nc.Block() as block:
            @block.gpsimd
            def _(pool):
                differences(pool, slice(HALF, 28), diff_p)

            @block.sync
            def _(sp):
                sp.dma_start(w_w2[:, :], d['rwkv_w_w2'][0]).then_inc(lora_in, 16)
                sp.dma_start(w_a2[:, :], d['rwkv_w_a2'][0]).then_inc(lora_in, 16)
                sp.wait_ge(last_copied, 28)
                sp.dma_start(outs[7][0], last[0:1, :]).then_inc(last_out, 16)
                sp.dma_start(outs[11][0], last[1:9, :]).then_inc(last_out, 16)
                sp.wait_ge(last_out, 32)

            @block.tensor
            def _(pe):
                for n, (t, m) in enumerate(cols):
                    if n >= 1:
                        pe.wait_ge(last_copied, n)
                    pe.transpose(p_last[0:9, 0:m], P[0:m, t, 256:329:9], S.ident[0:m, 0:m]).then_inc(last_turned, 1)
                pe.wait_ge(lora_in, 32)
                pe.wait_ge(tanh_done, 1)
                pe.wait_ge(mixed, 2)
                for n in range(16):
                    if n >= 2:
                        pe.wait_ge(z_used, n - 1)
                    w = (w_w2, w_a2)[n // 8]
                    x = xw[0:96, 0, :] if n < 8 else S.xa[0:96, :]
                    pe.matmul(p_z[n % 2][:, 0:T], w[:, 128 * (n % 8):128 * (n % 8) + 128], x, start=True, stop=True).then_inc(z_done, 1)

            @block.scalar
            def _(act):
                for n, (t, m) in enumerate(cols):
                    act.wait_ge(last_turned, n + 1)
                    act.copy(last[:, starts[n]:starts[n] + m], p_last[0:9, 0:m]).then_inc(last_copied, 1)
                act.wait_ge(mixed, 2)
                act.activation(xw[0:96, 0, :], xw[0:96, 1, :], ACT.Tanh).then_inc(tanh_done, 1)
                act.activation(S.sg[:, :, :], xw[:, 2:4, :], ACT.Sigmoid).then_inc(tanh_done, 1)
                for n in range(16):
                    act.wait_ge(z_done, n + 1)
                    o, b = (S.lw, S.vec('w0')) if n < 8 else (S.a, S.vec('a0'))
                    act.activation(o[:, n % 8, :], p_z[n % 2][:, 0:T], ACT.Sigmoid, bias=b[:, n % 8:n % 8 + 1]).then_inc(z_used, 1)

            @block.vector
            def _(dve):
                sp_ = P[:, :, 257:329].rearrange("p t (b c) -> p t b c", c=9)
                differences(dve, slice(0, HALF), chain)
                dve.wait_ge(chain, 2)
                dst = [S.r[:, t, :] for t in range(8)] + [S.k[:, t, :] for t in range(8)] + [S.v[:, t, :] for t in range(8)] + [xw[:, 1, :], S.xa, xw[:, 2, :], xw[:, 3, :]]
                mu = S.vec('mu')
                for t in range(28):
                    if t == HALF:
                        dve.wait_ge(diff_p, 2)
                    dve.scalar_tensor_tensor(dst[t][:, 0:256], diff[:, t, 0:256], mu[:, t:t + 1], P[:, t, 1:257], ALU.mult, ALU.add)
                    i2 = dve.scalar_tensor_tensor(dst[t][:, 256:320].rearrange("p (b c) -> p b c", c=8), diff[:, t, 256:320].rearrange("p (b c) -> p b c", c=8),
                                                  mu[:, t:t + 1], sp_[:, t, :, 1:9], ALU.mult, ALU.add)
                    if t in (23, 27):
                        i2.then_inc(mixed, 1)
                dve.wait_ge(z_used, 8)
                dve.tensor_scalar(S.lw[:, :, :].rearrange("p t n -> p (t n)"), S.lw[:, :, :].rearrange("p t n -> p (t n)"), -DECAY, None, ALU.mult).then_inc(lw_raw, 1)


def rwkv_pairs(nc, d, S, outs):
    with ExitStack() as ctx:
        sb = lambda n, s, t=F32: ctx.enter_context(nc.sbuf_tensor(n, s, t))
        ps = lambda n, s=(128, 512): ctx.enter_context(nc.psum_tensor(n, list(s), F32))
        sem = lambda n: S.semaphore(nc, n)
        ident = S.ident
        cum = [sb("cum0", [128, T]), sb("cum1", [128, T])]
        lpm = sb("lpm", [128, T]); lpe = sb("lpe", [128, T])
        e_pos = sb("e_pos", [128, T]); e_prev = sb("e_prev", [128, T]); e_inv = sb("e_inv", [128, T]); e_end = sb("e_end", [128, T])
        e_all = sb("e_all", [128, NCH + NB])
        kn = sb("kn", [128, T]); sq = sb("sq_k", [128, T]); nrm = sb("nrm", [128, T]); kp = sb("kp", [128, T]); bb = sb("bb", [128, T])
        al = sb("al", [128, T]); rho = sb("rho", [128, T]); be = sb("be", [128, T]); ka = sb("ka", [128, T])
        bend = sb("bend", [128, T]); kend = sb("kend", [128, T]); vv = sb("vv", [128, T])
        be_t = sb("be_t", [128, 3, 128]); ke_t = sb("ke_t", [128, 3, 128]); v_t = sb("v_t", [128, 3, 128])
        X0 = sb("X0", [128, 2, 3, 128]); Y1 = sb("Y1", [128, 2, 3, 128]); Z = sb("Z", [128, 2, 2, 128]); X = sb("X", [128, 2, 3, 128])
        mat = lambda n: sb(n, [128, 2, T])
        M = {n: mat("m_" + n) for n in ("DT", "D", "D2T", "D2", "ET", "AkT", "RbT", "RkT", "TA", "TB")}
        M["D4T"], M["D4"], M["D8"] = M["DT"], M["D"], M["D2T"]
        b_exp = sb("b_exp", [64, 2, 512]); k_exp = sb("k_exp", [64, 2, 512])
        mts = sb("mts", [128, 512]); st_in = sb("st_in", [64, 8, 128]); sig0 = sb("sig0", [128, 512]); st_out = sb("st_out", [128, 512]); st_a = sb("st_a", [128, 512])
        B = [ps(f"b{i}", (128, 1024)) for i in range(4)]
        PE_ = {n: i + 1 for i, n in enumerate(["DT", "tok1", "tok2", "AkT", "D", "D2", "RbT", "D2T", "T2", "D4", "RkT", "D4T", "T4", "X0", "D8", "T8",
                                              "Y1", "Z", "sig0", "mts", "stA", "W", "stB", "Rh", "MN", "Ys"])}
        DV = {n: i + 1 for i, n in enumerate(["DT", "D", "T1", "AkT", "exp", "RbT", "T2", "RkT", "T4", "T8",
                                             "mts", "W", "stB", "Rh", "MN"])}
        AC = {n: i + 1 for i, n in enumerate(["e_all", "tok1", "tok2", "D2", "D2T", "D4", "D4T", "X0", "D8", "Y1", "Z", "sig0", "stA", "Ys"])}
        mm = sem("pair_products"); dv = sem("pair_vector"); ac = sem("pair_scalar"); st_loaded = sem("st_loaded"); st_stored = sem("st_stored");
        vs = sem("pair_steps")
        front = sem("front_steps"); head_sums = sem("front_sums"); exps = sem("front_exps"); roots = sem("front_roots"); inverse = sem("front_inverse")
        bon = sb("bonus_sum", [128, T]); rho_s = sb("rho_s", [128, NB * ND])
        maxed = sem("front_maxed"); e_all_made = sem("e_all_made")
        root_n = sb("root_n", [128, T]); inv_n = sb("inv_n", [128, T])
        al_made = sem("front_al"); vv_made = sem("front_vv")
        F = dict(lp=19, sq=28, kn=30, rows=37)
        NPE, NDV, NAC = len(PE_), len(DV), len(AC)

        state = d['state_rwkv'][0]
        state_out = outs[10][0]
        with nc.Block() as block:
            @block.sync
            def _(sp):
                def load(j):
                    for h in range(2):
                        sp.dma_start(st_in[:, :, 64 * h:64 * h + 64], state[:, bass.ds(2 * j + h, 1), :, :].rearrange("b h v k -> v b (h k)")).then_inc(st_loaded, 16)

                def store(j):
                    sp.wait_ge(dv, j * NDV + DV["stB"])
                    sp.nop(nofuse=True)
                    for h in range(2):
                        sp.dma_start(state_out[:, bass.ds(2 * j + h, 1), :, :].rearrange("b h v k -> v b (h k)"), st_out[64 * h:64 * h + 64, :].rearrange("v (b k) -> v b k", b=NB)).then_inc(st_stored, 16)

                load(0)
                with sp.Fori(0, HP - 1) as j:
                    sp.wait_ge(mm, j * NPE + PE_["sig0"])
                    sp.nop(nofuse=True)
                    load(j + 1)
                    store(j)
                store(HP - 1)
                sp.wait_ge(st_stored, 32 * HP)

            @block.gpsimd
            def _(pool):
                def front_of(j):
                    k_ = [0]

                    def step(ins):
                        k_[0] += 1
                        ins.then_inc(front, 1)
                        pool.wait_ge(front, j * F["rows"] + k_[0])
                        pool.nop(nofuse=True)

                    at = lambda x: x[:, bass.ds(j, 1), :].rearrange("p j n -> p (j n)")
                    col = lambda n: S.vec(n)[:, bass.ds(j, 1)]
                    r, k, v, a, lw = at(S.r), at(S.k), at(S.v), at(S.a), at(S.lw)
                    if not isinstance(j, int):
                        pool.wait_ge(e_all_made, j)
                        pool.nop(nofuse=True)
                    pv = lambda x: x[:, 0:SEQ].rearrange("p (c t) -> p c t", t=CH)
                    sv = lambda x: x[:, SEQ:T].rearrange("p (c t) -> p c t", t=8)
                    src = lw
                    for n, s in enumerate((1, 2, 4, 8, 16)):
                        dst = cum[(n + 1) % 2]
                        step(pool.tensor_tensor(pv(dst)[:, :, s:CH], pv(src)[:, :, s:CH], pv(src)[:, :, 0:CH - s], ALU.add))
                        step(pool.tensor_copy(pv(dst)[:, :, 0:s], pv(src)[:, :, 0:s]))
                        if s < 8:
                            step(pool.tensor_tensor(sv(dst)[:, :, s:8], sv(src)[:, :, s:8], sv(src)[:, :, 0:8 - s], ALU.add))
                            step(pool.tensor_copy(sv(dst)[:, :, 0:s], sv(src)[:, :, 0:s]))
                        src = dst
                    lp = cum[1]
                    step(pool.tensor_tensor(lpm[:, :], lp[:, :], lw, ALU.subtract))
                    step(pool.tensor_tensor(pv(lpe), pv(lp)[:, :, CH - 1:CH].to_broadcast([128, NCH, CH]), pv(lp), ALU.subtract))
                    step(pool.tensor_tensor(sv(lpe), sv(lp)[:, :, 7:8].to_broadcast([128, NB, 8]), sv(lp), ALU.subtract))
                    assert k_[0] == F["lp"]
                    bc = lambda n: col(n).to_broadcast([128, T])
                    step(pool.tensor_copy(kp[:, :], a))
                    step(pool.tensor_scalar(kp[:, :], kp[:, :], -1.0, None, ALU.add))
                    step(pool.tensor_tensor(kp[:, :], kp[:, :], bc('k_a'), ALU.mult))
                    step(pool.tensor_scalar(kp[:, :], kp[:, :], 1.0, None, ALU.add))
                    step(pool.tensor_tensor(kp[:, :], kp[:, :], k, ALU.mult))
                    step(pool.tensor_tensor(bb[:, :], k, bc('k_k'), ALU.mult))
                    step(pool.tensor_tensor(nrm[:, :], r, bc('r_k'), ALU.mult))
                    step(pool.tensor_tensor(nrm[:, :], nrm[:, :], kp[:, :], ALU.mult))
                    step(pool.tensor_tensor(sq[:, :], bb[:, :], bb[:, :], ALU.mult))
                    assert k_[0] == F["sq"]
                    pool.wait_ge(inverse, j + 1)
                    pool.nop(nofuse=True)
                    step(pool.tensor_tensor(k, bon[:, :], v, ALU.mult))
                    step(pool.tensor_tensor(kn[:, :], bb[:, :], inv_n[:, :], ALU.mult))
                    assert k_[0] == F["kn"]
                    step(pool.tensor_tensor(bb[:, :], kn[:, :], a, ALU.mult))
                    if not isinstance(j, int):
                        pool.wait_ge(mm, (j - 1) * NPE + PE_["RkT"])
                        pool.nop(nofuse=True)
                    step(pool.tensor_tensor(r, r, e_pos[:, :], ALU.mult))
                    step(pool.tensor_copy(rho[:, :], r))
                    step(pool.tensor_tensor(be[:, :], bb[:, :], e_inv[:, :], ALU.mult))
                    step(pool.tensor_tensor(ka[:, :], kp[:, :], e_inv[:, :], ALU.mult))
                    step(pool.tensor_tensor(bend[:, :], bb[:, :], e_end[:, :], ALU.mult))
                    step(pool.tensor_tensor(kend[:, :], kp[:, :], e_end[:, :], ALU.mult))
                    assert k_[0] == F["rows"]

                front_of(0)
                with pool.Fori(1, HP) as j:
                    front_of(j)

            @block.tensor
            def _(pe):
                def sums(j):
                    pe.wait_ge(front, j * F["rows"] + F["sq"])
                    pe.matmul(B[0][:, 0:T], S.table('headsum'), sq[:, :], start=True, stop=True)
                    pe.matmul(B[0][:, 512:512 + T], S.table('headsum'), nrm[:, :], start=True, stop=True).then_inc(head_sums, 1)

                def body(j, more):
                    V = lambda n: pe.wait_ge(dv, j * NDV + DV[n])
                    A = lambda n: pe.wait_ge(ac, j * NAC + AC[n])

                    def prods(b, lhs, rhs, name, cols=lambda c, n: (c, n)):
                        for h in range(2):
                            for i, (c, n) in enumerate(SEC):
                                l, r = lhs(h, i), rhs(h, i)
                                o, w = cols(c, n)
                                ins = pe.matmul(B[b][0:n, 512 * h + o:512 * h + o + w], l, r, start=True, stop=True)
                        ins.then_inc(mm, 1)

                    feat = lambda x: lambda h, i: x[64 * h:64 * h + 64, SEC[i][0]:SEC[i][0] + SEC[i][1]]
                    sq_ = lambda x: lambda h, i: x[0:SEC[i][1], h, SEC[i][0]:SEC[i][0] + SEC[i][1]]
                    pe.wait_ge(front, (j + 1) * F["rows"])
                    pe.wait_ge(al_made, j + 1)
                    pe.wait_ge(vv_made, j + 1)
                    prods(3, feat(be), feat(al), "DT")
                    for b, name, srcs in ((1, "tok1", (al, bend)), (2, "tok2", (kend, vv))):
                        for x, src in enumerate(srcs):
                            for i, (c, n) in enumerate(SEC):
                                ins = pe.transpose(B[b][0:n, 512 * x + 128 * i:512 * x + 128 * i + 128], src[:, c:c + n], ident[:, :])
                        ins.then_inc(mm, 1)
                    def flip(b, x, name):
                        for h in range(2):
                            for i, (c, n) in enumerate(SEC):
                                ins = pe.transpose(B[b][0:n, 512 * h + c:512 * h + c + n], x[0:n, h, c:c + n], ident[0:n, 0:n])
                        ins.then_inc(mm, 1)

                    A("tok1"); prods(1, feat(ka), feat(al), "AkT")
                    V("DT"); flip(0, M["DT"], "D")
                    V("D"); prods(3, sq_(M["DT"]), sq_(M["D"]), "D2")
                    A("tok2"); prods(2, feat(be), feat(rho), "RbT")
                    A("D2"); flip(3, M["D2"], "D2T")
                    V("AkT"); prods(1, sq_(M["D2"]), sq_(M["TA"]), "T2")
                    A("D2T"); prods(0, sq_(M["D2T"]), sq_(M["D2"]), "D4")
                    V("RbT"); prods(2, feat(ka), feat(rho), "RkT")
                    A("D4"); flip(3, M["D4"], "D4T")
                    V("T2"); prods(1, sq_(M["D4"]), sq_(M["TB"]), "T4")
                    prods(0, sq_(M["AkT"]), lambda h, i: v_t[0:SEC[i][1], i, 64 * h:64 * h + 64], "X0", lambda c, n: (c // 2, 64))
                    A("D4T"); prods(3, sq_(M["D4T"]), sq_(M["D4"]), "D8")
                    A("D8"); V("T4")
                    prods(2, sq_(M["D8"]), sq_(M["TA"]), "T8")
                    A("X0"); V("T8")
                    wide = lambda x: lambda h, i: x[0:SEC[i][1], h, i, :]
                    prods(1, sq_(M["TB"]), wide(X0), "Y1", lambda c, n: (c, 128))
                    if more:
                        sums(j + 1)
                    A("Y1")
                    for h in range(2):
                        for i, (c, n) in enumerate(SEC[:2]):
                            ins = pe.matmul(B[2][:, 512 * h + 128 * i:512 * h + 128 * i + 128], M["ET"][:, h, c:c + n], Y1[:, h, i, :], start=True, stop=True)
                    ins.then_inc(mm, 1)
                    pe.wait_ge(st_loaded, 32 * (j + 1))
                    pe.nop(nofuse=True)
                    for b in range(NB):
                        ins = pe.transpose(B[1][:, 64 * b:64 * b + 64], st_in[:, b, :], ident[0:64, 0:64])
                    ins.then_inc(mm, 1)
                    for h in range(2):
                        ins = pe.matmul(B[1][64 * h:64 * h + 64, 512:1024], X[0:64, h, 2, 64:128], b_exp[:, h, :], start=True, stop=True)
                    ins.then_inc(mm, 1)
                    if more:
                        pe.wait_ge(roots, j + 2)
                        pe.nop(nofuse=True)
                    for h in range(2):
                        o = B[0][64 * h:64 * h + 64, 0:512]
                        pe.matmul(o, X[0:64, h, 2, 0:64], b_exp[:, h, :], start=True, stop=False)
                        ins = pe.matmul(o, v_t[0:64, 2, 64 * h:64 * h + 64], k_exp[:, h, :], start=False, stop=True)
                    ins.then_inc(mm, 1)
                    A("Z")
                    for h in range(2):
                        for i, (c, n) in enumerate(SEC[:2]):
                            ins = pe.matmul(B[3][:, 512 * h + 128 * i:512 * h + 128 * i + 128], M["TB"][:, h, c:c + n], Z[:, h, i, :], start=True, stop=True)
                    ins.then_inc(mm, 1)
                    V("mts"); A("sig0")
                    pe.nop(nofuse=True)
                    for h in range(2):
                        hk = slice(64 * h, 64 * h + 64)
                        for b in range(NB):
                            ins = pe.matmul(B[2][hk, 512 * h + 64 * b:512 * h + 64 * b + 64], sig0[hk, 64 * b:64 * b + 64], mts[hk, 64 * b:64 * b + 64], start=True, stop=True)
                    ins.then_inc(mm, 1)
                    V("W"); A("stA")
                    for h in range(2):
                        for i, (c, n) in enumerate(SEC):
                            pe.matmul(B[0][64 * h:64 * h + 64, c:c + n], X[0:n, h, i, 64:128], M["RbT"][0:n, h, c:c + n], start=True, stop=True)
                    for h in range(2):
                        for i, (c, n) in enumerate(SEC):
                            o = B[0][64 * h:64 * h + 64, 512 + c:512 + c + n]
                            pe.matmul(o, X[0:n, h, i, 0:64], M["RbT"][0:n, h, c:c + n], start=True, stop=False)
                            ins = pe.matmul(o, v_t[0:n, i, 64 * h:64 * h + 64], M["RkT"][0:n, h, c:c + n], start=False, stop=True)
                    ins.then_inc(mm, 1)
                    V("stB")
                    for c in range(NCH):
                        i, g = c // 4, c % 4
                        rows = slice(32 * g, 32 * g + 32)
                        bank = (B[2][:, 0:512], B[2][:, 512:1024], B[3][:, 0:512], B[3][:, 512:1024])[g]
                        for h in range(2):
                            hk = slice(64 * h, 64 * h + 64)
                            pe.matmul(bank[hk, 64 * i:64 * i + 64], X[rows, h, i, 64:128], be_t[rows, i, hk], start=True, stop=True)
                            o = bank[hk, 128 + 64 * i:128 + 64 * i + 64]
                            pe.matmul(o, be_t[rows, i, hk], X[rows, h, i, 0:64], start=True, stop=False)
                            ins = pe.matmul(o, ke_t[rows, i, hk], v_t[rows, i, hk], start=False, stop=True)
                    ins.then_inc(mm, 1)
                    V("Rh")
                    pe.nop(nofuse=True)
                    for h in range(2):
                        hk = slice(64 * h, 64 * h + 64)
                        for b in range(NB):
                            ins = pe.matmul(B[1][hk, 512 * h + 8 * b:512 * h + 8 * b + 8], sig0[hk, 64 * b:64 * b + 64],
                                            rho_s[hk, 8 * b:8 * b + 8], start=True, stop=True)
                    ins.then_inc(mm, 1)
                    V("MN"); A("Ys")

                sums(0)
                with pe.Fori(0, HP - 1) as j:
                    body(j, True)
                body(HP - 1, False)

            @block.scalar
            def _(act):
                def front_exps(j):
                    act.wait_ge(front, j * F["rows"] + F["lp"])
                    act.activation(e_pos[:, :], cum[1][:, :], ACT.Exp)
                    act.activation(e_prev[:, :], lpm[:, :], ACT.Exp)
                    act.activation(e_inv[:, :], cum[1][:, :], ACT.Exp, scale=-1.0)
                    act.activation(e_end[:, :], lpe[:, :], ACT.Exp).then_inc(exps, 1)

                def front_roots(j):
                    act.wait_ge(head_sums, j + 1)
                    act.activation(root_n[:, :], B[0][:, 0:T], ACT.Sqrt)
                    act.copy(bon[:, :], B[0][:, 512:512 + T]).then_inc(roots, 1)

                def front_values(j):
                    act.copy(vv[:, :], S.v[:, bass.ds(j, 1), :].rearrange("p j n -> p (j n)")).then_inc(vv_made, 1)

                def body(j, more):
                    V = lambda n: act.wait_ge(dv, j * NDV + DV[n])
                    Pm = lambda n: act.wait_ge(mm, j * NPE + PE_[n])
                    act.activation(e_all[:, 0:NCH], cum[1][:, CH - 1:SEQ:CH], ACT.Exp)
                    act.activation(e_all[:, NCH:], cum[1][:, SEQ + 7:T:8], ACT.Exp).then_inc(ac, 1)
                    act.wait_ge(ac, j * NAC + AC["e_all"])
                    act.nop().then_inc(e_all_made, 1)

                    def both(dst, b, name):
                        Pm(name)
                        src = B[b][:, :].rearrange("p (h n) -> p h n", h=2)
                        act.copy(dst[0:128, :, 0:256], src[0:128, :, 0:256])
                        act.copy(dst[0:64, :, 256:320], src[0:64, :, 256:320]).then_inc(ac, 1)

                    def two(dst0, dst1, b, name):
                        Pm(name)
                        act.copy(dst0[:, 0:2, :], B[b][:, 0:256].rearrange("p (i n) -> p i n", i=2))
                        act.copy(dst1[:, 0:2, :], B[b][:, 512:768].rearrange("p (i n) -> p i n", i=2))
                        act.copy(dst0[0:64, 2, :], B[b][0:64, 256:384])
                        return act.copy(dst1[0:64, 2, :], B[b][0:64, 768:896])

                    Pm("tok1")
                    for h in range(2):
                        act.copy(X0[:, h, 0:2, 64:128], B[1][:, 0:256].rearrange("p (i n) -> p i n", i=2)[:, :, 64 * h:64 * h + 64])
                        act.copy(X0[0:64, h, 2, 64:128], B[1][0:64, 256 + 64 * h:256 + 64 * h + 64])
                    act.copy(be_t[:, 0:2, :], B[1][:, 512:768].rearrange("p (i n) -> p i n", i=2))
                    act.copy(be_t[0:64, 2, :], B[1][0:64, 768:896]).then_inc(ac, 1)
                    two(ke_t, v_t, 2, "tok2").then_inc(ac, 1)
                    both(M["D2"], 3, "D2")
                    both(M["D2T"], 3, "D2T")
                    if more:
                        front_exps(j + 1)
                    both(M["D4"], 0, "D4")
                    both(M["D4T"], 3, "D4T")
                    Pm("X0")
                    src = B[0][:, :].rearrange("p (h n) -> p h n", h=2)
                    for i, (c, n) in enumerate(SEC):
                        ins = act.copy(X0[0:n, :, i, 0:64], src[0:n, :, c // 2:c // 2 + 64])
                    ins.then_inc(ac, 1)
                    both(M["D8"], 3, "D8")
                    for dst, b, name in ((Y1, 1, "Y1"), (Z, 2, "Z")):
                        Pm(name)
                        src = B[b][:, :].rearrange("p (h n) -> p h n", h=2)
                        if name == "Y1":
                            act.copy(X[0:64, :, 2, :], src[0:64, :, 256:384])
                        act.copy(dst[:, :, 0:2, :].rearrange("p h i n -> p h (i n)"), src[:, :, 0:256]).then_inc(ac, 1)
                        if name == "Y1" and more:
                            front_roots(j + 1)
                    Pm("sig0")
                    act.copy(sig0[:, :], B[1][:, 0:512]).then_inc(ac, 1)
                    Pm("stA")
                    act.copy(st_a[:, :], B[0][:, 0:512]).then_inc(ac, 1)
                    if more:
                        front_values(j + 1)
                    Pm("Ys")
                    act.copy(S.ys[0:64, bass.ds(j, 1), :].rearrange("p j n -> p (j n)"), B[1][0:64, 0:64])
                    act.copy(S.ys[64:128, bass.ds(j, 1), :].rearrange("p j n -> p (j n)"), B[1][64:128, 512:576]).then_inc(ac, 1)
                    V("MN")

                front_values(0)
                front_exps(0)
                front_roots(0)
                with act.Fori(0, HP - 1) as j:
                    body(j, True)
                body(HP - 1, False)

            @block.vector
            def _(dve):
                steps = 2

                def front_inverse(j):
                    dve.wait_ge(roots, j + 1)
                    dve.tensor_scalar(root_n[:, :], root_n[:, :], 1e-12, None, ALU.max).then_inc(maxed, 1)
                    dve.wait_ge(maxed, j + 1)
                    dve.reciprocal(inv_n[:, :], root_n[:, :]).then_inc(inverse, 1)

                def front_al(j):
                    dve.wait_ge(front, j * F["rows"] + F["kn"])
                    dve.scalar_tensor_tensor(al[:, :], kn[:, :], -1.0, e_prev[:, :], ALU.mult, ALU.mult).then_inc(al_made, 1)

                def body(j, more):
                    k_ = [0, 0]

                    def done(ins, n=None):
                        k_[0] += 1
                        assert n is None or DV[n] == k_[0], n
                        ins.then_inc(dv, 1)
                        dve.wait_ge(dv, j * NDV + k_[0])

                    def step(ins):
                        k_[1] += 1
                        ins.then_inc(vs, 1)
                        dve.wait_ge(vs, j * steps + k_[1])

                    A = lambda n: dve.wait_ge(ac, j * NAC + AC[n])
                    Pm = lambda n: dve.wait_ge(mm, j * NPE + PE_[n])
                    at = lambda x: x[:, bass.ds(j, 1), :].rearrange("p j n -> p (j n)")
                    r, a = at(S.r), at(S.a)

                    def masked(dst, b, mask):
                        ps_ = B[b][:, :].rearrange("p (h n) -> p h n", h=2)
                        m = S.table(mask)
                        dve.tensor_tensor(dst[0:128, :, 0:256], ps_[0:128, :, 0:256], m[0:128, 0:256].unsqueeze(1).to_broadcast([128, 2, 256]), ALU.mult)
                        return dve.tensor_tensor(dst[0:64, :, 256:320], ps_[0:64, :, 256:320], m[0:64, 256:320].unsqueeze(1).to_broadcast([64, 2, 64]), ALU.mult)

                    Pm("DT")
                    masked(M["DT"], 3, "before16")
                    done(masked(M["ET"], 3, "cross"), "DT")
                    Pm("D"); done(masked(M["D"], 0, "after16"), "D")
                    def added(dst, x, b, name):
                        if b is None:
                            y = S.table('one')
                            y1 = y[0:128, 0:256].unsqueeze(1).to_broadcast([128, 2, 256]); y2 = y[0:64, 256:320].unsqueeze(1).to_broadcast([64, 2, 64])
                        else:
                            ps_ = B[b][:, :].rearrange("p (h n) -> p h n", h=2)
                            y1, y2 = ps_[0:128, :, 0:256], ps_[0:64, :, 256:320]
                        dve.tensor_tensor(dst[0:128, :, 0:256], x[0:128, :, 0:256], y1, ALU.add)
                        done(dve.tensor_tensor(dst[0:64, :, 256:320], x[0:64, :, 256:320], y2, ALU.add), name)

                    added(M["TA"], M["DT"], None, "T1")
                    Pm("AkT"); done(masked(M["AkT"], 1, "before"), "AkT")
                    A("tok2")
                    for dst, src in ((b_exp, be_t), (k_exp, ke_t)):
                        for h in range(2):
                            ins = dve.tensor_tensor(dst[:, h, :].rearrange("p (b k) -> p b k", b=NB), src[0:64, 2, 64 * h:64 * h + 64].unsqueeze(1).to_broadcast([64, NB, 64]),
                                                    S.table('own')[0:64, :].unsqueeze(2).to_broadcast([64, NB, 64]), ALU.mult)
                    step(dve.tensor_tensor(mts[:, :].rearrange("p (b k) -> p b k", b=NB), S.table('eye2').unsqueeze(1).to_broadcast([128, NB, 64]),
                                           e_all[:, NCH:].unsqueeze(2).to_broadcast([128, NB, 64]), ALU.mult))
                    done(ins, "exp")
                    Pm("RbT"); done(masked(M["RbT"], 2, "upto"), "RbT")
                    Pm("T2"); added(M["TB"], M["TA"], 1, "T2")
                    Pm("RkT"); done(masked(M["RkT"], 2, "upto"), "RkT")
                    Pm("T4"); added(M["TA"], M["TB"], 1, "T4")
                    Pm("T8"); added(M["TB"], M["TA"], 2, "T8")
                    if more:
                        front_inverse(j + 1)
                    Pm("mts")
                    done(dve.tensor_tensor(mts[:, :], mts[:, :], B[1][:, 512:1024], ALU.add), "mts")
                    Pm("W"); A("Y1")
                    done(dve.tensor_tensor(X[:, :, 0:2, :].rearrange("p h i n -> p h (i n)"), Y1[:, :, 0:2, :].rearrange("p h i n -> p h (i n)"),
                                           B[3][:, :].rearrange("p (h n) -> p h n", h=2)[:, :, 0:256], ALU.add), "W")
                    if more:
                        front_al(j + 1)
                    Pm("stB"); A("stA")
                    dve.wait_ge(st_stored, 32 * j)
                    for h in range(2):
                        hk = slice(64 * h, 64 * h + 64)
                        ins = dve.tensor_tensor(st_out[hk, :], st_a[hk, :], B[2][hk, 512 * h:512 * h + 512], ALU.add)
                    done(ins, "stB")
                    Pm("Rh")
                    step(dve.tensor_tensor(r, r, B[0][:, 0:T], ALU.add))
                    dve.tensor_copy(rho_s[:, :], r[:, 256:320])
                    done(dve.tensor_copy(a, B[0][:, 512:512 + T]), "Rh")
                    Pm("MN")
                    for g in range(4):
                        bank = (B[2][:, 0:512], B[2][:, 512:1024], B[3][:, 0:512], B[3][:, 512:1024])[g]
                        for i in range(2):
                            c = 4 * i + g
                            dve.scalar_tensor_tensor(S.mt[:, bass.ds(j, 1), c, :].rearrange("p j n -> p (j n)"), S.table('eye2'), e_all[:, c:c + 1], bank[:, 64 * i:64 * i + 64], ALU.mult, ALU.add)
                            ins = dve.tensor_copy(S.nn[:, c, bass.ds(j, 1), :].rearrange("p j n -> p (j n)"), bank[:, 128 + 64 * i:128 + 64 * i + 64])
                    done(ins, "MN")
                    assert k_[0] == NDV and k_[1] == steps

                front_inverse(0)
                front_al(0)
                with dve.Fori(0, HP - 1) as j:
                    body(j, True)
                body(HP - 1, False)


def rwkv_chain(nc, d, S, outs):
    with ExitStack() as ctx:
        sb = lambda n, s, t=F32: ctx.enter_context(nc.sbuf_tensor(n, s, t))
        ps = lambda n, s=(128, 512): ctx.enter_context(nc.psum_tensor(n, list(s), F32))
        sem = lambda n: S.semaphore(nc, n)
        st = S.nn
        w_g2 = sb("w_g2", [128, 2, 1024])
        fin = sb("fin_state", [64, 16 * 64])
        cen = sb("gn_cen", [128, 2, T]); sqr = sb("gn_sq", [128, 2, T]); root = sb("gn_root", [128, 2, T]); inv = sb("gn_inv", [128, 2, T]); 
        eps = sb("gn_eps", [128, 1])
        p_s = [ps("p_s0"), ps("p_s1")]
        p_y = [[ps("p_y00"), ps("p_y01")], [ps("p_y10"), ps("p_y11")]]
        p_a = ps("p_ga"); p_b = ps("p_gb")
        stepped = sem("stepped"); added_ = sem("state_added"); y_done = sem("prompt_y"); y_used = sem("prompt_y_added")
        fin_turned = sem("fin_turned"); fin_copied = sem("fin_copied"); fin_out = sem("fin_out"); g2_in = sem("g2_in")
        meant = sem("gn_meant"); centred = sem("gn_centred"); squared = sem("gn_squared"); sq_summed = sem("gn_sq_summed"); rooted = sem("gn_rooted"); inverted = sem("gn_inverted")
        gate_made = sem("gate_made"); gated = sem("gated"); gs = sem("gn_steps"); eps_set = sem("gn_eps_set")
        p_mean, p_sq, p_gate = [p_a, p_b], p_y[0], p_y[1]
        y = S.a
        with nc.Block() as block:
            @block.sync
            def _(sp):
                sp.dma_start(w_g2[:, :, :], d['rwkv_w_g2'][0].rearrange("(t p) n -> p t n", p=128)).then_inc(g2_in, 16)
                sp.wait_ge(fin_copied, 2)
                sp.dma_start(outs[6][0, 0].rearrange("h v k -> v h k"), fin[:, :].rearrange("v (h k) -> v h k", h=16)).then_inc(fin_out, 16)
                sp.wait_ge(fin_out, 16)

            @block.tensor
            def _(pe):
                for c in range(1, NCH):
                    if c >= 2:
                        pe.wait_ge(added_, 2 * (c - 1))
                    for h in range(2):
                        hk = slice(64 * h, 64 * h + 64)
                        for j in range(HP):
                            ins = pe.matmul(p_s[h][hk, 64 * j:64 * j + 64], S.mt[hk, j, c, :], st[hk, c - 1, j, :], start=True, stop=True)
                        ins.then_inc(stepped, 1)
                pe.wait_ge(added_, 2 * (NCH - 1))
                for q in range(4):
                    if q >= 2:
                        pe.wait_ge(y_used, 4 * (q - 1))
                    for jj in range(2):
                        j = 2 * q + jj
                        for h in range(2):
                            hk = slice(64 * h, 64 * h + 64)
                            for c in range(1, NCH):
                                ins = pe.matmul(p_y[q % 2][h][hk, 256 * jj + CH * c:256 * jj + CH * c + CH], st[hk, c - 1, j, :], S.r[hk, j, CH * c:CH * c + CH], start=True, stop=True)
                    ins.then_inc(y_done, 1)
                for j in range(HP):
                    ins = pe.transpose(p_s[j // 4][0:64, 128 * (j % 4):128 * (j % 4) + 128], st[:, NCH - 1, j, :], S.ident)
                    if j % 4 == 3:
                        ins.then_inc(fin_turned, 1)
                pe.wait_ge(g2_in, 16)
                pe.wait_ge(y_used, 16)
                pe.wait_ge(gs, 1)
                def mean_of(j):
                    if j >= 2:
                        pe.wait_ge(centred, j - 1)
                    pe.matmul(p_mean[j % 2][:, 0:T], S.table('headsum'), y[:, j, :], start=True, stop=True).then_inc(meant, 1)

                mean_of(0)
                for j in range(HP):
                    if j + 1 < HP:
                        mean_of(j + 1)
                    if j >= 2:
                        pe.wait_ge(gated, j - 1)
                    for t in range(2):
                        ins = pe.matmul(p_gate[j % 2][:, 0:T], w_g2[:, t, 128 * j:128 * j + 128], S.sg[:, t, :], start=(t == 0), stop=(t == 1))
                    ins.then_inc(gate_made, 1)
                    pe.wait_ge(squared, j + 1)
                    if j >= 2:
                        pe.wait_ge(rooted, j - 1)
                    pe.matmul(p_sq[j % 2][:, 0:T], S.table('headsum'), sqr[:, j % 2, :], start=True, stop=True).then_inc(sq_summed, 1)

            @block.scalar
            def _(act):
                for q in range(2):
                    act.wait_ge(fin_turned, q + 1)
                    act.copy(fin[:, 512 * q:512 * q + 512], p_s[q][0:64, :]).then_inc(fin_copied, 1)
                act.wait_ge(eps_set, 1)
                def square_of(j):
                    act.wait_ge(centred, j + 1)
                    if j >= 2:
                        act.wait_ge(sq_summed, j - 1)
                    act.activation(sqr[:, j % 2, :], cen[:, j % 2, :], ACT.Square).then_inc(squared, 1)

                square_of(0)
                for j in range(HP):
                    if j + 1 < HP:
                        square_of(j + 1)
                    act.wait_ge(sq_summed, j + 1)
                    if j >= 2:
                        act.wait_ge(inverted, j - 1)
                    act.activation(root[:, j % 2, :], p_sq[j % 2][:, 0:T], ACT.Sqrt, bias=eps[:, :], scale=1.0 / HD).then_inc(rooted, 1)

            @block.vector
            def _(dve):
                dve.memset(eps[:, :], GN_EPS).then_inc(eps_set, 1)
                for c in range(1, NCH):
                    for h in range(2):
                        hk = slice(64 * h, 64 * h + 64)
                        dve.wait_ge(stepped, 2 * (c - 1) + h + 1)
                        s = st[hk, c, :, :].rearrange("p j v -> p (j v)")
                        dve.tensor_tensor(s, s, p_s[h][hk, :], ALU.add).then_inc(added_, 1)
                k = 0
                for q in range(4):
                    dve.wait_ge(y_done, q + 1)
                    for jj in range(2):
                        for h in range(2):
                            hk = slice(64 * h, 64 * h + 64)
                            o = y[hk, 2 * q + jj, CH:SEQ]
                            dve.tensor_tensor(o, o, p_y[q % 2][h][hk, 256 * jj + CH:256 * jj + 256], ALU.add).then_inc(y_used, 1)
                ys = y[:, :, 256:320]
                dve.tensor_tensor(ys, ys, S.ys[:, :, :], ALU.add).then_inc(gs, 1)
                done = [1]

                def step(ins):
                    done[0] += 1
                    ins.then_inc(gs, 1)
                    dve.wait_ge(gs, done[0])

                dve.wait_ge(gs, 1)
                dve.wait_ge(y_used, 16)
                def centre(j):
                    dve.wait_ge(meant, j + 1)
                    if j >= 2:
                        dve.wait_ge(gated, j - 1)
                    dve.scalar_tensor_tensor(cen[:, j % 2, :], p_mean[j % 2][:, 0:T], -1.0 / HD, y[:, j, :], ALU.mult, ALU.add).then_inc(centred, 1)

                centre(0)
                for j in range(HP):
                    if j + 1 < HP:
                        centre(j + 1)
                    x = cen[:, j % 2, :]
                    dve.wait_ge(rooted, j + 1)
                    dve.reciprocal(inv[:, j % 2, :], root[:, j % 2, :]).then_inc(inverted, 1)
                    dve.wait_ge(inverted, j + 1)
                    step(dve.tensor_tensor(x, x, inv[:, j % 2, :], ALU.mult))
                    step(dve.tensor_scalar(x, x, S.vec('gn_g')[:, j:j + 1], S.vec('gn_b')[:, j:j + 1], ALU.mult, ALU.add))
                    step(dve.tensor_tensor(x, x, S.k[:, j, :], ALU.add))
                    dve.wait_ge(gate_made, j + 1)
                    dve.tensor_tensor(S.mix[:, j, :], x, p_gate[j % 2][:, 0:T], ALU.mult).then_inc(gated, 1)


def mla_project(nc, d, S, outs):
    with ExitStack() as ctx:
        sb = lambda n, s, t=F32: ctx.enter_context(nc.sbuf_tensor(n, s, t))
        ps = lambda n, s=(128, 512): ctx.enter_context(nc.psum_tensor(n, list(s), F32))
        sem = lambda n: S.semaphore(nc, n)
        w_qb = S.w_qb
        w_ukT = sb("w_ukT", [128, MH, KVL])
        q_nope = sb("q_nope", [128, MH, T]); q_raw = sb("q_raw", [64, MH, T])
        turned_q = sb("turned_q", [64, MH, T]); turned_k = sb("turned_k", [64, T]); sin_k = sb("sin_k", [64, T])
        bank = [ps(f"p_proj{i}") for i in range(4)]; p_rot = [ps("p_rot0"), ps("p_rot1")]; p_tok = [ps("p_tok0"), ps("p_tok1")]
        w_in = S.qb_in; produced = sem("q_produced"); copied = [sem("q_copied_v"), sem("q_copied_a")]
        rotated = sem("rotated"); rot_used = sem("rot_used"); steps = sem("rope_steps"); tok_turned = sem("tok_turned"); tok_copied = sem("tok_copied"); latents_out = sem("latents_out")
        cos, sin = S.table("cos")[0:64, :], S.table("sin")[0:64, :]
        with nc.Block() as block:
            @block.sync
            def _(sp):
                for i, n in enumerate(TILE):
                    sp.wait_ge(tok_copied, 2 * (i + 1))
                    for o, src in ((0, S.c_tok), (1, S.kp_tok)):
                        dst = outs[2 + o][0, 0, 128 * i:128 * i + 128, :] if i < 2 else outs[8 + o][0].rearrange("b t n -> (b t) n")
                        sp.dma_start(dst, src[0:n, i, :]).then_inc(latents_out, 16)
                sp.wait_ge(latents_out, 96)

            @block.tensor
            def _(pe):
                pe.wait_ge(w_in, 32)

                def free(k):
                    if k >= 4:
                        pe.wait_ge(copied[k % 2], k // 2 - 1)
                k = 0
                for g in range(4):
                    for hh in range(2):
                        for ci in range(2):
                            h = 2 * g + hh
                            ins = pe.transpose(bank[k % 4][:, 256 * hh + 128 * ci:256 * hh + 128 * ci + 128], S.w_kvb[:, ci, 256 * h:256 * h + 128], S.ident)
                    ins.then_inc(produced, 1)
                    k += 1
                for h in range(MH):
                    for m, c in ((128, 192 * h), (64, 192 * h + 128)):
                        free(k)
                        for t in range(4):
                            ins = pe.matmul(bank[k % 4][0:m, 0:T], w_qb[:, t, c:c + m], S.qn[:, t, :], start=(t == 0), stop=(t == 3))
                        ins.then_inc(produced, 1)
                        k += 1
                pe.wait_ge(copied[0], 10)
                pe.wait_ge(copied[1], 10)
                for h in range(MH):
                    for ci in range(2):
                        free(k)
                        pe.matmul(bank[k % 4][:, 0:T], w_ukT[:, h, 128 * ci:128 * ci + 128], q_nope[:, h, :], start=True, stop=True).then_inc(produced, 1)
                        k += 1
                for h in range(MH + 1):
                    if h >= 2:
                        pe.wait_ge(rot_used, h - 1)
                    src = q_raw[:, h, :] if h < MH else S.kr[:, :]
                    pe.matmul(p_rot[h % 2][0:64, 0:T], S.table("rot")[0:64, 0:64], src, start=True, stop=True).then_inc(rotated, 1)
                pe.wait_ge(steps, 4)
                for i, n in enumerate(TILE):
                    if i >= 2:
                        pe.wait_ge(tok_copied, 2 * (i - 1))
                    for ci in range(2):
                        pe.transpose(p_tok[i % 2][0:n, 128 * ci:128 * ci + 128], S.c[:, ci, 128 * i:128 * i + n], S.ident)
                    pe.transpose(p_tok[i % 2][0:n, 256:320], S.kp[:, 128 * i:128 * i + n], S.ident[0:64, 0:64]).then_inc(tok_turned, 1)

            def copies(eng, copy, parity):
                k = 0
                for g in range(4):
                    if k % 2 == parity:
                        eng.wait_ge(produced, k + 1)
                        copy(w_ukT[:, 2 * g:2 * g + 2, :].rearrange("p h n -> p (h n)"), bank[k % 4][:, :]).then_inc(copied[parity], 1)
                    k += 1
                for h in range(MH):
                    for m, dst in ((128, q_nope), (64, q_raw)):
                        if k % 2 == parity:
                            eng.wait_ge(produced, k + 1)
                            copy(dst[:, h, :], bank[k % 4][0:m, 0:T]).then_inc(copied[parity], 1)
                        k += 1
                for h in range(MH):
                    for ci in range(2):
                        if k % 2 == parity:
                            eng.wait_ge(produced, k + 1)
                            copy(S.q_lat[:, ci, h, :], bank[k % 4][:, 0:T]).then_inc(copied[parity], 1)
                        k += 1

            @block.vector
            def _(dve):
                copies(dve, dve.tensor_copy, 0)
                dve.wait_ge(copied[1], 10)
                dve.tensor_tensor(S.q_pe[:, :, :], q_raw[:, :, :], cos.unsqueeze(1).to_broadcast([64, MH, T]), ALU.mult).then_inc(steps, 1)
                dve.tensor_tensor(sin_k[:, :], S.kr[:, :], cos, ALU.mult).then_inc(steps, 1)
                for h in range(MH + 1):
                    dve.wait_ge(rotated, h + 1)
                    dst = turned_q[:, h, :] if h < MH else turned_k[:, :]
                    dve.tensor_tensor(dst, p_rot[h % 2][0:64, 0:T], sin, ALU.mult).then_inc(rot_used, 1)
                dve.wait_ge(rot_used, MH + 1)
                dve.wait_ge(steps, 2)
                dve.tensor_tensor(S.kp[:, :], sin_k[:, :], turned_k[:, :], ALU.add).then_inc(steps, 1)
                dve.tensor_tensor(S.q_pe[:, :, :], S.q_pe[:, :, :], turned_q[:, :, :], ALU.add).then_inc(steps, 1)

            @block.scalar
            def _(act):
                copies(act, act.copy, 1)
                for i, n in enumerate(TILE):
                    act.wait_ge(tok_turned, i + 1)
                    act.copy(S.c_tok[0:n, i, :], p_tok[i % 2][0:n, 0:256]).then_inc(tok_copied, 1)
                    act.copy(S.kp_tok[0:n, i, :], p_tok[i % 2][0:n, 256:320]).then_inc(tok_copied, 1)


def mla_prompt(nc, d, S):
    with ExitStack() as ctx:
        sb = lambda n, s, t=F32: ctx.enter_context(nc.sbuf_tensor(n, s, t))
        ps = lambda n, s=(128, 1024): ctx.enter_context(nc.psum_tensor(n, list(s), F32))
        sem = lambda n: S.semaphore(nc, n)
        score = sb("score_p", [128, 2, 4, SEQ]); prob = sb("prob_p", [128, 2, 4, SEQ]); probT = sb("probT_p", [128, 4, 2, 128])
        stat = sb("stat_p", [128, 4, 4, 4])
        p_s = [ps("pp_s0"), ps("pp_s1")]; p_t = ps("pp_t"); p_o = ps("pp_o")
        scored = sem("p_scored"); masked = sem("p_masked"); chain = sem("p_chain"); bias = sem("p_bias"); exped = sem("p_exped"); norm = sem("p_norm")
        turned = sem("p_turned"); tv = sem("p_turn_v"); ta = sem("p_turn_a"); made = sem("p_made"); ov = sem("p_out_v")
        GROUPS = [(i, q) for i in range(2) for q in range(2)]
        with nc.Block() as block:
            @block.tensor
            def _(pe):
                def scores(g):
                    i, q = GROUPS[g]
                    w = 128 * (i + 1)
                    if g >= 2:
                        pe.wait_ge(masked, g - 1)
                    for x in range(4):
                        h = 4 * q + x
                        o = p_s[g % 2][:, 256 * x:256 * x + w]
                        for ci in range(2):
                            pe.matmul(o, S.q_lat[:, ci, h, 128 * i:128 * i + 128], S.c[:, ci, 0:w], start=(ci == 0), stop=False)
                        ins = pe.matmul(o, S.q_pe[:, h, 128 * i:128 * i + 128], S.kp[:, 0:w], start=False, stop=True)
                    ins.then_inc(scored, 1)

                scores(0)
                for g, (i, q) in enumerate(GROUPS):
                    if g + 1 < 4:
                        scores(g + 1)
                    pe.wait_ge(norm, g + 1)
                    if g >= 1:
                        pe.wait_ge(tv, g)
                        pe.wait_ge(ta, g)
                    for x in range(4):
                        for b in range(i + 1):
                            ins = pe.transpose(p_t[:, 256 * x + 128 * b:256 * x + 128 * b + 128], prob[:, g % 2, x, 128 * b:128 * b + 128], S.ident)
                    ins.then_inc(turned, 1)
                    pe.wait_ge(tv, g + 1)
                    pe.wait_ge(ta, g + 1)
                    if g >= 1:
                        pe.wait_ge(ov, g)
                    for x in range(4):
                        for ci in range(2):
                            for b in range(i + 1):
                                ins = pe.matmul(p_o[:, 512 * ci + 128 * x:512 * ci + 128 * x + 128], S.c_tok[:, b, 128 * ci:128 * ci + 128], probT[:, x, b, :], start=(b == 0), stop=(b == i))
                    ins.then_inc(made, 1)

            @block.vector
            def _(dve):
                done = [0]

                def step(ins):
                    done[0] += 1
                    ins.then_inc(chain, 1)
                    dve.wait_ge(chain, done[0])

                for g, (i, q) in enumerate(GROUPS):
                    w = 128 * (i + 1)
                    dve.wait_ge(scored, g + 1)
                    src = p_s[g % 2][:, :].rearrange("p (x n) -> p x n", x=4)
                    if i == 1:
                        step(dve.tensor_copy(score[:, g % 2, :, 0:128], src[:, :, 0:128]))
                    dve.tensor_tensor(score[:, g % 2, :, w - 128:w], src[:, :, w - 128:w], S.table("causal").unsqueeze(1).to_broadcast([128, 4, 128]), ALU.add).then_inc(masked, 1)
                    dve.wait_ge(masked, g + 1)
                    step(dve.tensor_reduce(stat[:, 0, g, :], score[:, g % 2, :, 0:w], AX.X, ALU.max))
                    dve.tensor_scalar(stat[:, 1, g, :], stat[:, 0, g, :], -MLA_SCALE, None, ALU.mult).then_inc(bias, 1)
                    dve.wait_ge(exped, 4 * (g + 1))
                    step(dve.reciprocal(stat[:, 3, g, :], stat[:, 2, g, :]))
                    dve.tensor_tensor(prob[:, g % 2, :, 0:w], prob[:, g % 2, :, 0:w], stat[:, 3, g, :].unsqueeze(2).to_broadcast([128, 4, w]), ALU.mult).then_inc(norm, 1)
                    dve.wait_ge(turned, g + 1)
                    if g >= 1:
                        dve.wait_ge(made, g)
                    dve.tensor_copy(probT[:, 0:2, 0:i + 1, :], p_t[:, 0:512].rearrange("p (x b n) -> p x b n", x=2, b=2)[:, :, 0:i + 1, :]).then_inc(tv, 1)
                    dve.wait_ge(made, g + 1)
                    dve.tensor_copy(S.o_lat[:, :, 4 * q:4 * q + 4, 128 * i:128 * i + 128], p_o[:, :].rearrange("p (c x n) -> p c x n", c=2, x=4)).then_inc(ov, 1)

            @block.scalar
            def _(act):
                for g, (i, q) in enumerate(GROUPS):
                    w = 128 * (i + 1)
                    act.wait_ge(bias, g + 1)
                    if g >= 2:
                        act.wait_ge(turned, g - 1)
                    for x in range(4):
                        act.activation(prob[:, g % 2, x, 0:w], score[:, g % 2, x, 0:w], ACT.Exp, bias=stat[:, 1, g, x:x + 1], scale=MLA_SCALE,
                                       accum_out=stat[:, 2, g, x:x + 1]).then_inc(exped, 1)
                    act.wait_ge(turned, g + 1)
                    if g >= 1:
                        act.wait_ge(made, g)
                    act.copy(probT[:, 2:4, 0:i + 1, :], p_t[:, 512:1024].rearrange("p (x b n) -> p x b n", x=2, b=2)[:, :, 0:i + 1, :]).then_inc(ta, 1)


def mla_sample(nc, d, S):
    NBUF = 3
    with ExitStack() as ctx:
        sb = lambda n, s, t=F32: ctx.enter_context(nc.sbuf_tensor(n, s, t))
        ps = lambda n, s=(128, 512): ctx.enter_context(nc.psum_tensor(n, list(s), F32))
        sem = lambda n: S.semaphore(nc, n)
        pages = sb("page_numbers", [1, NB * NPG], I32)
        lat = [sb(f"lat{i}", [128, NPG, KVL]) for i in range(NBUF)]; rope = [sb(f"rope{i}", [128, NPG, ROPE]) for i in range(NBUF)]
        kT = sb("kT", [128, 2, NPG * PAGE]); kpT = sb("kpT", [64, NPG * PAGE])
        qs = sb("q_of_sample", [128, 2, MH, ND]); qps = sb("qp_of_sample", [64, MH, ND])
        prob = sb("prob_s", [128, 1024]); probT = S.probT_s
        new = sb("new_scores", [64, 64]); p_new = sb("p_new", [64, 64]); p_newT = sb("p_newT", [64, 64])
        stat = sb("stat_s", [128, 12]); o_rows = sb("o_rows", [128, KVL]); o_sum = sb("o_half", [128, 2, 64])
        p_s = ps("ps_s", (128, 1024)); p_t = [ps("ps_t0"), ps("ps_t1")]; p_n = ps("ps_n"); p_pt = ps("ps_pt", (128, 1024)); p_o = ps("ps_o")
        table_in = sem("page_table_in"); sp_in = [sem(f"pages_in_sp{i}") for i in range(NBUF)]; pool_in = [sem(f"pages_in_pool{i}") for i in range(NBUF)]
        turned = sem("k_turned"); kept = [sem("k_copied_v"), sem("k_copied_a")]; q_ready = sem("sq_ready"); scored = sem("s_scored"); chain = sem("s_chain"); bias = sem("s_bias")
        exped = sem("s_exped"); p_turned = sem("s_p_turned"); p_v = sem("s_pt_v"); p_a = sem("s_pt_a"); made = sem("s_made"); rows = sem("s_rows"); o_turned = sem("s_o_turned"); stored = sem("s_kept")
        SP_ROPE = 3
        ring = [p_t[0], p_t[1], p_pt[:, 0:512], p_pt[:, 512:1024]]
        NI = 12

        def samples(eng, first, body):
            first()
            with eng.Fori(0, NB // NBUF) as it:
                for par in range(NBUF):
                    body(NBUF * it + par, par, it)
            for b in range(NB // NBUF * NBUF, NB):
                body(b, b % NBUF, b // NBUF)

        with nc.Block() as block:
            def load_pages(eng, loads, signal):
                def one(b, par):
                    for p in range(NPG):
                        if any(p in which for _, _, which in loads):
                            page = eng.value_load(pages[0:1, bass.ds(NPG * b + p, 1)], min_val=0, max_val=NPHYS - 1)
                        for cache, dst, which in loads:
                            if p in which:
                                eng.dma_start(dst[par][:, p, :], cache[bass.ds(page, 1), :, :].rearrange("i p n -> p (i n)")).then_inc(signal[par], 16)
                def turn(b, par):
                    eng.wait_ge(made, b + 1)
                    eng.nop(nofuse=True)
                    one(b, par)

                with eng.Fori(0, NB // NBUF) as it:
                    for par in range(NBUF):
                        turn(NBUF * it + par, par)
                for b in range(NB // NBUF * NBUF, NB):
                    turn(b, b % NBUF)

            @block.sync
            def _(sp):
                sp.dma_start(pages[:, :], d['page_table'].rearrange("b n -> (b n)").unsqueeze(0)).then_inc(table_in, 16)
                sp.wait_ge(table_in, 16)
                load_pages(sp, [(d['cache_kv_latent'][0], lat, range(NPG)), (d['cache_k_rope'][0], rope, range(SP_ROPE))], sp_in)

            @block.gpsimd
            def _(pool):
                pool.wait_ge(table_in, 16)
                load_pages(pool, [(d['cache_k_rope'][0], rope, range(SP_ROPE, NPG))], pool_in)

            @block.tensor
            def _(pe):
                def turn(b, par, it):
                    pe.wait_ge(sp_in[par], 16 * (NPG + SP_ROPE) * (it + 1))
                    pe.wait_ge(pool_in[par], 16 * (NPG - SP_ROPE) * (it + 1))
                    for k in range(NI):
                        pe.wait_ge(kept[k % 2], NI // 2 * b + max(0, k // 2 - 1))
                        if k < 8:
                            for ci in range(2):
                                for x in range(2):
                                    ins = pe.transpose(ring[k % 4][:, 256 * ci + 128 * x:256 * ci + 128 * x + 128], lat[par][:, 2 * k + x, 128 * ci:128 * ci + 128], S.ident)
                        else:
                            pe.nop(nofuse=True)
                            for x in range(4):
                                ins = pe.transpose(ring[k % 4][0:64, 128 * x:128 * x + 128], rope[par][:, 4 * (k - 8) + x, :], S.ident)
                        ins.then_inc(turned, 1)

                def past(b):
                    for e in range(2):
                        pe.wait_ge(kept[e], NI // 2 * (b + 1))
                    pe.wait_ge(q_ready, b + 1)
                    for kc in range(4):
                        o = p_s[64 * (kc // 2):64 * (kc // 2) + 64, 512 * (kc % 2):512 * (kc % 2) + 512]
                        for ci in range(2):
                            pe.matmul(o, qs[:, ci, :, :].rearrange("p h t -> p (h t)"), kT[:, ci, 512 * kc:512 * kc + 512], start=(ci == 0), stop=False)
                        pe.matmul(o, qps[:, :, :].rearrange("p h t -> p (h t)"), kpT[:, 512 * kc:512 * kc + 512], start=False, stop=True)

                def new_keys(b):
                    pe.wait_ge(stored, b)
                    pe.nop(nofuse=True)
                    for ci in range(2):
                        pe.matmul(p_n[0:64, 0:64], qs[:, ci, :, :].rearrange("p h t -> p (h t)"), S.c[:, ci, SEQ:T], start=(ci == 0), stop=False)
                    pe.matmul(p_n[0:64, 0:64], qps[:, :, :].rearrange("p h t -> p (h t)"), S.kp[:, SEQ:T], start=False, stop=True).then_inc(scored, 1)

                def body(b, par, it):
                    pe.wait_ge(exped, b + 1)
                    if not isinstance(b, int) or b + 1 < NB:
                        for e in range(2):
                            pe.wait_ge(kept[e], NI // 2 * (b + 2))
                    for j in range(8):
                        pe.transpose(p_pt[:, 128 * j:128 * j + 128], prob[:, 128 * j:128 * j + 128], S.ident)
                    pe.transpose(p_n[0:64, 64:128], p_new[:, :], S.ident[0:64, 0:64]).then_inc(p_turned, 1)
                    pe.wait_ge(p_v, b + 1)
                    pe.wait_ge(p_a, b + 1)
                    for j in range(8):
                        for half in range(2):
                            ins = pe.matmul(p_o[64 * half:64 * half + 64, 0:KVL], probT[:, j, 64 * half:64 * half + 64], lat[par][:, 8 * half + j, :], start=(j == 0), stop=(j == 7 and half == 1))
                    pe.matmul(p_o[0:64, 0:KVL], p_newT[:, :], S.c_tok[0:64, 2, :], start=False, stop=True).then_inc(made, 1)
                    more = not isinstance(b, int) or b + 1 < NB
                    if more:
                        past(b + 1)
                    pe.wait_ge(rows, b + 1)
                    for ci in range(2):
                        ins = pe.transpose(p_n[:, 256 + 128 * ci:256 + 128 * ci + 128], o_rows[:, 128 * ci:128 * ci + 128], S.ident)
                    ins.then_inc(o_turned, 1)
                    if more:
                        new_keys(b + 1)
                    if not isinstance(b, int) or b + 2 < NB:
                        turn(b + 2, (par + 2) % NBUF, it + (par + 2) // NBUF)

                def first():
                    turn(0, 0, 0)
                    past(0)
                    new_keys(0)
                    turn(1, 1, 0)

                for _ in range(NBUF):
                    pe.nop().then_inc(made, 1)
                samples(pe, first, body)

            def keep(eng, copy, parity, b):
                for k in range(parity, NI, 2):
                    eng.wait_ge(turned, NI * b + k + 1)
                    if k < 8:
                        ins = copy(kT[:, :, 256 * k:256 * k + 256], ring[k % 4][:, :].rearrange("p (c n) -> p c n", c=2))
                    else:
                        ins = copy(kpT[:, 512 * (k - 8):512 * (k - 8) + 512], ring[k % 4][0:64, :])
                    ins.then_inc(kept[parity], 1)

            @block.vector
            def _(dve):
                STEPS = 12

                def body(b, par, it):
                    done = [0]

                    def step(ins):
                        done[0] += 1
                        ins.then_inc(chain, 1)
                        dve.wait_ge(chain, STEPS * b + done[0])

                    dve.wait_ge(scored, b + 1)
                    st = lambda k, half=0: stat[64 * half:64 * half + 64, k:k + 1]
                    dve.tensor_reduce(stat[:, 0:1], p_s[:, :], AX.X, ALU.max)
                    step(dve.tensor_tensor(new[:, :], p_n[0:64, 0:64], S.table("own_causal")[0:64, bass.ds(64 * b, 64)], ALU.add))
                    dve.tensor_copy(st(1), st(0, 1))
                    step(dve.tensor_reduce(st(2), new[:, :], AX.X, ALU.max))
                    step(dve.tensor_tensor(st(3), st(0), st(2), ALU.max))
                    step(dve.tensor_tensor(st(3), st(3), st(1), ALU.max))
                    step(dve.tensor_scalar(st(4), st(3), -MLA_SCALE, None, ALU.mult))
                    dve.tensor_copy(st(4, 1), st(4)).then_inc(bias, 1)
                    if not isinstance(b, int) or b + 1 < NB:
                        keep(dve, dve.tensor_copy, 0, b + 1)
                    dve.wait_ge(exped, b + 1)
                    step(dve.tensor_copy(st(7), st(5, 1)))
                    step(dve.tensor_tensor(st(8), st(5), st(6), ALU.add))
                    step(dve.tensor_tensor(st(8), st(8), st(7), ALU.add))
                    step(dve.reciprocal(st(9), st(8)))
                    step(dve.tensor_copy(st(9, 1), st(9)))
                    dve.wait_ge(p_turned, b + 1)
                    dve.tensor_copy(probT[:, 0:4, :].rearrange("p j n -> p (j n)"), p_pt[:, 0:512]).then_inc(p_v, 1)
                    dve.wait_ge(made, NBUF + b + 1)
                    dve.tensor_scalar(o_rows[:, :], p_o[:, 0:KVL], stat[:, 9:10], None, ALU.mult).then_inc(rows, 1)
                    dve.wait_ge(o_turned, b + 1)
                    src = p_n[:, 256:512].rearrange("p (c half n) -> p c half n", c=2, half=2)
                    step(dve.tensor_copy(o_sum[:, :, :], src[:, :, 0, :]))
                    for ci in range(2):
                        ins = dve.tensor_tensor(S.o_lat[:, ci, :, bass.ds(SEQ + ND * b, ND)], o_sum[:, ci, :].rearrange("p (h t) -> p h t", h=MH),
                                                src[:, ci, 1, :].rearrange("p (h t) -> p h t", h=MH), ALU.add)
                        if ci == 0:
                            step(ins)
                    ins.then_inc(stored, 1)
                    assert done[0] == 12

                samples(dve, lambda: keep(dve, dve.tensor_copy, 0, 0), body)

            @block.scalar
            def _(act):
                def queries(b):
                    act.copy(qs[:, :, :, :].rearrange("p c h t -> p (c h) t"), S.q_lat[:, :, :, bass.ds(SEQ + ND * b, ND)].rearrange("p c h t -> p (c h) t"))
                    act.copy(qps[:, :, :], S.q_pe[:, :, bass.ds(SEQ + ND * b, ND)]).then_inc(q_ready, 1)

                def first():
                    queries(0)
                    keep(act, act.copy, 1, 0)

                def body(b, par, it):
                    act.wait_ge(bias, b + 1)
                    act.activation(prob[:, :], p_s[:, :], ACT.Exp, bias=stat[:, 4:5], scale=MLA_SCALE, accum_out=stat[:, 5:6])
                    act.activation(p_new[:, :], new[:, :], ACT.Exp, bias=stat[0:64, 4:5], scale=MLA_SCALE, accum_out=stat[0:64, 6:7]).then_inc(exped, 1)
                    if not isinstance(b, int) or b + 1 < NB:
                        queries(b + 1)
                        keep(act, act.copy, 1, b + 1)
                    act.wait_ge(p_turned, b + 1)
                    act.copy(p_newT[:, :], p_n[0:64, 64:128])
                    act.copy(probT[:, 4:8, :].rearrange("p j n -> p (j n)"), p_pt[:, 512:1024]).then_inc(p_a, 1)
                    act.wait_ge(made, NBUF + b + 1)

                samples(act, first, body)


def mla_out(nc, S):
    with ExitStack() as ctx:
        bank = [ctx.enter_context(nc.psum_tensor(f"p_uv{i}", [128, 512], F32)) for i in range(4)]
        made = S.semaphore(nc, "uv_made"); copied = [S.semaphore(nc, "uv_copied_v"), S.semaphore(nc, "uv_copied_a")]
        with nc.Block() as block:
            @block.tensor
            def _(pe):
                for h in range(MH):
                    if h >= 4:
                        pe.wait_ge(copied[h % 2], h // 2 - 1)
                    for ci in range(2):
                        ins = pe.matmul(bank[h % 4][:, 0:T], S.w_kvb[:, ci, 256 * h + 128:256 * h + 256], S.o_lat[:, ci, h, :], start=(ci == 0), stop=(ci == 1))
                    ins.then_inc(made, 1)

            def copies(eng, copy, parity):
                for h in range(parity, MH, 2):
                    eng.wait_ge(made, h + 1)
                    copy(S.mix[:, 8 + h, :], bank[h % 4][:, 0:T]).then_inc(copied[parity], 1)

            @block.vector
            def _(dve):
                copies(dve, dve.tensor_copy, 0)

            @block.scalar
            def _(act):
                copies(act, act.copy, 1)


def memory_keys(nc, d, S, outs):
    with ExitStack() as ctx:
        sb = lambda n, s, t=F32: ctx.enter_context(nc.sbuf_tensor(n, s, t))
        sem = lambda n: S.semaphore(nc, n)
        mem_n = sb("mem_n", [128, DT, MEM])
        w = [sb("w_mk", [128, DT, 512]), sb("w_mv", [128, DT, 512])]
        w_in = [sem("wmk_in"), sem("wmv_in")]
        with ExitStack() as c1:
            mem, mem_in = S.mem_tokens, S.mem_in; memT = c1.enter_context(nc.sbuf_tensor("memT", [128, DT, MEM], F32))
            p_t = [c1.enter_context(nc.psum_tensor(f"pm_t{i}", [128, 512], F32)) for i in range(4)]
            turned = S.semaphore(nc, "mem_turned")
            copied = [S.semaphore(nc, "mem_copied_v"), S.semaphore(nc, "mem_copied_a")]
            with nc.Block() as block:
                @block.sync
                def _(sp):
                    for x, n in ((0, 'w_mk'), (1, 'w_mv')):
                        sp.dma_start(w[x][:, :, :], d[n][0].rearrange("(t p) n -> p t n", p=128)).then_inc(w_in[x], 16)

                @block.tensor
                def _(pe):
                    pe.wait_ge(mem_in, 16)
                    for k in range(8):
                        if k >= 4:
                            pe.wait_ge(copied[k % 2], k // 2 - 1)
                        for t in range(2):
                            for i in range(2):
                                ins = pe.transpose(p_t[k % 4][:, 256 * t + 128 * i:256 * t + 128 * i + 128], mem[:, i, 128 * (2 * k + t):128 * (2 * k + t) + 128], S.ident)
                        ins.then_inc(turned, 1)

                def copies(eng, copy, parity):
                    for k in range(parity, 8, 2):
                        eng.wait_ge(turned, k + 1)
                        copy(memT[:, 2 * k:2 * k + 2, :].rearrange("p t n -> p (t n)"), p_t[k % 4][:, :]).then_inc(copied[parity], 1)

                @block.vector
                def _(dve):
                    copies(dve, dve.tensor_copy, 0)

                @block.scalar
                def _(act):
                    copies(act, act.copy, 1)
            feature_norm(nc, S, "norm_memory", memT[:, :, :], mem_n[:, :, :], S.vec("mem_norm"), DT, D)
        mem_k = sb("mem_k", [128, 2, 512])
        bank = [ctx.enter_context(nc.psum_tensor(f"pm_kv{i}", [128, 512], F32)) for i in range(4)]; p_kt = [ctx.enter_context(nc.psum_tensor(f"pm_kt{i}", [128, 512], F32)) for i in range(2)]
        made = sem("mkv_made"); copied = sem("mkv_copied"); k_turned = sem("mk_turned"); k_kept = sem("mk_kept"); out = sem("mkv_out")
        with nc.Block() as block:
            @block.sync
            def _(sp):
                for x, buf in ((0, mem_k), (1, S.mem_v)):
                    for i in range(2):
                        sp.wait_ge(copied, 2 * x + i + 1)
                        sp.dma_start(outs[4 + x][0, 0, 128 * i:128 * i + 128].rearrange("p h n -> p (h n)"), buf[:, i, :]).then_inc(out, 16)
                sp.wait_ge(out, 64)

            @block.tensor
            def _(pe):
                for x in range(2):
                    pe.wait_ge(w_in[x], 16)
                    for i in range(2):
                        for t in range(DT):
                            ins = pe.matmul(bank[2 * x + i][:, :], mem_n[:, t, 128 * i:128 * i + 128], w[x][:, t, :], start=(t == 0), stop=(t == DT - 1))
                        ins.then_inc(made, 1)
                pe.wait_ge(copied, 2)
                for h in range(MEMH):
                    for i in range(2):
                        ins = pe.transpose(p_kt[h // 2][:, 256 * (h % 2) + 128 * i:256 * (h % 2) + 128 * i + 128], mem_k[:, i, 128 * h:128 * h + 128], S.ident)
                    if h % 2:
                        ins.then_inc(k_turned, 1)

            @block.vector
            def _(dve):
                for x, buf in ((0, mem_k), (1, S.mem_v)):
                    for i in range(2):
                        dve.wait_ge(made, 2 * x + i + 1)
                        dve.tensor_copy(buf[:, i, :], bank[2 * x + i][:, :]).then_inc(copied, 1)
                for q in range(2):
                    dve.wait_ge(k_turned, q + 1)
                    dve.tensor_copy(S.mem_kT[:, 2 * q:2 * q + 2, :].rearrange("p h n -> p (h n)"), p_kt[q][:, :]).then_inc(k_kept, 1)


def memory_prompt(nc, S):
    with ExitStack() as ctx:
        sb = lambda n, s, t=F32: ctx.enter_context(nc.sbuf_tensor(n, s, t))
        ps = lambda n, s=(128, 1024): ctx.enter_context(nc.psum_tensor(n, list(s), F32))
        sem = lambda n: S.semaphore(nc, n)
        prob = sb("prob_m", [128, 2, MEMH, MEM]); probT = sb("probT_m", [128, 2, MEMH, 2, 128]); stat = sb("stat_m", [128, 4, 2, MEMH])
        p_s = [ps("pm_s0"), ps("pm_s1")]; p_t = ps("pm_turn"); p_o = ps("pm_o")
        scored = sem("mp_scored"); chain = sem("mp_chain"); bias = sem("mp_bias"); exped = sem("mp_exped"); norm = sem("mp_norm"); turned = sem("mp_turned"); kept = sem("mp_kept"); made = sem("mp_made"); out = sem("mp_out")
        with nc.Block() as block:
            @block.tensor
            def _(pe):
                for i in range(2):
                    for h in range(MEMH):
                        ins = pe.matmul(p_s[i][:, 256 * h:256 * h + 256], S.mem_q[:, h, 128 * i:128 * i + 128], S.mem_kT[:, h, :], start=True, stop=True)
                    ins.then_inc(scored, 1)
                for i in range(2):
                    pe.wait_ge(norm, i + 1)
                    if i:
                        pe.wait_ge(kept, 1)
                    for h in range(MEMH):
                        for b in range(2):
                            ins = pe.transpose(p_t[:, 256 * h + 128 * b:256 * h + 128 * b + 128], prob[:, i, h, 128 * b:128 * b + 128], S.ident)
                    ins.then_inc(turned, 1)
                    pe.wait_ge(kept, i + 1)
                    for h in range(MEMH):
                        for b in range(2):
                            ins = pe.matmul(p_o[:, 512 * i + 128 * h:512 * i + 128 * h + 128], S.mem_v[:, b, 128 * h:128 * h + 128], probT[:, i, h, b, :], start=(b == 0), stop=(b == 1))
                    ins.then_inc(made, 1)

            @block.vector
            def _(dve):
                done = [0]

                def step(ins):
                    done[0] += 1
                    ins.then_inc(chain, 1)
                    dve.wait_ge(chain, done[0])

                for i in range(2):
                    dve.wait_ge(scored, i + 1)
                    step(dve.tensor_reduce(stat[:, 0, i, :], p_s[i][:, :].rearrange("p (h n) -> p h n", h=MEMH), AX.X, ALU.max))
                    dve.tensor_scalar(stat[:, 1, i, :], stat[:, 0, i, :], -MEM_SCALE, None, ALU.mult).then_inc(bias, 1)
                for i in range(2):
                    dve.wait_ge(exped, MEMH * (i + 1))
                    step(dve.reciprocal(stat[:, 3, i, :], stat[:, 2, i, :]))
                    dve.tensor_tensor(prob[:, i, :, :], prob[:, i, :, :], stat[:, 3, i, :].unsqueeze(2).to_broadcast([128, MEMH, MEM]), ALU.mult).then_inc(norm, 1)
                for i in range(2):
                    dve.wait_ge(made, i + 1)
                    dve.tensor_copy(S.mem_o[:, :, 128 * i:128 * i + 128], p_o[:, 512 * i:512 * i + 512].rearrange("p (h n) -> p h n", h=MEMH)).then_inc(out, 1)

            @block.scalar
            def _(act):
                for i in range(2):
                    act.wait_ge(bias, i + 1)
                    for h in range(MEMH):
                        act.activation(prob[:, i, h, :], p_s[i][:, 256 * h:256 * h + 256], ACT.Exp, bias=stat[:, 1, i, h:h + 1], scale=MEM_SCALE, accum_out=stat[:, 2, i, h:h + 1]).then_inc(exped, 1)
                for i in range(2):
                    act.wait_ge(turned, i + 1)
                    act.copy(probT[:, i, :, :, :].rearrange("p h b n -> p (h b n)"), p_t[:, :]).then_inc(kept, 1)


def memory_sample(nc, d, S):
    with ExitStack() as ctx:
        sb = lambda n, s, t=F32: ctx.enter_context(nc.sbuf_tensor(n, s, t))
        sem = lambda n: S.semaphore(nc, n)
        k, k_in = S.mem_k_s, S.msk_in
        kT = sb("mem_kT_s", [128, NB, MEMH, MEM]); v = sb("mem_v_s", [128, NB, 2, 512])
        q = sb("mem_q_s", [128, NB, MEMH, 32]); stat = sb("stat_ms", [128, 4, NB])
        v_in = sem("msv_in"); q_ready = sem("ms_q")
        with ExitStack() as c1:
            p_t = [c1.enter_context(nc.psum_tensor(f"pms_t{i}", [128, 1024], F32)) for i in range(4)]
            turned = S.semaphore(nc, "msk_turned"); copied = [S.semaphore(nc, "msk_copied_v"), S.semaphore(nc, "msk_copied_a")]
            with nc.Block() as block:
                @block.sync
                def _(sp):
                    for b in range(NB):
                        sp.dma_start(v[:, b, :, :], d['cache_mem_v'][0, b].rearrange("(i p) h n -> p i (h n)", p=128)).then_inc(v_in, 16)

                @block.tensor
                def _(pe):
                    pe.wait_ge(k_in, 16 * NB)
                    for b in range(NB):
                        if b >= 4:
                            pe.wait_ge(copied[b % 2], b // 2 - 1)
                        for h in range(MEMH):
                            for i in range(2):
                                ins = pe.transpose(p_t[b % 4][:, 256 * h + 128 * i:256 * h + 128 * i + 128], k[:, b, i, 128 * h:128 * h + 128], S.ident)
                        ins.then_inc(turned, 1)

                def copies(eng, copy, parity):
                    for b in range(parity, NB, 2):
                        eng.wait_ge(turned, b + 1)
                        copy(kT[:, b, :, :].rearrange("p h n -> p (h n)"), p_t[b % 4][:, :]).then_inc(copied[parity], 1)

                @block.gpsimd
                def _(pool):
                    pool.memset(q[:, :, :, :], 0.0).then_inc(q_ready, 1)
                    pool.wait_ge(q_ready, 1)
                    pool.tensor_copy(q[:, :, :, 0:ND].rearrange("p b h t -> p h b t"), S.mem_q[:, :, SEQ:T].rearrange("p h (b t) -> p h b t", b=NB)).then_inc(q_ready, 1)
                    pool.wait_ge(q_ready, 2)

                @block.vector
                def _(dve):
                    copies(dve, dve.tensor_copy, 0)

                @block.scalar
                def _(act):
                    copies(act, act.copy, 1)
        with ExitStack() as c1:
            prob = c1.enter_context(nc.sbuf_tensor("prob_ms", [128, NB, MEM], F32)); probT = c1.enter_context(nc.sbuf_tensor("probT_ms", [128, NB, 2, 128], F32))
            o_rows = c1.enter_context(nc.sbuf_tensor("o_rows_ms", [128, NB, 128], F32))
            pa = [c1.enter_context(nc.psum_tensor(f"pms_a{i}", [128, 1024], F32)) for i in range(2)]; pb = [c1.enter_context(nc.psum_tensor(f"pms_b{i}", [128, 1024], F32)) for i in range(2)]
            s1 = lambda n: S.semaphore(nc, n)
            scored = s1("ms_scored"); chain = s1("ms_chain"); ready = s1("ms_shifted"); exped = s1("ms_exped"); turned = s1("ms_turned"); kept = [s1("ms_kept_v"), s1("ms_kept_a")]
            made = s1("ms_made"); rows = s1("ms_rows"); o_turned = s1("ms_o_turned")
            with nc.Block() as block:
                @block.tensor
                def _(pe):
                    for b in range(NB):
                        for h in range(MEMH):
                            ins = pe.matmul(pa[b // 4][32 * h:32 * h + 32, 256 * (b % 4):256 * (b % 4) + 256], q[:, b, h, :], kT[:, b, h, :], start=True, stop=True)
                    ins.then_inc(scored, 1)
                    pe.wait_ge(exped, 1)
                    for b in range(NB):
                        for i in range(2):
                            ins = pe.transpose(pb[b // 4][:, 256 * (b % 4) + 128 * i:256 * (b % 4) + 128 * i + 128], prob[:, b, 128 * i:128 * i + 128], S.ident)
                        if b % 4 == 3:
                            ins.then_inc(turned, 1)
                    for e in range(2):
                        pe.wait_ge(kept[e], 1)
                    pe.wait_ge(v_in, 16 * NB)
                    for b in range(NB):
                        for h in range(MEMH):
                            for i in range(2):
                                ins = pe.matmul(pa[0][32 * h:32 * h + 32, 128 * b:128 * b + 128], probT[:, b, i, 32 * h:32 * h + 32], v[:, b, i, 128 * h:128 * h + 128], start=(i == 0), stop=(i == 1))
                    ins.then_inc(made, 1)
                    pe.wait_ge(rows, 1)
                    for b in range(NB):
                        ins = pe.transpose(pa[1][:, 128 * b:128 * b + 128], o_rows[:, b, :], S.ident)
                    ins.then_inc(o_turned, 1)

                @block.vector
                def _(dve):
                    done = [0]

                    def step(ins):
                        done[0] += 1
                        ins.then_inc(chain, 1)
                        dve.wait_ge(chain, done[0])

                    dve.wait_ge(scored, 1)
                    sv = lambda x: pa[x][:, :].rearrange("p (b n) -> p b n", b=4)
                    for x in range(2):
                        ins = dve.tensor_reduce(stat[:, 0, 4 * x:4 * x + 4], sv(x), AX.X, ALU.max)
                    step(ins)
                    for x in range(2):
                        ins = dve.tensor_tensor(prob[:, 4 * x:4 * x + 4, :], sv(x), stat[:, 0, 4 * x:4 * x + 4].unsqueeze(2).to_broadcast([128, 4, MEM]), ALU.subtract)
                    ins.then_inc(ready, 1)
                    dve.wait_ge(exped, 1)
                    step(dve.tensor_reduce(stat[:, 1, :], prob[:, :, :], AX.X, ALU.add))
                    step(dve.reciprocal(stat[:, 2, :], stat[:, 1, :]))
                    dve.wait_ge(turned, 1)
                    dve.tensor_copy(probT[:, 0:4, :, :].rearrange("p b i n -> p (b i n)"), pb[0][:, :]).then_inc(kept[0], 1)
                    dve.wait_ge(made, 1)
                    dve.tensor_tensor(o_rows[:, :, :], pa[0][:, :].rearrange("p (b n) -> p b n", b=NB), stat[:, 2, :].unsqueeze(2).to_broadcast([128, NB, 128]), ALU.mult).then_inc(rows, 1)
                    dve.wait_ge(o_turned, 1)
                    step(dve.tensor_copy(S.mem_o[:, :, SEQ:T].rearrange("p h (b t) -> p b h t", b=NB), pa[1][:, :].rearrange("p (b h t) -> p b h t", b=NB, h=MEMH)[:, :, :, 0:ND]))

                @block.scalar
                def _(act):
                    act.wait_ge(ready, 1)
                    act.activation(prob[:, :, :], prob[:, :, :], ACT.Exp, scale=MEM_SCALE).then_inc(exped, 1)
                    act.wait_ge(turned, 2)
                    act.copy(probT[:, 4:8, :, :].rearrange("p b i n -> p (b i n)"), pb[1][:, :]).then_inc(kept[1], 1)


def memory_out(nc, d, S):
    with ExitStack() as ctx:
        w = [S.mix[:, :, :].rearrange("p t n -> p (t n)")[:, 0:MEMH * D // 2].rearrange("p (t n) -> p t n", t=MEMH), ctx.enter_context(nc.sbuf_tensor("w_mo", [128, MEMH, D // 2], F32))]
        bank = [ctx.enter_context(nc.psum_tensor(f"p_mo{i}", [128, 512], F32)) for i in range(4)]
        w_in = [S.semaphore(nc, f"wmo_in{i}") for i in range(4)]; made = S.semaphore(nc, "mo_made"); added = S.semaphore(nc, "mo_added")
        with nc.Block() as block:
            @block.sync
            def _(sp):
                for q in range(4):
                    sp.dma_start(w[q // 2][:, :, 512 * (q % 2):512 * (q % 2) + 512], d['w_mo'][0, :, 512 * q:512 * q + 512].rearrange("(t p) n -> p t n", p=128)).then_inc(w_in[q], 16)
                for g in range(6):
                    sp.dma_start(S.w[g][:, :], w_granule(d, g, 0)).then_inc(S.w_in[g], 16)

            @block.tensor
            def _(pe):
                for m in range(DT):
                    if m % 4 == 0:
                        pe.wait_ge(w_in[m // 4], 16)
                    if m >= 4:
                        pe.wait_ge(added, m - 3)
                    for t in range(MEMH):
                        ins = pe.matmul(bank[m % 4][:, 0:T], w[m // 8][:, t, 128 * (m % 8):128 * (m % 8) + 128], S.mem_o[:, t, :], start=(t == 0), stop=(t == MEMH - 1))
                    ins.then_inc(made, 1)

            @block.vector
            def _(dve):
                for m in range(DT):
                    dve.wait_ge(made, m + 1)
                    dve.tensor_tensor(S.xT[:, m, :], S.xT[:, m, :], bank[m % 4][:, 0:T], ALU.add).then_inc(added, 1)


def w_granule(d, g, e):
    if g < 4:
        return d[('w_gate', 'w_up')[g % 2]][0][bass.ds(e, 1)].rearrange("e (p t) n -> p (e t n)", t=DT)[:, 8 * FF * (g // 2):8 * FF * (g // 2) + 8 * FF]
    return d['w_down'][0][bass.ds(e, 1), 256 * (g - 4):256 * (g - 4) + 256, :].rearrange("e (k p) n -> p (e k) n", p=128)


def route_tokens(nc, d, S, h3T, x2T, ident):
    T = S.T
    with ExitStack() as ctx:
        sb = lambda n, s, t=F32: ctx.enter_context(nc.sbuf_tensor(n, s, t))
        ps = lambda n, s=(128, 512): ctx.enter_context(nc.psum_tensor(n, list(s), F32))
        sem = lambda n: S.semaphore(nc, n)
        w_router = sb("w_router", [128, DT, NG + NE])
        bias = sb("router_bias", [128, NG + NE])
        x2 = sb("x2_tokens", [128, 3, D])
        logits = sb("logits", [128, 3, NG + NE])
        lc = sb("lc", [128, 3, NG]); ec = sb("ec", [128, 3, NG])
        stat = sb("stat", [128, 12, 3])
        group_hot = sb("group_hot", [128, 3, NG])
        order = sb("order", [128, 8])
        prod = sb("prod", [128, 3, NG, EG])
        lf = sb("lf", [128, 3, EG]); pf = sb("pf", [128, 3, EG]); pf2 = sb("pf2", [128, 3, EG])
        score = sb("score", [128, 3, EG])
        hot1 = sb("hot1", [128, 3, EG]); hot2 = sb("hot2", [128, 3, EG])
        sel1 = sb("sel1", [128, 3, NG, EG]); sel2 = sb("sel2", [128, 3, NG, EG])
        sel = sb("sel", [128, 3, NE])
        valid = sb("valid", [128, 3])
        before = sb("before", [128, 128])
        ones = S.table("ones")
        token = sb("token", [128, 3])
        count = sb("count", [128, 1])
        p_logit = ps("p_logit"); p_pos = ps("p_pos"); p_turn = [ps("p_turn0"), ps("p_turn1")]
        loaded = sem("router_loaded"); consts = sem("router_consts"); logit_ready = sem("logit_ready")
        turned = sem("turned"); turn_copied = sem("turn_copied"); exp_in = sem("exp_in"); exp_out = sem("exp_out")
        chain = sem("route_chain"); positions = sem("positions"); sel_ready = sem("sel_ready"); parked = sem("parked")
        with nc.Block() as block:
            @block.sync
            def _(sp):
                sp.dma_start(w_router[:, :, 0:NG], d['w_router_c'][0].rearrange("(t p) n -> p t n", p=128)).then_inc(loaded, 16)
                sp.dma_start(w_router[:, :, NG:], d['w_router_f'][0].rearrange("(t p) n -> p t n", p=128)).then_inc(loaded, 16)
                sp.dma_start(bias[:, 0:NG], d['b_router_c'].to_broadcast([128, NG])).then_inc(loaded, 16)
                sp.dma_start(bias[:, NG:], d['b_router_f'].to_broadcast([128, NE])).then_inc(loaded, 16)
                for i, n in enumerate(TILE):
                    sp.wait_ge(turn_copied, 16 // 4 * 2 * (i + 1))
                    sp.dma_start(S.x2_dram[128 * i:128 * i + n, :], x2[0:n, i, :]).then_inc(parked, 16)
                sp.wait_ge(parked, 48)

            @block.gpsimd
            def _(pool):
                done = [0]

                def step(ins):
                    done[0] += 1
                    ins.then_inc(consts, 1)
                    pool.wait_ge(consts, done[0])

                step(pool.affine_select(out=before[:, :], in_=ones, compare_op=ALU.is_gt, fill=0.0, base=0,
                                        pattern=[[1, 128]], channel_multiplier=-1))
                step(pool.iota(token[:, :], pattern=[[2 * 128, 3]], base=0, channel_multiplier=2,
                               allow_small_or_imprecise_dtypes=True))
                step(pool.iota(S.no_row[:, :], pattern=[[0, 1]], base=2 * ROWS, channel_multiplier=1,
                               allow_small_or_imprecise_dtypes=True))
                step(pool.memset(S.row_of[:, :, :, 1:2], 1.0))
                step(pool.iota(order[:, :], pattern=[[-1, 8]], base=8, channel_multiplier=0,
                               allow_small_or_imprecise_dtypes=True))
                step(pool.iota(S.slot_of[:, :], pattern=[[0, 2], [1, SL]], base=0, channel_multiplier=0,
                               allow_small_or_imprecise_dtypes=True))
                step(pool.memset(valid[:, :], 1.0))
                step(pool.memset(valid[64:128, 2:3], 0.0))
                step(pool.memset(logits[64:128, 2, :], 0.0))
                step(pool.memset(S.pos_of[:, :, NE:NE + 1], -1.0))
                step(pool.memset(S.h3[64:128, 2, :, :], 0.0))

            @block.tensor
            def _(pe):
                pe.wait_ge(loaded, 64)
                for i, n in enumerate(TILE):
                    for t in range(DT):
                        mm = pe.matmul(p_logit[0:n, 64 * i:64 * i + NG + NE], h3T[:, t, 128 * i:128 * i + n],
                                       w_router[:, t, :], start=(t == 0), stop=(t == DT - 1))
                    mm.then_inc(logit_ready, 1)
                k = 0
                for i, n in enumerate(TILE):
                    for src in (h3T, x2T):
                        for q in range(4):
                            if k >= 2:
                                pe.wait_ge(turn_copied, k - 1)
                            for j in range(4):
                                mm = pe.transpose(p_turn[k % 2][0:n, 128 * j:128 * j + 128],
                                                  src[:, 4 * q + j, 128 * i:128 * i + n], ident[:, :])
                            mm.then_inc(turned, 1)
                            k += 1
                pe.wait_ge(sel_ready, 1)
                for i, n in enumerate(TILE):
                    for ii in range(i):
                        pe.matmul(p_pos[:, 32 * i:32 * i + 32], ones, sel[:, ii, :], start=(ii == 0), stop=False)
                    pe.matmul(p_pos[:, 32 * i:32 * i + 32], before[:, :], sel[:, i, :], start=(i == 0), stop=True)
                for i in range(3):
                    mm = pe.matmul(p_pos[:, 96:128], ones, sel[:, i, :], start=(i == 0), stop=(i == 2))
                mm.then_inc(positions, 1)

            @block.scalar
            def _(act):
                k = 0
                for i, n in enumerate(TILE):
                    for src in (h3T, x2T):
                        for q in range(4):
                            act.wait_ge(turned, k + 1)
                            if src is h3T:
                                o = S.h3[0:n, i, :, 32 * q:32 * q + 32].rearrange("k t p -> k p t")
                                src_ps = p_turn[k % 2][0:n, :].rearrange("k (p t) -> k p t", t=DT)
                            else:
                                o = x2[0:n, i, 512 * q:512 * q + 512]
                                src_ps = p_turn[k % 2][0:n, :]
                            act.copy(o, src_ps).then_inc(turn_copied, 1)
                            k += 1
                for n in range(2):
                    act.wait_ge(exp_in, n + 1)
                    if n == 0:
                        act.activation(ec[:, :, :], lc[:, :, :], ACT.Exp).then_inc(exp_out, 1)
                    else:
                        act.activation(pf[:, :, :], lf[:, :, :], ACT.Exp).then_inc(exp_out, 1)

            @block.vector
            def _(dve):
                done = [0]

                def step(ins):
                    done[0] += 1
                    ins.then_inc(chain, 1)
                    dve.wait_ge(chain, done[0])

                def bc(a, n):
                    return a.unsqueeze(2).to_broadcast([128, 3, n])

                dve.wait_ge(consts, 11)
                dve.wait_ge(loaded, 64)
                dve.wait_ge(logit_ready, 3)
                for i, n in enumerate(TILE):
                    step(dve.tensor_tensor(logits[0:n, i, :], p_logit[0:n, 64 * i:64 * i + NG + NE], bias[0:n, :], ALU.add))
                step(dve.tensor_reduce(stat[:, 0, :], logits[:, :, 0:NG], AX.X, ALU.max))
                dve.tensor_tensor(lc[:, :, :], logits[:, :, 0:NG], bc(stat[:, 0, :], NG), ALU.subtract).then_inc(exp_in, 1)
                dve.wait_ge(exp_in, 1)
                step(dve.scalar_tensor_tensor(score[:, :, 0:NG], lc[:, :, :], 0.0, order[:, 0:NG].unsqueeze(1).to_broadcast([128, 3, NG]), ALU.is_ge, ALU.mult))
                step(dve.tensor_reduce(stat[:, 1, :], score[:, :, 0:NG], AX.X, ALU.max))
                step(dve.tensor_tensor(group_hot[:, :, :], score[:, :, 0:NG], bc(stat[:, 1, :], NG), ALU.is_equal))
                hot4 = group_hot[:, :, :].unsqueeze(3).to_broadcast([128, 3, NG, EG])
                step(dve.tensor_tensor(prod[:, :, :, :], logits[:, :, NG:].rearrange("p a (g e) -> p a g e", g=NG), hot4, ALU.mult))
                step(dve.tensor_reduce(lf[:, :, :], prod[:, :, :, :].rearrange("p a g e -> p a e g"), AX.X, ALU.add))
                step(dve.tensor_reduce(stat[:, 2, :], lf[:, :, :], AX.X, ALU.max))
                dve.tensor_tensor(lf[:, :, :], lf[:, :, :], bc(stat[:, 2, :], EG), ALU.subtract).then_inc(exp_in, 1)
                dve.wait_ge(exp_out, 1)
                step(dve.tensor_reduce(stat[:, 3, :], ec[:, :, :], AX.X, ALU.add))
                step(dve.reciprocal(stat[:, 4, :], stat[:, 3, :]))
                dve.wait_ge(exp_out, 2)
                order3 = order[:, :].unsqueeze(1).to_broadcast([128, 3, EG])
                for src, hot, m in ((pf, hot1, 5), (pf2, hot2, 6)):
                    step(dve.tensor_reduce(stat[:, m, :], src[:, :, :], AX.X, ALU.max))
                    step(dve.tensor_tensor(score[:, :, :], src[:, :, :], bc(stat[:, m, :], EG), ALU.is_equal))
                    step(dve.tensor_tensor(score[:, :, :], score[:, :, :], order3, ALU.mult))
                    step(dve.tensor_reduce(stat[:, 7, :], score[:, :, :], AX.X, ALU.max))
                    step(dve.tensor_tensor(hot[:, :, :], score[:, :, :], bc(stat[:, 7, :], EG), ALU.is_equal))
                    if src is pf:
                        step(dve.scalar_tensor_tensor(pf2[:, :, :], hot1[:, :, :], -2.0, pf[:, :, :], ALU.mult, ALU.add))
                step(dve.tensor_tensor(stat[:, 8, :], stat[:, 5, :], stat[:, 6, :], ALU.add))
                step(dve.reciprocal(stat[:, 9, :], stat[:, 8, :]))
                step(dve.tensor_tensor(stat[:, 10, :], stat[:, 9, :], stat[:, 4, :], ALU.mult))
                step(dve.tensor_tensor(S.weight[:, 0, :], stat[:, 5, :], stat[:, 10, :], ALU.mult))
                step(dve.tensor_tensor(S.weight[:, 1, :], stat[:, 6, :], stat[:, 10, :], ALU.mult))
                step(dve.tensor_tensor(group_hot[:, :, :], group_hot[:, :, :], bc(valid[:, :], NG), ALU.mult))
                for hot, s in ((hot1, sel1), (hot2, sel2)):
                    step(dve.tensor_tensor(s[:, :, :, :], hot4, hot[:, :, :].unsqueeze(2).to_broadcast([128, 3, NG, EG]), ALU.mult))
                s1 = sel1[:, :, :, :].rearrange("p a g e -> p a (g e)")
                s2 = sel2[:, :, :, :].rearrange("p a g e -> p a (g e)")
                dve.tensor_tensor(sel[:, :, :], s1, s2, ALU.add).then_inc(sel_ready, 1)
                dve.wait_ge(sel_ready, 1)
                dve.wait_ge(positions, 1)
                pos = p_pos[:, 0:96].rearrange("p (a e) -> p a e", a=3)
                step(dve.tensor_tensor(S.pos_of[:, :, 0:NE], pos, sel[:, :, :], ALU.mult))
                step(dve.tensor_tensor(S.pos_of[:, :, 0:NE], S.pos_of[:, :, 0:NE], sel[:, :, :], ALU.add))
                step(dve.tensor_scalar(S.pos_of[:, :, 0:NE], S.pos_of[:, :, 0:NE], -1.0, None, ALU.add))
                for i in range(3):
                    step(dve.tensor_scalar(S.row_of[:, i, :, 0], s2[:, i, :], float(2 * T), token[:, i:i + 1], ALU.mult, ALU.add))
                step(dve.tensor_scalar(S.row_base[:, :], S.no_row[:, :], 0.0, None, ALU.add))
                step(dve.tensor_scalar(S.row_base[64:128, :], S.no_row[64:128, :], 1.0, None, ALU.add))
                step(dve.tensor_reduce(count[:, :], p_pos[:, 96:128], AX.X, ALU.max))
                step(dve.tensor_copy(S.most[:, :], count[:, :]))


def experts(nc, d, S, ident):
    with ExitStack() as ctx:
        sb = lambda n, s, t=F32: ctx.enter_context(nc.sbuf_tensor(n, s, t))
        ps = lambda n, s=(128, 512): ctx.enter_context(nc.psum_tensor(n, list(s), F32))
        sem = lambda n: S.semaphore(nc, n)
        sel = sb("slot_sel", [128, 3, 2 * SL]); rowf = sb("rowf", [128, 1]); row = sb("row", [128, 1], I32)
        xg = sb("xg", [128, 8, 128])
        xgT = sb("xgT", [128, 8, 2, SL])
        act_g = sb("act_g", [128, FF // 2]); hid = sb("hid", [128, FF // 2])
        hidT = sb("hidT", [128, 2, 2, SL])
        y = sb("y_slots", [128, D // 2])
        p_xg = ps("p_xg", (128, 1024)); p_xgT = ps("p_xgT", (128, 1024)); p_g = ps("p_g"); p_u = ps("p_u"); p_y = ps("p_y", (128, 1024))
        w = S.w
        w_free = [sem(f"w_free{g}") for g in range(6)]
        w_in = S.w_in
        sel_made = sem("sel_made"); gathered = sem("gathered")
        xg_v = sem("xg_v"); xg_a = sem("xg_a"); xgT_done = sem("xgT_done"); xgT_v = sem("xgT_v"); xgT_a = sem("xgT_a")
        gate_up = sem("gate_up"); silu_done = sem("silu_done"); hid_done = sem("hid_done"); hid_turned = sem("hid_turned")
        hidT_done = sem("hidT_done"); y_done = sem("y_done"); y_v = sem("y_v"); y_a = sem("y_a"); y_out = sem("y_out"); y_free = sem("y_free")
        ybuf = S.ybuf
        row_sum = sem("row_sum"); row_made = sem("row_made")

        def rounds(eng, body):
            body(0)
            most = eng.value_load(S.most[0:1, 0:1], min_val=0, max_val=SLOTS_MAX)
            with eng.Fori(1, SLOTS_MAX // SL) as r:
                with eng.If(most > r * SL):
                    body(r)
                eng.nop()

        with nc.Block() as block:
            @block.sync
            def _(sp):
                def load(e, r_e, first):
                    for g in range(6):
                        if not first:
                            sp.wait_ge(w_free[g], r_e)
                        sp.dma_start(w[g][:, :], w_granule(d, g, e)).then_inc(w_in[g], 16)

                def body(r):
                    if not isinstance(r, int):
                        load(0, NE * r, False)
                    with sp.Fori(1, NE) as e:
                        load(e, NE * r + e, False)
                rounds(sp, body)

            @block.tensor
            def _(pe):
                def gather(k, r):
                    pe.wait_ge(sel_made, (NE + 1) * r + k + 1)
                    for b in range(2):
                        for i in range(3):
                            for h in range(2):
                                mm = pe.matmul(p_xg[SL * h:SL * h + SL, 512 * b:512 * b + 512], sel[:, i, SL * h:SL * h + SL],
                                               S.h3[:, i, 8 * h + 4 * b:8 * h + 4 * b + 4, :].rearrange("k t p -> k (t p)"),
                                               start=(i == 0), stop=(i == 2))
                    mm.then_inc(gathered, 1)

                def body(r):
                    if not isinstance(r, int):
                        pe.wait_ge(xg_v, (NE + 1) * r)
                        pe.wait_ge(xg_a, (NE + 1) * r)
                    gather(0, r)
                    with pe.Fori(0, NE) as e:
                        n = NE * r + e + 1
                        pe.wait_ge(xg_v, (NE + 1) * r + e + 1)
                        pe.wait_ge(xg_a, (NE + 1) * r + e + 1)
                        for t in range(8):
                            mm = pe.transpose(p_xgT[:, 128 * t:128 * t + 128], xg[:, t, :], ident[:, :])
                        for i in range(3):
                            mm = pe.matmul(p_g[:, 256:258], sel[:, i, :], S.row_of[:, i, bass.ds(e, 1), :].rearrange("k e c -> k (e c)"),
                                           start=(i == 0), stop=(i == 2))
                        mm.then_inc(xgT_done, 1)
                        pe.wait_ge(xgT_v, n)
                        pe.wait_ge(xgT_a, n)
                        for g in range(4):
                            pe.wait_ge(w_in[g], 16 * n)
                            acc = (p_g, p_u)[g % 2]
                            for t in range(8):
                                for h in range(2):
                                    mm = pe.matmul(acc[SL * h:SL * h + SL, 0:FF // 2], xgT[:, t, g // 2, :],
                                                   w[g][:, FF * t + FF // 2 * h:FF * t + FF // 2 * h + FF // 2],
                                                   start=(g < 2 and t == 0), stop=(g >= 2 and t == 7))
                            mm.then_inc(w_free[g], 1)
                        gather(e + 1, r)
                        pe.wait_ge(hid_done, n)
                        for j in range(2):
                            mm = pe.transpose(p_xgT[:, 128 * j:128 * j + 128], hid[:, 128 * j:128 * j + 128], ident[:, :])
                        mm.then_inc(hid_turned, 1)
                        pe.wait_ge(hidT_done, n)
                        pe.wait_ge(y_free, n)
                        for k in range(4):
                            if k % 2 == 0:
                                pe.wait_ge(w_in[4 + k // 2], 16 * n)
                            for b in range(2):
                                for h in range(2):
                                    mm = pe.matmul(p_y[SL * h:SL * h + SL, 512 * b:512 * b + 512],
                                                   hidT[:, k % 2, k // 2, :],
                                                   w[4 + k // 2][:, D * (k % 2) + 1024 * h + 512 * b:D * (k % 2) + 1024 * h + 512 * b + 512],
                                                   start=(k == 0), stop=(k == 3))
                            if k % 2 == 1:
                                mm.then_inc(w_free[4 + k // 2], 1)
                rounds(pe, body)

            @block.vector
            def _(dve):
                def select(k, r):
                    for i in range(3):
                        ins = dve.tensor_scalar(sel[:, i, :], S.slot_of[:, :], slot_shift, S.pos_of[:, i, bass.ds(k, 1)], ALU.add, ALU.is_equal)
                    ins.then_inc(sel_made, 1)

                def copy_xg(k, r):
                    dve.wait_ge(gathered, (NE + 1) * r + k + 1)
                    dve.tensor_copy(xg[:, 0:4, :].rearrange("p t q -> p (t q)"), p_xg[:, 0:512]).then_inc(xg_v, 1)

                slot_shift = S.shift[:, 0:1]

                def body(r):
                    if isinstance(r, int):
                        dve.memset(S.shift[:, :], 0.0).then_inc(S.shifted, 1)
                        dve.wait_ge(S.shifted, 1)
                    else:
                        dve.tensor_scalar(S.shift[:, :], S.shift[:, :], float(SL), None, ALU.add).then_inc(S.shifted, 1)
                        dve.wait_ge(S.shifted, r + 1)
                    select(0, r)
                    copy_xg(0, r)
                    with dve.Fori(0, NE) as e:
                        n = NE * r + e + 1
                        dve.wait_ge(xgT_done, n)
                        dve.tensor_scalar(rowf[:, :], p_g[:, 257:258], S.no_row[:, :], None, ALU.mult).then_inc(row_sum, 1)
                        dve.wait_ge(row_sum, 2 * n - 1)
                        dve.scalar_tensor_tensor(rowf[:, :], p_g[:, 256:257], S.row_base[:, :], rowf[:, :], ALU.add, ALU.subtract).then_inc(row_sum, 1)
                        dve.tensor_copy(xgT[:, 0:4, :, :].rearrange("p t h s -> p (t h s)"), p_xgT[:, 0:512]).then_inc(xgT_v, 1)
                        select(e + 1, r)
                        dve.wait_ge(y_free, n)
                        dve.wait_ge(row_sum, 2 * n)
                        dve.tensor_copy(row[:, :], rowf[:, :]).then_inc(row_made, 1)
                        dve.wait_ge(silu_done, n)
                        dve.tensor_tensor(hid[:, :], act_g[:, :], p_u[:, 0:FF // 2], ALU.mult).then_inc(hid_done, 1)
                        copy_xg(e + 1, r)
                        dve.wait_ge(hid_turned, n)
                        dve.tensor_copy(hidT[:, :, :, :].rearrange("p j h s -> p (j h s)"), p_xgT[:, 0:256]).then_inc(hidT_done, 1)
                        dve.wait_ge(w_free[5], n)
                        dve.tensor_copy(y[:, 0:512], p_y[:, 0:512]).then_inc(y_v, 1)
                rounds(dve, body)

            @block.scalar
            def _(act):
                def copy_xg(k, r):
                    act.wait_ge(gathered, (NE + 1) * r + k + 1)
                    act.copy(xg[:, 4:8, :].rearrange("p t q -> p (t q)"), p_xg[:, 512:1024]).then_inc(xg_a, 1)

                def body(r):
                    copy_xg(0, r)
                    with act.Fori(0, NE) as e:
                        n = NE * r + e + 1
                        act.wait_ge(xgT_done, n)
                        act.copy(xgT[:, 4:8, :, :].rearrange("p t h s -> p (t h s)"), p_xgT[:, 512:1024]).then_inc(xgT_a, 1)
                        act.wait_ge(w_free[3], n)
                        act.activation(act_g[:, :], p_g[:, 0:FF // 2], ACT.Silu).then_inc(silu_done, 1)
                        copy_xg(e + 1, r)
                        act.wait_ge(w_free[5], n)
                        act.copy(y[:, 512:1024], p_y[:, 512:1024]).then_inc(y_a, 1)
                rounds(act, body)

            @block.gpsimd
            def _(pool):
                last_row = pool.to_reg(2 * ROWS - 1)
                pool.nop().then_inc(y_free, 1)

                def body(r):
                    with pool.Fori(0, NE) as e:
                        n = NE * r + e + 1
                        pool.wait_ge(row_made, n)
                        pool.wait_ge(y_v, n)
                        pool.wait_ge(y_a, n)
                        pool.nop(nofuse=True)
                        pool.indirect_dma_start(out=ybuf[:, :], out_offset=bass.IndirectOffsetOnAxis(ap=row[:, 0:1], axis=0),
                                                in_=y[:, :], in_offset=None, bounds_check=last_row, oob_is_err=False).then_inc(y_out, 16)
                        pool.wait_ge(y_out, 16 * n)
                        pool.nop().then_inc(y_free, 1)
                rounds(pool, body)


def combine(nc, d, S, outs):
    with ExitStack() as ctx:
        sb = lambda n, s, t=F32: ctx.enter_context(nc.sbuf_tensor(n, s, t))
        sem = lambda n: S.semaphore(nc, n)
        xo = sb("xo", [128, 3, D]); r1 = sb("r1", [128, 3, D]); r2 = sb("r2", [128, 3, D]); g = sb("final_g", [128, D])
        ss = sb("final_ss", [128, 3, 4]); sq = sb("final_sq", [128, D])
        g_in = sem("final_g_in"); rows_in = [sem(f"rows_in{i}") for i in range(3)]; results = S.ybuf.rearrange("(r h) n -> r (h n)", h=2); chain = sem("combine_chain"); squared = sem("final_squared"); root = sem("final_root"); stored = sem("stored")
        ready = sem("out_ready")
        eps = sb("eps_f", [128, 1]); eps_set = sem("eps_set")
        with nc.Block() as block:
            @block.sync
            def _(sp):
                sp.dma_start(g[:, :], d['final_norm_g'].unsqueeze(0).to_broadcast([128, D])).then_inc(g_in, 16)
                for i, n in enumerate(TILE):
                    sp.dma_start(xo[0:n, i, :], S.x2_dram[128 * i:128 * i + n, :]).then_inc(rows_in[i], 16)
                    for c, r in ((0, r1), (1, r2)):
                        sp.dma_start(r[0:n, i, :], results[T * c + 128 * i:T * c + 128 * i + n, :]).then_inc(rows_in[i], 16)
                for i, n in enumerate(TILE):
                    sp.wait_ge(ready, i + 1)
                    dst = outs[0][0, 128 * i:128 * i + 128, :] if i < 2 else outs[1].rearrange("b t n -> (b t) n")
                    sp.dma_start(dst, xo[0:n, i, :]).then_inc(stored, 16)
                sp.wait_ge(stored, 48)

            @block.scalar
            def _(act):
                act.wait_ge(eps_set, 1)
                for i, n in enumerate(TILE):
                    act.wait_ge(chain, 2 * i + 2)
                    act.activation(sq[0:n, :], xo[0:n, i, :], ACT.Square, accum_out=ss[0:n, i, 0:1]).then_inc(squared, 1)
                    act.wait_ge(squared, i + 1)
                    act.activation(ss[0:n, i, 1:2], ss[0:n, i, 0:1], ACT.Sqrt, bias=eps[0:n, :], scale=1.0 / D).then_inc(root, 1)

            @block.vector
            def _(dve):
                dve.memset(eps[:, :], EPS).then_inc(eps_set, 1)
                for i, n in enumerate(TILE):
                    dve.wait_ge(rows_in[i], 48)
                    for c, r in ((0, r1), (1, r2)):
                        dve.scalar_tensor_tensor(xo[0:n, i, :], r[0:n, i, :], S.weight[0:n, c, i:i + 1], xo[0:n, i, :], ALU.mult, ALU.add).then_inc(chain, 1)
                        dve.wait_ge(chain, 2 * i + c + 1)
                dve.wait_ge(g_in, 16)
                for i, n in enumerate(TILE):
                    dve.wait_ge(root, i + 1)
                    dve.reciprocal(ss[0:n, i, 2:3], ss[0:n, i, 1:2]).then_inc(chain, 1)
                    dve.wait_ge(chain, 6 + i + 1)
                    dve.scalar_tensor_tensor(xo[0:n, i, :], xo[0:n, i, :], ss[0:n, i, 2:3], g[0:n, :], ALU.mult, ALU.mult).then_inc(ready, 1)


def build(nc, d, outs):
    with ExitStack() as ctx:
        sb = lambda n, s, t=F32: ctx.enter_context(nc.sbuf_tensor(n, s, t))
        sem = lambda n: ctx.enter_context(nc.semaphore(n))
        S = Shared()
        S.T = T
        S.x2_dram = nc.dram_tensor("x2_dram", [T, D], F32).ap()
        S.xT_dram = nc.dram_tensor("xT_dram", [128, DT * T], F32).ap()
        S.ybuf = nc.dram_tensor("ybuf", [2 * ROWS, D // 2], F32).ap()
        S.tables_sb = sb("tables_sb", [128, TABLE_W]); S.vectors = sb("vectors", [128, 256]); S.eps = sb("eps", [128, 1])
        S.ident = S.table("ident")
        S.slot_of = sb("slot_of", [128, 2 * SL]); S.no_row = sb("no_row", [128, 1]); S.row_base = sb("row_base", [128, 1]); S.row_of = sb("row_of", [128, 3, NE, 2])
        S.pos_of = sb("pos_of", [128, 3, NE + 1]); S.weight = sb("weight", [128, 2, 3]); S.most = sb("most", [128, 1], I32); S.shift = sb("shift", [128, 1])
        S.shifted = sem("shifted"); S.w_in = [sem(f"w_in_e{g}") for g in range(6)]
        low = sb("low", [128, 3 * D])
        at = [0]

        def part(n, *shape):
            size = math.prod(shape)
            out = low[0:n, at[0]:at[0] + size]
            at[0] += size
            assert at[0] <= 3 * D
            return out.rearrange("p (a b) -> p a b", a=shape[0]) if len(shape) == 2 else out

        S.qa, S.kv, S.kr, S.k, S.sg, S.ys = part(128, 4, T), part(128, 2, T), part(64, T), part(128, 8, T), part(128, 2, T), part(128, HP, 64)
        at[0] = 0
        S.mem_kT, S.mem_v, S.mem_q, S.mem_o = part(128, MEMH, MEM), part(128, 2, 512), part(128, MEMH, T), part(128, MEMH, T)
        S.o_lat = low[:, 0:2 * MH * T].rearrange("p (c h n) -> p c h n", c=2, h=MH)
        S.probT_s = low[:, 2 * MH * T:2 * MH * T + 1024].rearrange("p (j n) -> p j n", j=8)
        S.h3 = low[:, :].rearrange("p (i t q) -> p i t q", i=3, t=DT)
        with ExitStack() as c1:
            sb1 = lambda n, s, t=F32: c1.enter_context(nc.sbuf_tensor(n, s, t))
            mix = sb1("mix", [128, DT, T])
            S.mix, S.r, S.lw = mix, mix[:, 0:8, :], mix[:, 8:16, :]
            with ExitStack() as c2:
                sb2 = lambda n, s, t=F32: c2.enter_context(nc.sbuf_tensor(n, s, t))
                va = sb2("rw_va", [128, DT, T]); S.v, S.a = va[:, 0:8, :], va[:, 8:16, :]; S.xa = sb2("rw_xa", [128, T])
                with ExitStack() as c3:
                    S.P = c3.enter_context(nc.sbuf_tensor("P", [128, 28, SEQ + 1 + 9 * NB], F32))
                    S.hT = mix
                    flat = va[:, :, :].rearrange("p t n -> p (t n)")
                    S.spare = [a.rearrange("p (t n) -> p t n", t=DT) for a in (flat[:, 0:D], flat[:, D:2 * D], low[:, 7 * T:7 * T + D])]
                    with ExitStack() as c4:
                        S.xT = c4.enter_context(nc.sbuf_tensor("xT", [128, DT, T], F32))
                        load_front(nc, d, S)
                        feature_norm(nc, S, "norm_mix", S.xT[:, :, :], mix[:, :, :], S.vec("ln_mix"), DT, D)
                    project_in(nc, d, S)
                    rwkv_mix(nc, d, S, outs)
                with ExitStack() as c3:
                    sb3 = lambda n, s, t=F32: c3.enter_context(nc.sbuf_tensor(n, s, t))
                    S.mt = sb3("maps_m", [128, HP, NCH, 64]); S.nn = sb3("maps_n", [128, NCH, HP, 64])
                    rwkv_pairs(nc, d, S, outs)
                    rwkv_chain(nc, d, S, outs)
            S.recycle(nc)
            with ExitStack() as c2:
                sb2 = lambda n, s, t=F32: c2.enter_context(nc.sbuf_tensor(n, s, t))
                S.c = sb2("latent", [128, 2, T]); S.kp = sb2("rot_key", [64, T]); S.c_tok = sb2("c_tok", [128, 3, KVL]); S.kp_tok = sb2("kp_tok", [128, 3, ROPE])
                S.w_kvb = sb2("w_kvb", [128, 2, MH * (NOPE + VD)]); S.q_lat = sb2("q_lat", [128, 2, MH, T]); S.q_pe = sb2("q_pe", [64, MH, T])
                with ExitStack() as c3:
                    S.qn = c3.enter_context(nc.sbuf_tensor("qn", [128, 4, T], F32)); S.w_qb = c3.enter_context(nc.sbuf_tensor("w_qb", [128, 4, MH * (NOPE + ROPE)], F32))
                    S.qb_in = S.semaphore(nc, "qb_in")
                    with nc.Block() as block:
                        @block.sync
                        def _(sp):
                            sp.dma_start(S.w_qb[:, :, :], d['mla_w_qb'][0].rearrange("(t p) n -> p t n", p=128)).then_inc(S.qb_in, 16)
                            sp.dma_start(S.w_kvb[:, :, :], d['mla_w_kvb'][0].rearrange("(t p) n -> p t n", p=128)).then_inc(S.qb_in, 16)
                    feature_norm(nc, S, "norm_q", S.qa, S.qn[:, :, :], S.vec("q_norm"), 4, QL)
                    feature_norm(nc, S, "norm_kv", S.kv, S.c[:, :, :], S.vec("kv_norm"), 2, KVL)
                    mla_project(nc, d, S, outs)
                mla_prompt(nc, d, S)
                mla_sample(nc, d, S)
                mla_out(nc, S)
            S.xT = sb1("xT_again", [128, DT, T])
            with ExitStack() as c2:
                S.mem_tokens = c2.enter_context(nc.sbuf_tensor("mem_tokens", [128, 2, D], F32)); S.mem_in = sem("mem_in")
                with nc.Block() as block:
                    @block.sync
                    def _(sp):
                        sp.dma_start(S.mem_tokens[:, :, :], d['mem_prompt'][0].rearrange("(i p) n -> p i n", p=128)).then_inc(S.mem_in, 16)
                project_out(nc, d, S)
                S.recycle(nc)
                memory_keys(nc, d, S, outs)
            with ExitStack() as c2:
                S.mem_k_s = c2.enter_context(nc.sbuf_tensor("mem_k_s", [128, NB, 2, 512], F32)); S.msk_in = S.semaphore(nc, "msk_in")
                with nc.Block() as block:
                    @block.sync
                    def _(sp):
                        for b in range(NB):
                            sp.dma_start(S.mem_k_s[:, b, :, :], d['cache_mem_k'][0, b].rearrange("(i p) h n -> p i (h n)", p=128)).then_inc(S.msk_in, 16)
                at = TABLE_AT["before16"][0]
                assert at + D <= TABLE_AT["cos"][0]
                S.spare_late = [a.rearrange("p (t n) -> p t n", t=DT) for a in (low[:, 3 * D - D:3 * D], S.tables_sb[:, at:at + D])]
                feature_norm(nc, S, "norm_mem", S.xT[:, :, :], mix[:, :, :], S.vec("ln_mem"), DT, D)
                memory_queries(nc, d, S)
                memory_prompt(nc, S)
                memory_sample(nc, d, S)
            S.w = [sb1(f"w_expert{g}", [128, 4096]) for g in range(6)]
            memory_out(nc, d, S)
            S.recycle(nc)
            feature_norm(nc, S, "norm_moe", S.xT[:, :, :], mix[:, :, :], S.vec("ln_moe"), DT, D)
            route_tokens(nc, d, S, mix, S.xT, S.ident)
            experts(nc, d, S, S.ident)
        combine(nc, d, S, outs)


OUTPUTS = [(1, SEQ, D), (NB, ND, D), (1, 1, SEQ, KVL), (1, 1, SEQ, ROPE), (1, 1, MEM, MEMH, 128), (1, 1, MEM, MEMH, 128), (1, 1, 2 * HP, HD, HD),
           (1, 1, RPROJ), (1, NB, ND, KVL), (1, NB, ND, ROPE), (1, NB, 2 * HP, HD, HD), (1, NB, RPROJ)]


def kernel(**inputs):
    import concourse.bacc as _bacc
    from concourse.bass_utils import run_bass_kernel_spmd as _run

    nc = _bacc.Bacc("TRN2", target_bir_lowering=False, num_devices=1)
    arrays, d = {}, {}
    for name, value in list(inputs.items()) + [("tables", tables())]:
        a = np.ascontiguousarray(value)
        arrays[f"in_{name}_dram"] = a
        d[name] = nc.dram_tensor(f"in_{name}_dram", a.shape, mybir.dt.from_np(a.dtype), kind="ExternalInput").ap()
    outs = [nc.dram_tensor(f"out_{i}_dram", shape, F32, kind="ExternalOutput").ap() for i, shape in enumerate(OUTPUTS)]
    build(nc, d, outs)
    results = _run(nc, [arrays], core_ids=[0]).results[0]
    return tuple(results[f"out_{i}_dram"] for i in range(len(OUTPUTS)))
```
